# Optimizing a Trainium2 kernel written in Bass

```python
import jax, jax.numpy as jnp
from jax import lax
import numpy as np

D_MODEL = 1024
BATCH = 1
SEQ = 512
DEPTH = 1
DEC_BATCH = 8
DEC_SEQ = 1
PAST_LEN = 4096
PAGE_SIZE = 128

SSD_EXPAND = 2
D_INNER = SSD_EXPAND * D_MODEL
SSD_HEAD_DIM = 64
SSD_HEADS = D_INNER // SSD_HEAD_DIM
SSD_GROUPS = 4
SSD_HPG = SSD_HEADS // SSD_GROUPS
SSD_STATE = 128
CONV_WIDTH = 4
CONV_DIM = D_INNER + 2 * SSD_GROUPS * SSD_STATE
CHUNK = 128
POOL_WINDOWS = (2, 4, 8, 16)
POOL_GROUPS = 4
POOL_WIDTH = D_MODEL
POOL_GW = POOL_WIDTH // POOL_GROUPS
POOL_BUF = 15
MEM_LEN = 256
X_HEADS = 4
X_HEAD_DIM = D_MODEL // X_HEADS
D_FF = 4 * D_MODEL
EPS = 1e-6
OFF_XBC = D_INNER
OFF_DT = OFF_XBC + CONV_DIM
OFF_POOL = OFF_DT + SSD_HEADS
OFF_GA = OFF_POOL + POOL_WIDTH
OFF_GB = OFF_GA + D_MODEL
IN_DIM = OFF_GB + D_MODEL

kernel_name = "hybrid_ssd_pool_gated_decoder_step"

def rmsnorm(x, g):
    xf = x.astype(jnp.float32)
    y = xf * lax.rsqrt(jnp.mean(xf * xf, axis=-1, keepdims=True) + EPS)
    return (y * g.astype(jnp.float32)).astype(x.dtype)

def ssd_scan(xs, dt, A, Bm, Cm, s0):
    b, L = xs.shape[0], xs.shape[1]
    lc = CHUNK if L % CHUNK == 0 else L
    nc = L // lc
    xs = xs.reshape(b, nc, lc, SSD_GROUPS, SSD_HPG, SSD_HEAD_DIM)
    dt = dt.reshape(b, nc, lc, SSD_GROUPS, SSD_HPG)
    Bm = Bm.reshape(b, nc, lc, SSD_GROUPS, SSD_STATE)
    Cm = Cm.reshape(b, nc, lc, SSD_GROUPS, SSD_STATE)
    cs = jnp.cumsum(dt * A, axis=2)
    seg = cs[:, :, :, None] - cs[:, :, None, :]
    causal = jnp.tril(jnp.ones((lc, lc), dtype=bool))[None, None, :, :, None, None]
    lmat = jnp.exp(jnp.where(causal, seg, -jnp.inf))
    xdt = xs * dt[..., None]
    cb = jnp.einsum('bclgn,bcsgn->bclsg', Cm, Bm)
    y_diag = jnp.einsum('bclsgk,bcsgkp->bclgkp', cb[..., None] * lmat, xdt)
    decay_to_end = jnp.exp(cs[:, :, -1:] - cs)
    chunk_states = jnp.einsum('bclgn,bclgkp->bcgkpn', Bm, xdt * decay_to_end[..., None])
    chunk_decay = jnp.exp(cs[:, :, -1])

    def step(s, inp):
        dec, st = inp
        return s * dec[..., None, None] + st, s

    s_fin, s_prev = lax.scan(step, s0, (jnp.moveaxis(chunk_decay, 1, 0), jnp.moveaxis(chunk_states, 1, 0)))
    s_prev = jnp.moveaxis(s_prev, 0, 1)
    y_off = jnp.einsum('bclgn,bcgkpn->bclgkp', Cm, s_prev) * jnp.exp(cs)[..., None]
    y = (y_diag + y_off).reshape(b, L, SSD_GROUPS, SSD_HPG, SSD_HEAD_DIM)
    return y, s_fin

def ssd_branch(z, xbc, dt_raw, conv_buf, ssm0, conv_w, conv_b, dt_bias, a_log, d_skip, norm_w):
    b, L, _ = xbc.shape
    cat = jnp.concatenate([conv_buf.astype(xbc.dtype), xbc], axis=1)
    new_conv = cat[:, -(CONV_WIDTH - 1):]
    conv = conv_b + cat[:, 0:L] * conv_w[0]
    for k in range(1, CONV_WIDTH):
        conv = conv + cat[:, k:k + L] * conv_w[k]
    act = jax.nn.silu(conv.astype(jnp.float32))
    xs = act[..., :D_INNER].reshape(b, L, SSD_GROUPS, SSD_HPG, SSD_HEAD_DIM)
    Bm = act[..., D_INNER:D_INNER + SSD_GROUPS * SSD_STATE].reshape(b, L, SSD_GROUPS, SSD_STATE)
    Cm = act[..., D_INNER + SSD_GROUPS * SSD_STATE:].reshape(b, L, SSD_GROUPS, SSD_STATE)
    dt = jax.nn.softplus(dt_raw.astype(jnp.float32) + dt_bias.astype(jnp.float32)).reshape(b, L, SSD_GROUPS, SSD_HPG)
    A = -jnp.exp(a_log.astype(jnp.float32)).reshape(SSD_GROUPS, SSD_HPG)
    s0 = ssm0.astype(jnp.float32).reshape(b, SSD_GROUPS, SSD_HPG, SSD_HEAD_DIM, SSD_STATE)
    y, s_fin = ssd_scan(xs, dt, A, Bm, Cm, s0)
    y = y + d_skip.astype(jnp.float32).reshape(SSD_GROUPS, SSD_HPG)[:, :, None] * xs
    y = y.reshape(b, L, D_INNER) * jax.nn.silu(z.astype(jnp.float32))
    yg = y.reshape(b, L, SSD_GROUPS, D_INNER // SSD_GROUPS)
    yg = yg * lax.rsqrt(jnp.mean(yg * yg, axis=-1, keepdims=True) + EPS)
    y = yg.reshape(b, L, D_INNER) * norm_w.astype(jnp.float32)
    new_ssm = s_fin.reshape(b, SSD_HEADS, SSD_HEAD_DIM, SSD_STATE)
    return y.astype(z.dtype), new_conv, new_ssm.astype(z.dtype)

def pool_branch(u, pool_buf, start_pos, pool_w, pool_scale):
    b, L, _ = u.shape
    cat = jnp.concatenate([pool_buf.astype(u.dtype), u], axis=1)
    new_buf = cat[:, -POOL_BUF:]
    cs = jnp.cumsum(cat.astype(jnp.float32), axis=1)
    cs = jnp.concatenate([jnp.zeros((b, 1, POOL_WIDTH), jnp.float32), cs], axis=1)
    end = cs[:, POOL_BUF + 1:]
    pos = start_pos + jnp.arange(L, dtype=jnp.int32)
    parts = []
    for gi, w in enumerate(POOL_WINDOWS):
        lo, hi = gi * POOL_GW, (gi + 1) * POOL_GW
        wsum = end[..., lo:hi] - cs[:, POOL_BUF + 1 - w:POOL_BUF + 1 - w + L, lo:hi]
        cnt = jnp.minimum(w, pos + 1).astype(jnp.float32)[None, :, None]
        parts.append(wsum / cnt)
    mean = jnp.concatenate(parts, axis=-1)
    d = (mean - u.astype(jnp.float32)).reshape(b, L, POOL_GROUPS, POOL_GW)
    out = jnp.einsum('blgc,gcd->blgd', d, pool_w.astype(jnp.float32)).reshape(b, L, POOL_WIDTH)
    out = out * pool_scale.astype(jnp.float32)
    return out.astype(u.dtype), new_buf

def cross_attn(h, mem_k, mem_v, w_xq, w_xo):
    b, L, _ = h.shape
    q = (h @ w_xq).reshape(b, L, X_HEADS, X_HEAD_DIM)
    s = jnp.einsum('blhd,bmhd->bhlm', q.astype(jnp.float32), mem_k.astype(jnp.float32)) * (X_HEAD_DIM ** -0.5)
    pr = jax.nn.softmax(s, axis=-1)
    o = jnp.einsum('bhlm,bmhd->blhd', pr, mem_v.astype(jnp.float32)).reshape(b, L, D_MODEL)
    return o.astype(h.dtype) @ w_xo

def layer(x, conv_buf, ssm0, pool_buf, mem_k, mem_v, start_pos, p):
    u = rmsnorm(x, p['norm_mix'])
    proj = u @ p['w_in']
    z = proj[..., :OFF_XBC]
    xbc = proj[..., OFF_XBC:OFF_DT]
    dt_raw = proj[..., OFF_DT:OFF_POOL]
    pu = proj[..., OFF_POOL:OFF_GA]
    ga = proj[..., OFF_GA:OFF_GB]
    gb = proj[..., OFF_GB:]
    ya, new_conv, new_ssm = ssd_branch(z, xbc, dt_raw, conv_buf, ssm0, p['conv_w'], p['conv_b'],
                                       p['dt_bias'], p['a_log'], p['d_skip'], p['ssd_norm'])
    yb, new_pool = pool_branch(pu, pool_buf, start_pos, p['pool_w'], p['pool_scale'])
    merged = jax.nn.sigmoid(ga) * (ya @ p['w_ssd_proj']) + jax.nn.sigmoid(gb) * yb
    x = x + merged @ p['w_o']
    x = x + cross_attn(rmsnorm(x, p['norm_x']), mem_k, mem_v, p['w_xq'], p['w_xo'])
    hmid = rmsnorm(x, p['norm_mlp']) @ p['w_up']
    x = x + jnp.square(jax.nn.relu(hmid)) @ p['w_down']
    return x, new_conv, new_ssm, new_pool

def setup_inputs(seed: int = 0) -> dict:
    key = jax.random.key(seed)
    ks = jax.random.split(key, 40)
    f32 = jnp.float32
    nrm = lambda k, shape, scale: jax.random.normal(k, shape, f32) * scale
    dt0 = jnp.exp(jax.random.uniform(ks[10], (DEPTH, SSD_HEADS), f32) * (np.log(0.1) - np.log(0.001)) + np.log(0.001))
    dt_bias = dt0 + jnp.log(-jnp.expm1(-dt0))
    a_log = jnp.log(jax.random.uniform(ks[11], (DEPTH, SSD_HEADS), f32, 1.0, 16.0))
    return {
        'x_prompt': nrm(ks[0], (BATCH, SEQ, D_MODEL), 1.0),
        'x_sample': nrm(ks[1], (DEC_BATCH, DEC_SEQ, D_MODEL), 1.0),
        'mem_prompt': nrm(ks[2], (BATCH, MEM_LEN, D_MODEL), 1.0),
        'state_ssm': nrm(ks[3], (DEPTH, DEC_BATCH, SSD_HEADS, SSD_HEAD_DIM, SSD_STATE), 0.1),
        'state_conv': nrm(ks[4], (DEPTH, DEC_BATCH, CONV_WIDTH - 1, CONV_DIM), 1.0),
        'state_pool': nrm(ks[5], (DEPTH, DEC_BATCH, POOL_BUF, POOL_WIDTH), 1.0),
        'cache_mem_k': nrm(ks[6], (DEPTH, DEC_BATCH, MEM_LEN, X_HEADS, X_HEAD_DIM), 1.0),
        'cache_mem_v': nrm(ks[7], (DEPTH, DEC_BATCH, MEM_LEN, X_HEADS, X_HEAD_DIM), 1.0),
        'norm_mix': 1.0 + nrm(ks[8], (DEPTH, D_MODEL), 0.02),
        'w_in': nrm(ks[9], (DEPTH, D_MODEL, IN_DIM), D_MODEL ** -0.5),
        'conv_w': nrm(ks[12], (DEPTH, CONV_WIDTH, CONV_DIM), CONV_WIDTH ** -0.5),
        'conv_b': nrm(ks[13], (DEPTH, CONV_DIM), 0.01),
        'dt_bias': dt_bias,
        'a_log': a_log,
        'd_skip': 1.0 + nrm(ks[14], (DEPTH, SSD_HEADS), 0.02),
        'ssd_norm': 1.0 + nrm(ks[15], (DEPTH, D_INNER), 0.02),
        'w_ssd_proj': nrm(ks[16], (DEPTH, D_INNER, D_MODEL), D_INNER ** -0.5),
        'pool_w': nrm(ks[17], (DEPTH, POOL_GROUPS, POOL_GW, POOL_GW), POOL_GW ** -0.5),
        'pool_scale': 1.0 + nrm(ks[18], (DEPTH, POOL_WIDTH), 0.1),
        'w_o': nrm(ks[19], (DEPTH, D_MODEL, D_MODEL), D_MODEL ** -0.5),
        'norm_x': 1.0 + nrm(ks[20], (DEPTH, D_MODEL), 0.02),
        'w_xq': nrm(ks[21], (DEPTH, D_MODEL, D_MODEL), D_MODEL ** -0.5),
        'w_xk': nrm(ks[22], (DEPTH, D_MODEL, D_MODEL), D_MODEL ** -0.5),
        'w_xv': nrm(ks[23], (DEPTH, D_MODEL, D_MODEL), D_MODEL ** -0.5),
        'w_xo': nrm(ks[24], (DEPTH, D_MODEL, D_MODEL), D_MODEL ** -0.5),
        'norm_mlp': 1.0 + nrm(ks[25], (DEPTH, D_MODEL), 0.02),
        'w_up': nrm(ks[26], (DEPTH, D_MODEL, D_FF), D_MODEL ** -0.5),
        'w_down': nrm(ks[27], (DEPTH, D_FF, D_MODEL), D_FF ** -0.5),
        'norm_final': 1.0 + nrm(ks[28], (D_MODEL,), 0.02),
    }

def reference(x_prompt, x_sample, mem_prompt, state_ssm, state_conv, state_pool, cache_mem_k, cache_mem_v,
              norm_mix, w_in, conv_w, conv_b, dt_bias, a_log, d_skip, ssd_norm, w_ssd_proj, pool_w, pool_scale,
              w_o, norm_x, w_xq, w_xk, w_xv, w_xo, norm_mlp, w_up, w_down, norm_final):
    bp = x_prompt.shape[0]
    dtp = x_prompt.dtype
    hp, hs = x_prompt, x_sample
    ssm_p, conv_p, pool_p, mk_p, mv_p = [], [], [], [], []
    ssm_s, conv_s, pool_s = [], [], []
    zero_conv = jnp.zeros((bp, CONV_WIDTH - 1, CONV_DIM), dtp)
    zero_ssm = jnp.zeros((bp, SSD_HEADS, SSD_HEAD_DIM, SSD_STATE), dtp)
    zero_pool = jnp.zeros((bp, POOL_BUF, POOL_WIDTH), dtp)
    for l in range(DEPTH):
        p = dict(norm_mix=norm_mix[l], w_in=w_in[l], conv_w=conv_w[l], conv_b=conv_b[l], dt_bias=dt_bias[l],
                 a_log=a_log[l], d_skip=d_skip[l], ssd_norm=ssd_norm[l], w_ssd_proj=w_ssd_proj[l],
                 pool_w=pool_w[l], pool_scale=pool_scale[l], w_o=w_o[l], norm_x=norm_x[l], w_xq=w_xq[l],
                 w_xo=w_xo[l], norm_mlp=norm_mlp[l], w_up=w_up[l], w_down=w_down[l])
        mk = (mem_prompt @ w_xk[l]).reshape(bp, MEM_LEN, X_HEADS, X_HEAD_DIM)
        mv = (mem_prompt @ w_xv[l]).reshape(bp, MEM_LEN, X_HEADS, X_HEAD_DIM)
        hp, nc, ns, npool = layer(hp, zero_conv, zero_ssm, zero_pool, mk, mv, 0, p)
        ssm_p.append(ns); conv_p.append(nc); pool_p.append(npool); mk_p.append(mk); mv_p.append(mv)
        hs, nc, ns, npool = layer(hs, state_conv[l], state_ssm[l], state_pool[l],
                                  cache_mem_k[l], cache_mem_v[l], PAST_LEN, p)
        ssm_s.append(ns); conv_s.append(nc); pool_s.append(npool)
    y_prompt = rmsnorm(hp, norm_final)
    y_sample = rmsnorm(hs, norm_final)
    return (y_prompt, y_sample,
            jnp.stack(ssm_p), jnp.stack(conv_p), jnp.stack(pool_p), jnp.stack(mk_p), jnp.stack(mv_p),
            jnp.stack(ssm_s), jnp.stack(conv_s), jnp.stack(pool_s))


_drawn_inputs = setup_inputs


def setup_inputs(seed=0):
    import zlib

    import numpy as np

    out = dict(_drawn_inputs(seed))
    spreads = {}
    factors = {'conv_b': 3.355,
     'd_skip': 24.055,
     'ssd_norm': 5.836,
     'norm_x': 28.971,
     'norm_mlp': 3.412,
     'norm_final': 7.465,
     'pool_scale': 3.012}
    for name, (base, spread) in spreads.items():
        noise = np.random.default_rng([zlib.crc32(name.encode()), seed]).standard_normal(out[name].shape)
        drawn = base * np.exp(spread * noise) if base else spread * noise
        out[name] = __import__('jax').numpy.asarray(drawn.astype(out[name].dtype))
    for name, factor in factors.items():
        out[name] = (out[name] * factor).astype(out[name].dtype)
    return out
```

```python
from contextlib import ExitStack

import concourse.bass as bass
from concourse import mybir

P = 128
D = 1024
KT = D // P
SEQ = 512
NS = 8
TT = SEQ + NS
HALF = TT // 2
NCH = SEQ // P
HEADS, HD, N_STATE, GROUPS = 32, 64, 128, 4
HPG = HEADS // GROUPS
GW = HPG * HD
D_INNER = HEADS * HD
CONV_DIM = D_INNER + 2 * GROUPS * N_STATE
CT = CONV_DIM // P
XT_TILES = D_INNER // P
TAPS = 4
EDGE = TAPS - 1 + NS
OFF_XBC, OFF_DT = D_INNER, D_INNER + CONV_DIM
OFF_POOL = OFF_DT + HEADS
OFF_GA, OFF_GB = OFF_POOL + D, OFF_POOL + 2 * D
IN_DIM = OFF_GB + D
PBUF = 15
PEDGE = PBUF + NS
WINDOWS = (2, 4, 8, 16)
MEM = 256
XH, XD = 4, 256
D_FF = 4 * D
EPS = 1e-6
UW = 256
NEG = -1.0e30

F32 = mybir.dt.float32
R32 = mybir.dt.float32r
BF16 = mybir.dt.bfloat16
ALU = mybir.AluOpType
ACT = mybir.ActivationFunctionType
AX = mybir.AxisListType

T_XBC = 0
T_Z = T_XBC + CT
T_PU = T_Z + 16
T_GA = T_PU + 8
T_GB = T_GA + 8
T_POOL = T_GB + 8
T_SSD = T_POOL + 2
T_O = T_SSD + 16
T_K = T_O + 8
T_V = T_K + 8
T_Q = T_V + 8
T_XO = T_Q + 8
T_MLP = T_XO + 8
FF_CHUNKS = D_FF // D
T_END = T_MLP + 16 * FF_CHUNKS


class Chain:

    def __init__(self, eng, sem):
        self.eng, self.sem, self.n, self.extra = eng, sem, 0, 0

    def __call__(self, ins):
        self.n += 1
        ins.then_inc(self.sem, 1)
        self.eng.wait_ge(self.sem, self.n + self.extra)

    def loop(self, i, per):
        self.start, self.per, self.extra = self.n, per, i * per

    def end(self, times):
        assert self.n - self.start == self.per, (self.n - self.start, self.per)
        self.n, self.extra = self.start + self.per * times, 0


def build(nc, a, o):
    win = a["w_in"][0].rearrange("(k p) m -> p k m", p=P)
    x_dram = nc.dram_tensor("residual_spill", (P, KT * TT), F32, kind="Internal").ap()

    with ExitStack() as ctx:
        base = (nc.sbuf_base + 63) // 32 * 32
        R_RING = base
        R_A = R_RING + 32768
        R_1 = R_A + 2 * KT * TT * 4
        R_2 = R_1 + 2 * KT * TT * 4
        R_3 = R_2 + 2 * KT * TT * 4
        R_4 = R_3 + KT * TT * 4
        R_4N = R_4 + 2 * KT * TT * 4
        R_4S = R_4N + 12480
        R_5 = R_4N + 18720

        def at(name, shape, off, dt=F32):
            return nc.alloc_sbuf_tensor_at(name, shape, dt, offset=off)

        cur = [R_5 // 32 * 32]

        def const(name, shape, dt=F32):
            n = 1
            for d in shape[1:]:
                n *= d
            n *= 2 if dt == BF16 else 4
            t = at(name, shape, cur[0], dt)
            cur[0] += (n + 31) // 32 * 32
            return t

        w_raw = at("w_raw", [P, 2, KT, UW], R_RING)
        w_hi = at("w_hi", [P, 2, KT, P], R_RING + 16384, R32)
        w_lo = at("w_lo", [P, 2, KT, P], R_RING + 24576, R32)
        SZ = KT * TT * 4
        a_hi, a_lo = (at(n, [P, KT, TT], R_A + k * SZ, R32) for k, n in enumerate(("a_hi", "a_lo")))
        x0 = at("x0", [P, KT, TT], R_1)
        zs = at("zs", [P, 16, TT], R_1)
        c_hi, c_lo = (at(n, [P, KT, TT], R_1 + k * SZ, R32) for k, n in enumerate(("c_hi", "c_lo")))
        x_tok = at("x_tok", [P, NCH, D], R_2)
        xs_tok = at("xs_tok", [P, NCH, D_INNER], R_2)
        b_hi, b_lo = (at(n, [P, KT, TT], R_2 + k * SZ, R32) for k, n in enumerate(("b_hi", "b_lo")))
        qT = at("qT", [P, KT, TT], R_2)
        v_tok = at("v_tok", [P, 2, D], R_2 + SZ)
        kT = at("kT", [P, KT, MEM], R_2 + SZ + 8192)
        pu = at("pu", [P, KT, TT], R_3)
        x = at("x", [P, KT, TT], R_3)
        bc = at("bc", [P, 8, TT], R_4)
        gate_a = at("gate_a", [P, KT, TT], R_4)
        conv_rows = at("conv_rows", [NS * 3, CONV_DIM], R_4)
        spread = at("spread", [HEADS, 16, P], R_4)
        pool_rows = at("pool_rows", [NS * PBUF, D], R_4 + 12288)
        mem_hi = at("mem_hi", [P, KT, MEM], R_4, R32)
        mem_lo = at("mem_lo", [P, KT, MEM], R_4 + 8192, R32)
        y_tok = at("y_tok", [P, NCH, D], R_4)
        g = R_4 + SZ
        cbuf = [at(f"cbuf{k}", [P, TAPS - 1 + TT], g + 2112 * k) for k in range(2)]
        hbuf = [at(f"hbuf{k}", [P, SEQ], g + 4224 + 2048 * k) for k in range(2)]
        tbuf = at("tbuf", [P, SEQ], g + 8320)
        abuf = [at(f"abuf{k}", [P, SEQ], g + 10368 + 2048 * k) for k in range(2)]
        decay = at("decay", [P, HPG, P], g)
        xdt = at("xdt", [P, GW], g + 4096)
        xdd = at("xdd", [P, GW], g + 6144)
        xskip = at("xskip", [P, GW], g + 8192)
        yacc = at("yacc", [P, GW], g + 10240)
        b_tok = at("b_tok", [P, N_STATE], g + 12288)
        cbm = at("cbm", [P, P], g + 12800)
        gate_b = at("gate_b", [P, KT, TT], g)
        state_out = at("state_out", [P, 16, N_STATE], g)
        sp_cols = at("sp_cols", [P, KT, NS * PBUF], g + 8192)
        pool_edge = at("pool_edge", [PEDGE, D], g + 12032)
        mem_tok = at("mem_tok", [P, 2, D], g)
        k_tok = at("k_tok", [P, 2, D], g + 8192)
        ys_tok = at("ys_tok", [NS, D], g)
        cache = [at(f"cache{k}", [P, 2, D], off) for k, off in
                 enumerate((R_4, R_4 + 8192, g, g + 8192))]
        sq = [at(f"sq{k}", [P, TT], R_4N + 2080 * k) for k in range(2)]
        ut = [at(f"ut{k}", [P, TT], R_4N + 4160 + 2080 * k) for k in range(2)]
        std = at("std", [P, TT], R_4N + 8320)
        rstd = at("rstd", [P, TT], R_4N + 10400)
        state = at("state", [P, GROUPS, GW], R_4N)
        tz = [at(f"tz{k}", [P, TT], R_4N + 8192 + 2080 * k) for k in range(2)]
        conv_edge = at("conv_edge", [EDGE, CONV_DIM], R_4N)
        sring = [at(f"sring{k}", [P, 8, N_STATE], R_4N + 4096 * k) for k in range(3)]
        bc_s = at("bc_s", [NS, 8 * N_STATE], R_4N + 12288)
        win_sum = [at(f"win_sum{k}", [P, SEQ], R_4N + 12480 + 2048 * k) for k in range(2)]
        st_cols = at("st_cols", [P, CT, NS * 3], R_4N + 16384)
        junk_s = at("junk_s", [P, 8, N_STATE], R_4N + 16384, BF16)
        prob = [at(f"prob{k}", [P, MEM], R_4N + 1024 * k) for k in range(2)]
        probT = [at(f"probT{k}", [P, 2, SEQ], R_4N + 2048 + 4096 * k) for k in range(2)]
        q_tok = at("q_tok", [NS, D], R_4N + 10240)
        junk = at("junk", [P, 2, XH, XD], R_4N + 2048, BF16)
        prob_s = at("prob_s", [32, MEM], R_4N + 15360)
        s_cols = at("s_cols", [P, 64], R_4N + 16384)
        pT_s = at("pT_s", [P, 64], R_4N + 16640)
        stats = at("stats", [P, 80], R_4N + 16896)
        rt = [at(f"rt{k}", [P, TT], R_4N + 2080 * k) for k in range(2)]
        dtw = at("dtw", [P, KT, HEADS], R_3)
        dtw_hi = at("dtw_hi", [P, KT, HEADS], R_3 + 1024, R32)
        dtw_lo = at("dtw_lo", [P, KT, HEADS], R_3 + 2048, R32)
        dtT = at("dtT", [HEADS, 2, TT], R_3 + 3072)
        dt_tmp = [at(f"dt_tmp{k}", [HEADS, TT], R_3 + 7232 + 2080 * k) for k in range(4)]
        xs_row = at("xs_row", [NS, D], R_4)
        vr1 = at("vr1", [56, P], R_4 + 4096)
        vr2 = at("vr2", [120, P], R_4 + 4608)

        ident = const("ident", [P, P])
        identb = const("identb", [P, P], BF16)
        triu = const("triu", [P, P])
        ones = const("ones", [P, P])
        maskneg = const("maskneg", [P, P], BF16)
        cols = const("cols", [P, 176])
        CN_MIX, CN_X, CN_MLP, CN_FIN, C_PS, C_SSD, C_CW, C_CB = 0, 8, 16, 24, 32, 40, 56, 152
        dtk = const("dtk", [P, 2, NCH, HEADS])
        ncs = const("ncs", [P, NCH, HEADS])
        ecs = const("ecs", [P, NCH, HEADS])
        cdec = const("cdec", [P, NCH, HEADS])
        dtd = const("dtd", [P, NCH, HEADS])
        dskip = const("dskip", [P, HEADS])
        rcount = const("rcount", [P, 16])
        xedge = const("xedge", [P, CT, EDGE])
        hcol = const("hcol", [HEADS, 4])
        hs_rhs = const("hs_rhs", [HEADS, 17])
        acts_s = const("acts_s", [P, CT, NS])
        exp_s = const("exp_s", [P, 16, 17])
        xdt_s = const("xdt_s", [P, 16, NS])
        y_s = const("y_s", [P, 16, NS])
        eps_col = const("eps_col", [P, 1])
        tmp_s = const("tmp_s", [P, CT, NS])
        assert cur[0] <= nc.sbuf_usable_end, (cur[0], nc.sbuf_usable_end)

        slot = [ctx.enter_context(nc.psum_tensor(f"slot{k}", [P, 2, 512], F32)) for k in range(2)]
        aux = ctx.enter_context(nc.psum_tensor("aux", [P, 4, 512], F32))

        names = {}

        def sem(name):
            names[name] = ctx.enter_context(nc.semaphore(name))
            return names[name]

        raw_landed = [sem(f"raw_landed{k}") for k in range(2)]
        hi_ready, lo_ready, gemm_done = sem("hi_ready"), sem("lo_ready"), sem("gemm_done")
        evacuated = [sem(f"evacuated{k}") for k in range(2)]
        v_step, a_step, p_step = sem("v_step"), sem("a_step"), sem("p_step")
        consts, x_in, s_in, vec_in, small_in = (sem(n) for n in ("consts", "x_in", "s_in", "vec_in", "small_in"))
        xtr_done, xtr_evac = sem("xtr_done"), sem("xtr_evac")
        sq_ready, sq_used, std_ready = (sem(n) for n in ("sq_ready", "sq_used", "std_ready"))
        ut_ready, uh_ready, u_ready = sem("ut_ready"), sem("uh_ready"), sem("u_ready")
        spilled, reloaded = sem("spilled"), sem("reloaded")
        dtw_hi_s, dtw_lo_s, dt_mm, dt_evac = (sem(n) for n in ("dtw_hi_s", "dtw_lo_s", "dt_mm", "dt_evac"))
        dt_a, dt_b, dt_tr, dt_trv, cs_mm, cs_v = (sem(n) for n in ("dt_a", "dt_b", "dt_tr", "dt_trv", "cs_mm", "cs_v"))
        conv_done, tanh_done, act_ready = sem("conv_done"), sem("tanh_done"), sem("act_ready")
        xtr2_done, xtr2_evac = sem("xs_turned"), sem("xs_stored")
        bc_ready = sem("bc_ready")
        cb_ready, exp_a, exp_b, x_prep, m_ready = (sem(n) for n in ("cb_ready", "exp_a", "exp_b", "x_prep", "m_ready"))
        off_ready, y_mm, skip_ready, y_ready, tz_ready = (sem(n) for n in ("off_ready", "y_mm", "skip_ready", "y_ready", "tz_ready"))
        st_zero = sem("st_zero")
        pre_in, pre_tr, pre_ev = sem("pre_in"), sem("pre_tr"), sem("pre_ev")
        out_ssm, out_edge, out_pool, out_sst, out_kv, out_y = (sem(n) for n in ("out_ssm", "out_edge", "out_pool", "out_sst", "out_kv", "out_y"))
        smp_a, smp_mm, smp_v = sem("smp_a"), sem("smp_mm"), sem("smp_v")
        st_in = [sem(f"st_in{k}") for k in range(3)]
        st_out = [sem(f"st_out{k}") for k in range(3)]
        st_dec, st_new, bc_mm, bc_used = sem("st_dec"), sem("st_new"), sem("bc_mm"), sem("bc_used")
        gate_t = sem("gate_t")
        pool_sum, pool_sum_s, pool_hi, pool_lo, pool_mm, pool_ev = (sem(n) for n in ("pool_sum", "pool_sum_s", "pool_hi", "pool_lo", "pool_mm", "pool_ev"))
        yt_mm, yt_ev = sem("yt_mm"), sem("yt_ev")
        mg_ready, mgh_ready, mgl_ready = sem("mg_ready"), sem("mgh_ready"), sem("mgl_ready")
        mem_in, mem_tr, mem_hi_s, mem_lo_s = (sem(n) for n in ("mem_in", "mem_tr", "mem_hi_s", "mem_lo_s"))
        kt_mm, kt_ev = sem("kt_mm"), sem("kt_ev")
        cache_in = [sem(f"cache_in{k}") for k in range(4)]
        cache_used = sem("cache_used")
        qt_mm, qt_ev, qb_mm, sc_s = (sem(n) for n in ("qt_mm", "qt_ev", "qb_mm", "sc_s"))
        sm_a, sm_b, sm_c, sm_d, sm_e, sm_f = (sem(f"sm_{n}") for n in "abcdef")
        score_mm, negmax, prob_exp, prob_n, pt_mm, pt_ev, pv_mm, pv_hi, pv_lo = (
            sem(n) for n in ("score_mm", "negmax", "prob_exp", "prob_n", "pt_mm", "pt_ev", "pv_mm", "pv_hi", "pv_lo"))
        o_s_hi, o_s_lo = sem("o_s_hi"), sem("o_s_lo")
        relu_done, ff_sq, ff_hi, ff_lo = (sem(n) for n in ("relu_done", "ff_sq", "ff_hi", "ff_lo"))
        fin_n, fin_mm, fin_ev = sem("fin_n"), sem("fin_mm"), sem("fin_ev")

        block = ctx.enter_context(nc.Block())

        def halves(t):
            return t.rearrange("p (h n) -> p h n", h=2)

        def in_slot(k):
            return slot[k][:, :, 0:HALF]

        def uses(t):
            if t <= T_POOL:
                return t // 2
            if t < T_O:
                return T_POOL // 2 + (t - T_SSD) // 4
            return T_POOL // 2 + 4 + (t - T_O) // 2

        def load_unit(sp, u, src, i=0, step=0):
            if u >= 2:
                sp.wait_ge(lo_ready, 2 * u - 2 + i * step)
            sp.dma_start(w_raw[:, u % 2], src).then_inc(raw_landed[u % 2], 16)

        def split_hi(act, t, i=0, step=0):
            if t >= T_END:
                return
            if t % 2 == 0:
                act.wait_ge(raw_landed[t // 2 % 2], 16 * (t // 4 + 1) + i * (4 * step))
            if t >= 2:
                act.wait_ge(gemm_done, t - 1 + i * step)
            nc.scalar.activation(w_hi[:, t % 2], w_raw[:, t // 2 % 2, :, t % 2 * P:t % 2 * P + P],
                                 ACT.Copy).then_inc(hi_ready, 1)

        def split_lo(dve, t, i=0, step=0):
            if t >= T_END:
                return
            dve.wait_ge(hi_ready, t + 1 + i * step)
            nc.vector.tensor_tensor(w_lo[:, t % 2], w_raw[:, t // 2 % 2, :, t % 2 * P:t % 2 * P + P],
                                    w_hi[:, t % 2].bitcast(F32), ALU.subtract).then_inc(lo_ready, 1)

        def gemm(pe, t, hi, lo, i=0, step=0, kts=range(KT), ktwait=None, start=True, stop=True):
            k0 = kts[0] == 0
            if k0:
                pe.wait_ge(lo_ready, t + 1 + i * step)
                if start:
                    pe.wait_ge(evacuated[t % 2], uses(t) + 1 + i * (step // 2))
            for k in kts:
                if ktwait is not None:
                    ktwait(k)
                for n, (w, act) in enumerate(((w_hi, hi), (w_hi, lo), (w_lo, hi))):
                    for h in range(2):
                        last = nc.tensor.matmul(slot[t % 2][:, h, 0:HALF], w[:, t % 2, k, :],
                                                act[:, k, h * HALF:(h + 1) * HALF],
                                                start=(start and k == 0 and n == 0),
                                                stop=(stop and k == KT - 1 and n == 2))
            if kts[-1] == KT - 1:
                last.then_inc(gemm_done, 1)

        def unit_src(name, cb, row=0):
            return a[name][0][row:row + D].rearrange("(k p) m -> p k m", p=P)[:, :, cb * UW:(cb + 1) * UW]

        @block.sync
        def _(sp):
            for u in range(4):
                load_unit(sp, u, win[:, :, OFF_XBC + u * UW:OFF_XBC + (u + 1) * UW])
            with sp.Fori(0, 2) as i:
                for u in range(4):
                    load_unit(sp, 4 + u, win[:, :, bass.ds(OFF_XBC + D + u * UW + i * D, UW)], i, 8)
            with sp.Fori(0, 2) as i:
                for u in range(4):
                    load_unit(sp, T_Z // 2 + u, win[:, :, bass.ds(u * UW + i * D, UW)], i, 8)
            with sp.Fori(0, 3) as i:
                for u in range(4):
                    load_unit(sp, T_PU // 2 + u, win[:, :, bass.ds(OFF_POOL + u * UW + i * D, UW)], i, 8)
            load_unit(sp, T_POOL // 2, a["pool_w"][0].rearrange("g (k p) d -> p (g k) d", p=P))
            for u in range(8):
                load_unit(sp, T_SSD // 2 + u, unit_src("w_ssd_proj", u // 2, D * (u % 2)))
            for n, name in enumerate(("w_o", "w_xk", "w_xv", "w_xq", "w_xo")):
                for u in range(4):
                    load_unit(sp, T_O // 2 + 4 * n + u, unit_src(name, u))
            up = a["w_up"][0].rearrange("(k p) m -> p k m", p=P)
            down = a["w_down"][0].rearrange("(j k p) m -> p j k m", p=P, k=KT)
            with sp.Fori(0, FF_CHUNKS) as i:
                for u in range(4):
                    load_unit(sp, T_MLP // 2 + u, up[:, :, bass.ds(i * D + u * UW, UW)], i, 16)
                for u in range(4):
                    load_unit(sp, T_MLP // 2 + 4 + u, down[:, i, :, u * UW:(u + 1) * UW], i, 16)

        @block.gpsimd
        def _(pool):
            chain = Chain(pool, p_step)
            nc.gpsimd.memset(ident[:], 0.0)
            nc.gpsimd.memset(identb[:], 0.0)
            nc.gpsimd.memset(ones[:], 1.0)
            nc.gpsimd.memset(triu[:], 1.0)
            nc.gpsimd.memset(maskneg[:], 0.0)
            for k in range(2):
                nc.gpsimd.memset(cbuf[k][:, 0:TAPS - 1], 0.0)
            for j in range(16):
                ins = nc.gpsimd.memset(rcount[:, j:j + 1], 1.0 / (j + 1))
            chain(ins)
            nc.gpsimd.affine_select(out=ident[:], in_=ident[:], compare_op=ALU.not_equal, fill=1.0, base=0,
                                    pattern=[[-1, P]], channel_multiplier=1).then_inc(consts, 1)
            nc.gpsimd.affine_select(out=identb[:], in_=identb[:], compare_op=ALU.not_equal, fill=1.0, base=0,
                                    pattern=[[-1, P]], channel_multiplier=1).then_inc(consts, 1)
            nc.gpsimd.affine_select(out=triu[:], in_=triu[:], compare_op=ALU.is_ge, fill=0.0, base=0,
                                    pattern=[[1, P]], channel_multiplier=-1).then_inc(consts, 1)
            nc.gpsimd.affine_select(out=maskneg[:], in_=maskneg[:], compare_op=ALU.is_ge, fill=NEG, base=0,
                                    pattern=[[1, P]], channel_multiplier=-1).then_inc(consts, 1)
            pool.dma_start(o["conv_sample"][0, :, 0:2, :], a["state_conv"][0, :, 1:3, :]).then_inc(out_edge, 16)
            pool.dma_start(o["pool_sample"][0, :, 0:PBUF - 1, :], a["state_pool"][0, :, 1:PBUF, :]).then_inc(out_pool, 16)
            pool.wait_ge(xtr_evac, 10)
            pool.dma_start(x_dram, x0[:].rearrange("p k n -> p (k n)")).then_inc(spilled, 16)
            pool.wait_ge(u_ready, KT)
            nc.gpsimd.memset(state[:], 0.0).then_inc(st_zero, 1)

            def skip_term(c, gr, s):
                pool.wait_ge(x_prep, s)
                nc.gpsimd.tensor_tensor(
                    xskip[:].rearrange("p (h d) -> p h d", h=HPG),
                    xs_tok[:, c, gr * GW:(gr + 1) * GW].rearrange("p (h d) -> p h d", h=HPG),
                    dskip[:, gr * HPG:(gr + 1) * HPG].unsqueeze(2).to_broadcast([P, HPG, HD]),
                    ALU.mult).then_inc(skip_ready, 1)

            with pool.Fori(0, NCH) as i:
                for gr in range(GROUPS):
                    skip_term(i, gr, 4 * i + gr + 1)

            pool.wait_ge(y_ready, 16)
            pool.dma_start(conv_rows[:], a["state_conv"][0].rearrange("b k c -> (b k) c")).then_inc(pre_in, 16)
            pool.dma_start(pool_rows[:], a["state_pool"][0].rearrange("b k c -> (b k) c")).then_inc(pre_in, 16)
            pool.wait_ge(pre_ev, 4)
            pool.dma_start(o["ssm_prompt"][0, 0].rearrange("(t h) p n -> (h p) t n", h=2), state_out[:]).then_inc(out_ssm, 16)
            pool.wait_ge(pre_ev, 6)
            pool.dma_start(o["pool_prompt"][0, 0], pool_edge[0:PBUF, :]).then_inc(out_pool, 16)
            pool.dma_start(o["pool_sample"][0, :, PBUF - 1, :], pool_edge[PBUF:PEDGE, :]).then_inc(out_pool, 16)
            pool.wait_ge(pre_ev, 12)
            pool.dma_start(o["conv_prompt"][0, 0], conv_edge[0:3, :]).then_inc(out_edge, 16)
            pool.dma_start(o["conv_sample"][0, :, 2, :], conv_edge[3:EDGE, :]).then_inc(out_edge, 16)
            pool.wait_ge(out_edge, 48)
            pool.wait_ge(smp_v, 3)
            s_dram = a["state_ssm"][0].rearrange("b (j t h) p n -> b j (h p) t n", j=2, h=2)
            so_dram = o["ssm_sample"][0].rearrange("b (j t h) p n -> b j (h p) t n", j=2, h=2)

            def load_state(n):
                if n >= 3:
                    pool.wait_ge(st_out[n % 3], 16 * (n // 3))
                    pool.wait_ge(bc_used, n - 2)
                pool.dma_start(sring[n % 3][:], s_dram[n // 2, n % 2]).then_inc(st_in[n % 3], 16)

            load_state(0)
            load_state(1)
            for n in range(2 * NS):
                b, j = n // 2, n % 2
                if n >= 1:
                    pool.wait_ge(st_new, n)
                    pool.dma_start(so_dram[(n - 1) // 2, (n - 1) % 2], sring[(n - 1) % 3][:]).then_inc(st_out[(n - 1) % 3], 16)
                if n + 2 < 2 * NS:
                    load_state(n + 2)
                pool.wait_ge(st_in[n % 3], 16 * (n // 3 + 1))
                nc.gpsimd.tensor_tensor(sring[n % 3][:], sring[n % 3][:],
                                        exp_s[:, 8 * j:8 * j + 8, NS + b:NS + b + 1].to_broadcast([P, 8, N_STATE]),
                                        ALU.mult).then_inc(st_dec, 1)
            pool.wait_ge(st_new, 2 * NS)
            pool.dma_start(so_dram[NS - 1, 1], sring[(2 * NS - 1) % 3][:]).then_inc(st_out[(2 * NS - 1) % 3], 16)

            pool.wait_ge(bc_used, 2 * NS)
            for k in range(KT):
                w = WINDOWS[k // 2]
                if k >= 1:
                    pool.wait_ge(pool_sum, k)
                src, span = pu[:, k, 0:SEQ], 1
                bufs = list(win_sum)
                while span < w:
                    dst = bufs[0]
                    nc.gpsimd.tensor_copy(dst[:, 0:span], src[:, 0:span])
                    chain(nc.gpsimd.tensor_tensor(dst[:, span:SEQ], src[:, span:SEQ], src[:, 0:SEQ - span], ALU.add))
                    src, span = dst[:, 0:SEQ], span * 2
                    bufs.reverse()
                dst = bufs[0]
                nc.gpsimd.tensor_scalar(dst[:, w:SEQ], src[:, w:SEQ], 1.0 / w, 1.0, ALU.mult, ALU.mult)
                chain(nc.gpsimd.tensor_tensor(dst[:, 0:w], src[:, 0:w], rcount[:, 0:w], ALU.mult))
                nc.gpsimd.tensor_tensor(pu[:, k, 0:SEQ], dst[:, 0:SEQ], pu[:, k, 0:SEQ], ALU.subtract).then_inc(pool_sum, 1)

            pool.wait_ge(pool_ev, 8)
            pool.wait_ge(spilled, 16)
            pool.dma_start(x[:].rearrange("p k n -> p (k n)"), x_dram).then_inc(reloaded, 16)
            pool.wait_ge(mgl_ready, KT)
            pool.dma_start(mem_tok[:], a["mem_prompt"][0].rearrange("(m p) d -> p m d", p=P)).then_inc(mem_in, 16)
            pool.wait_ge(evacuated[1], uses(T_V) + 1)
            pool.wait_ge(evacuated[0], uses(T_V) + 1)
            pool.dma_start(o["memk_prompt"][0, 0].rearrange("(m p) h d -> p m (h d)", p=P), k_tok[:]).then_inc(out_kv, 16)
            pool.wait_ge(evacuated[1], uses(T_Q) + 1)
            pool.wait_ge(evacuated[0], uses(T_Q) + 1)
            pool.dma_start(o["memv_prompt"][0, 0].rearrange("(m p) h d -> p m (h d)", p=P), v_tok[:]).then_inc(out_kv, 16)
            pool.wait_ge(kt_ev, 4)
            pool.wait_ge(out_kv, 32)
            for n in range(2 * NS):
                if n >= 4:
                    pool.wait_ge(cache_used, n - 3)
                src = a["cache_mem_k" if n < NS else "cache_mem_v"][0, n % NS]
                pool.dma_start(cache[n % 4][:], src.rearrange("(m p) h d -> p m (h d)", p=P)).then_inc(cache_in[n % 4], 16)
            pool.wait_ge(fin_ev, 2)
            pool.dma_start(o["y_sample"].rearrange("b s d -> (b s) d"), ys_tok[:]).then_inc(out_y, 16)
            for c in range(NCH):
                pool.wait_ge(fin_ev, 4 + 2 * c)
                pool.dma_start(o["y_prompt"][0, c * P:(c + 1) * P, :], y_tok[:, c, :]).then_inc(out_y, 16)
            pool.wait_ge(out_y, 16 * (NCH + 1))
            pool.wait_ge(out_ssm, 16)
            pool.wait_ge(out_pool, 48)
            for k in range(3):
                pool.wait_ge(st_out[k], 16 * len(range(k, 2 * NS, 3)))

        @block.scalar
        def _(act):
            chain = Chain(act, a_step)
            act.dma_start(xs_row[:], a["x_sample"].rearrange("b s d -> (b s) d")).then_inc(s_in, 16)
            for n, name in enumerate(("norm_mix", "norm_x", "norm_mlp", "norm_final", "pool_scale")):
                src = a[name] if name == "norm_final" else a[name][0]
                act.dma_start(vr1[8 * n:8 * n + 8, :], src.rearrange("(k p) -> k p", p=P)).then_inc(vec_in, 16)
            act.dma_start(vr1[40:56, :], a["ssd_norm"][0].rearrange("(k p) -> k p", p=P)).then_inc(vec_in, 16)
            act.dma_start(vr2[0:96, :], a["conv_w"][0].rearrange("w (k p) -> (w k) p", p=P)).then_inc(vec_in, 16)
            act.dma_start(vr2[96:120, :], a["conv_b"][0].rearrange("(k p) -> k p", p=P)).then_inc(vec_in, 16)
            act.dma_start(x_tok[:], a["x_prompt"][0].rearrange("(c p) d -> p c d", p=P)).then_inc(x_in, 16)
            act.dma_start(dtw[:], win[:, :, OFF_DT:OFF_DT + HEADS]).then_inc(small_in, 16)
            act.dma_start(hcol[:, 0:1], a["dt_bias"].rearrange("o h -> h o")).then_inc(small_in, 16)
            act.dma_start(hcol[:, 1:2], a["a_log"].rearrange("o h -> h o")).then_inc(small_in, 16)
            act.dma_start(hs_rhs[:, 16:17], a["d_skip"].rearrange("o h -> h o")).then_inc(small_in, 16)
            act.dma_start(dskip[:], a["d_skip"].to_broadcast([P, HEADS])).then_inc(small_in, 16)

            def norm_sum(q, src, ready, n=KT, first=0):
                for k in range(first, first + n):
                    ready(k)
                    if q + k >= 2:
                        act.wait_ge(sq_used, q + k - 1)
                    nc.scalar.activation(sq[k % 2][:], src(k), ACT.Square).then_inc(sq_ready, 1)

            def norm_std(used, scale):
                act.wait_ge(sq_used, used)
                nc.scalar.activation(halves(std[:]), aux[:, 2:4, 0:HALF], ACT.Sqrt, bias=eps_col[:, 0:1],
                                     scale=scale).then_inc(std_ready, 1)

            def norm_hi(q, dst, n=KT):
                for k in range(n):
                    act.wait_ge(ut_ready, q + k + 1)
                    nc.scalar.activation(dst[:, k, :], ut[k % 2][:], ACT.Copy).then_inc(uh_ready, 1)

            norm_sum(0, lambda k: x0[:, k, :], lambda k: act.wait_ge(xtr_evac, 3 + k))
            split_hi(act, 0)
            split_hi(act, 1)
            act.wait_ge(small_in, 80)
            nc.scalar.activation(dtw_hi[:], dtw[:], ACT.Copy).then_inc(dtw_hi_s, 1)
            norm_std(8, 1.0 / D)
            norm_hi(0, a_hi)
            act.wait_ge(dt_evac, 1)
            chain(nc.scalar.activation(dt_tmp[1][:], dt_tmp[0][:], ACT.Abs))
            nc.scalar.activation(dt_tmp[1][:], dt_tmp[1][:], ACT.Exp, scale=-1.0).then_inc(dt_a, 1)
            nc.scalar.activation(hcol[:, 2:3], hcol[:, 1:2], ACT.Exp).then_inc(dt_a, 1)
            act.wait_ge(dt_b, 1)
            nc.scalar.activation(dt_tmp[2][:], dt_tmp[2][:], ACT.Ln).then_inc(dt_a, 1)
            act.wait_ge(cs_mm, 1)
            act.wait_ge(cs_v, 1)
            nc.scalar.activation(ecs[:].rearrange("p c h -> p (c h)"), aux[:, 0, 0:P], ACT.Exp).then_inc(dt_a, 1)
            nc.scalar.activation(cdec[:].rearrange("p c h -> p (c h)"), aux[:, 0, P:2 * P], ACT.Exp).then_inc(dt_a, 1)
            nc.scalar.activation(dtd[:].rearrange("p c h -> p (c h)"), dtd[:].rearrange("p c h -> p (c h)"),
                                 ACT.Exp).then_inc(dt_a, 1)
            nc.scalar.activation(hs_rhs[:, NS:2 * NS], dtT[:, 1, SEQ:TT], ACT.Exp).then_inc(dt_a, 1)

            def conv_front(t, i=0):
                act.wait_ge(gemm_done, t + 1 + i * 8)
                nc.scalar.activation(halves(cbuf[t % 2][:, TAPS - 1:TAPS - 1 + TT]), in_slot(t % 2),
                                     ACT.Copy).then_inc(evacuated[t % 2], 1)
                split_hi(act, t + 2, i, 8)
                act.wait_ge(conv_done, t + 1 + i * 8)
                nc.scalar.activation(tbuf[:], hbuf[t % 2][:], ACT.Tanh).then_inc(tanh_done, 1)

            conv_front(0)
            with act.Fori(0, 2) as i:
                for t in range(8):
                    conv_front(t + 1, i)
                    act.wait_ge(xtr2_done, t + 1 + i * 8)
                    nc.scalar.activation(xs_tok[:, :, bass.ds(i * D + t * P, P)],
                                         aux[:, t % 2, :].rearrange("p (c f) -> p c f", c=NCH),
                                         ACT.Copy).then_inc(xtr2_evac, 1)
            for t in range(17, 24):
                conv_front(t)

            def decays(sem_in, s, c, gr, j0, sem_out):
                act.wait_ge(sem_in, s)
                for j in range(j0, j0 + 4):
                    last = nc.scalar.activation(decay[:, j, :], aux[:, 0, (j - j0) * P:(j - j0 + 1) * P], ACT.Exp,
                                                bias=ncs[:, c, gr * HPG + j:gr * HPG + j + 1])
                last.then_inc(sem_out, 1)

            def z_tile(t, i):
                act.wait_ge(gemm_done, t + 1 + i * 8)
                split_hi(act, t + 2, i, 8)
                nc.scalar.activation(halves(tz[t % 2][:]), in_slot(t % 2), ACT.Tanh, scale=0.5).then_inc(tz_ready, 1)

            def b_turned(s):
                act.wait_ge(cb_ready, s)
                nc.scalar.activation(b_tok[:], aux[:, 3, 0:P], ACT.Copy)

            with act.Fori(0, 2) as i:
                for gr in range(GROUPS):
                    s = 4 * i + gr + 1
                    b_turned(s)
                    decays(cb_ready, s, i, gr, 0, exp_a)
                    z_tile(T_Z + 2 * gr, i)
                    decays(off_ready, s, i, gr, 4, exp_b)
                    z_tile(T_Z + 2 * gr + 1, i)
            with act.Fori(0, 2) as i:
                for gr in range(GROUPS):
                    s = 8 + 4 * i + gr + 1
                    t = T_PU + gr
                    b_turned(s)
                    decays(cb_ready, s, 2 + i, gr, 0, exp_a)
                    decays(off_ready, s, 2 + i, gr, 4, exp_b)
                    act.wait_ge(gemm_done, t + 1 + i * 4)
                    split_hi(act, t + 2, i, 4)
                    nc.scalar.activation(halves(pu[:, 4 * i + gr, :]), in_slot(t % 2),
                                         ACT.Copy).then_inc(evacuated[t % 2], 1)

            act.wait_ge(smp_v, 1)
            nc.scalar.activation(acts_s[:], tmp_s[:], ACT.Tanh).then_inc(smp_a, 1)
            for k in range(8):
                t = T_GA + k
                act.wait_ge(gemm_done, t + 1)
                split_hi(act, t + 2)
                nc.scalar.activation(halves(gate_a[:, k, :]), in_slot(t % 2), ACT.Tanh, scale=0.5).then_inc(evacuated[t % 2], 1)
            act.wait_ge(out_ssm, 16)
            act.wait_ge(out_pool, 48)
            for k in range(8):
                t = T_GB + k
                act.wait_ge(gemm_done, t + 1)
                split_hi(act, t + 2)
                nc.scalar.activation(halves(gate_b[:, k, :]), in_slot(t % 2), ACT.Tanh, scale=0.5).then_inc(evacuated[t % 2], 1)
            act.wait_ge(yt_ev, 16)
            for k in range(KT):
                act.wait_ge(pool_sum, KT)
                act.wait_ge(pool_sum_s, 1)
                nc.scalar.activation(b_hi[:, k, :], pu[:, k, :], ACT.Copy).then_inc(pool_hi, 1)
            for k in range(3):
                act.wait_ge(st_out[k], 16 * len(range(k, 2 * NS, 3)))
            for gr in range(GROUPS):
                norm_sum(8, lambda k: zs[:, k, :], lambda k: act.wait_ge(yt_ev, 17), 4, 4 * gr)
                norm_std(8 + 4 * (gr + 1), 1.0 / (4 * GW))
                if gr == 2:
                    act.wait_ge(pool_mm, 8)
                dst = a_hi if gr < 2 else b_hi
                for k in range(4 * gr, 4 * gr + 4):
                    act.wait_ge(ut_ready, 8 + k + 1)
                    nc.scalar.activation(dst[:, k % 8, :], ut[k % 2][:], ACT.Copy).then_inc(uh_ready, 1)
                if gr == 1:
                    split_hi(act, T_POOL + 2)
                    split_hi(act, T_POOL + 3)
            for c4 in range(4):
                for m in range(2):
                    split_hi(act, T_SSD + 4 * c4 + m + 2)
                for m in range(2):
                    k = 2 * c4 + m
                    split_hi(act, T_SSD + 4 * c4 + m + 4)
                    act.wait_ge(mg_ready, k + 1)
                    nc.scalar.activation(c_hi[:, k, :], ut[k % 2][:], ACT.Copy).then_inc(mgh_ready, 1)

            def res_tile(q, t, k):
                act.wait_ge(gemm_done, t + 1)
                split_hi(act, t + 2)
                act.wait_ge(evacuated[t % 2], uses(t) + 2)
                act.wait_ge(sq_used, q + k - 1)
                nc.scalar.activation(sq[k % 2][:], x[:, k, :], ACT.Square).then_inc(sq_ready, 1)

            for k in range(KT):
                res_tile(24, T_O + k, k)
            norm_std(32, 1.0 / D)
            for n in range(4):
                act.wait_ge(mem_tr, n + 1)
                nc.scalar.activation(mem_hi[:, 2 * n:2 * n + 2, :], aux[:, n % 2, :].rearrange("p (k m) -> p k m", k=2),
                                     ACT.Copy).then_inc(mem_hi_s, 1)
            for k in range(KT):
                act.wait_ge(ut_ready, 24 + k + 1)
                nc.scalar.activation(a_hi[:, k, :], ut[k % 2][:], ACT.Copy).then_inc(uh_ready, 1)
            for k in range(16):
                t = T_K + k
                act.wait_ge(gemm_done, t + 1)
                split_hi(act, t + 2)
                dst = k_tok if k < 8 else v_tok
                nc.scalar.activation(dst[:, :, k % 8 * P:k % 8 * P + P], slot[t % 2][:, 0, 0:2 * P].rearrange("p (m d) -> p m d", m=2),
                                     ACT.Copy).then_inc(evacuated[t % 2], 1)
            for k in range(8):
                t = T_Q + k
                act.wait_ge(gemm_done, t + 1)
                split_hi(act, t + 2)
                nc.scalar.activation(halves(qT[:, k, :]), in_slot(t % 2), ACT.Copy).then_inc(evacuated[t % 2], 1)
            act.wait_ge(sm_b, 1)
            nc.scalar.activation(prob_s[:], aux[0:32, 0, 0:MEM], ACT.Exp, bias=stats[0:32, 1:2], scale=XD ** -0.5,
                                 accum_out=stats[0:32, 2:3]).then_inc(sm_c, 1)
            for n in range(16):
                h, tq = n // 4, n % 4
                act.wait_ge(negmax, n + 1)
                nc.scalar.activation(prob[n % 2][:], aux[:, n % 2, 0:MEM], ACT.Exp, bias=stats[:, 16 + n:17 + n],
                                     scale=XD ** -0.5, accum_out=stats[:, 32 + n:33 + n]).then_inc(prob_exp, 1)
                act.wait_ge(pt_mm, n + 1)
                nc.scalar.activation(probT[h % 2][:, :, tq * P:(tq + 1) * P],
                                     aux[:, 2 + n % 2, 0:MEM].rearrange("p (m l) -> p m l", m=2), ACT.Copy).then_inc(pt_ev, 1)
                if tq == 3:
                    for dt in range(2):
                        act.wait_ge(pv_mm, 2 * h + dt + 1)
                        nc.scalar.activation(c_hi[:, 2 * h + dt, 0:SEQ], slot[dt][:, 0, :], ACT.Copy).then_inc(pv_hi, 1)
            act.wait_ge(cache_used, 2 * NS)
            nc.scalar.activation(c_hi[:, :, SEQ:TT], aux[:, 0, 0:64].rearrange("p (k b) -> p k b", k=KT),
                                 ACT.Copy).then_inc(o_s_hi, 1)
            for k in range(KT):
                res_tile(32, T_XO + k, k)
            norm_std(40, 1.0 / D)
            norm_hi(32, a_hi)

            def ff_up(t, k, n, i=0):
                act.wait_ge(gemm_done, t + 1 + i * 16)
                split_hi(act, t + 2, i, 16)
                nc.scalar.activation(halves(rt[k % 2][:]), in_slot(t % 2), ACT.Relu).then_inc(evacuated[t % 2], 1)
                act.wait_ge(ff_sq, n + 1 + i * 8)
                nc.scalar.activation(c_hi[:, k, :], ut[k % 2][:], ACT.Copy).then_inc(ff_hi, 1)

            with act.Fori(0, FF_CHUNKS - 1) as i:
                for k in range(8):
                    ff_up(T_MLP + k, k, k, i)
                for k in range(8):
                    split_hi(act, T_MLP + 8 + k + 2, i, 16)
            T_LAST = T_MLP + 16 * (FF_CHUNKS - 1)
            for k in range(8):
                ff_up(T_LAST + k, k, 8 * (FF_CHUNKS - 1) + k)
            for k in range(8):
                res_tile(40, T_LAST + 8 + k, k)
            norm_std(48, 1.0 / D)

        @block.vector
        def _(dve):
            chain = Chain(dve, v_step)
            dve.sem_inc(evacuated[0], 1)
            dve.sem_inc(evacuated[1], 1)
            dve.sem_inc(xtr2_evac, 2)
            nc.vector.memset(eps_col[:], EPS).then_inc(consts, 1)

            def norm_scale(q, m, src, gain, dst, n=KT, first=0, split=True):
                dve.wait_ge(std_ready, m + 1)
                chain(nc.vector.reciprocal(rstd[:], std[:]))

                def lo(k):
                    dve.wait_ge(uh_ready, q + k + 1)
                    d = dst(k)
                    nc.vector.tensor_tensor(d[1], ut[k % 2][:], d[0].bitcast(F32), ALU.subtract).then_inc(u_ready, 1)

                for k in range(first, first + n):
                    if k >= first + 2:
                        lo(k - 2)
                        dve.wait_ge(u_ready, q + k - 1)
                    nc.vector.scalar_tensor_tensor(out=ut[k % 2][:], in0=src(k), scalar=cols[:, gain + k:gain + k + 1],
                                                   in1=rstd[:], op0=ALU.mult, op1=ALU.mult).then_inc(ut_ready, 1)
                lo(first + n - 2)
                lo(first + n - 1)

            dve.wait_ge(xtr_done, 1)
            nc.vector.tensor_copy(x0[:, :, SEQ:TT], aux[:, 0, 0:64].rearrange("p (k b) -> p k b", k=KT)).then_inc(xtr_evac, 1)
            dve.wait_ge(xtr_done, 2)
            nc.vector.tensor_copy(cols[:, 0:C_PS], aux[:, 1, 0:C_PS])
            nc.vector.tensor_scalar(cols[:, C_PS:C_SSD], aux[:, 1, C_PS:C_SSD], 0.5, None, ALU.mult)
            nc.vector.tensor_scalar(cols[:, C_SSD:C_CW], aux[:, 1, C_SSD:C_CW], 0.25, None, ALU.mult)
            nc.vector.tensor_scalar(cols[:, C_CW:176], aux[:, 1, C_CW:176], 0.5, None, ALU.mult).then_inc(xtr_evac, 1)
            for k in range(KT):
                dve.wait_ge(xtr_done, 3 + k)
                nc.vector.tensor_copy(x0[:, k, 0:SEQ], aux[:, k % 2, :]).then_inc(xtr_evac, 1)
            split_lo(dve, 0)
            split_lo(dve, 1)
            dve.wait_ge(dtw_hi_s, 1)
            nc.vector.tensor_tensor(dtw_lo[:], dtw[:], dtw_hi[:].bitcast(F32), ALU.subtract).then_inc(dtw_lo_s, 1)
            norm_scale(0, 0, lambda k: x0[:, k, :], CN_MIX, lambda k: (a_hi[:, k, :], a_lo[:, k, :]))

            dve.wait_ge(dt_mm, 1)
            nc.vector.tensor_scalar(halves(dt_tmp[0][:]), aux[0:HEADS, 0:2, 0:HALF], hcol[:, 0:1], None, ALU.add).then_inc(dt_evac, 1)
            dve.wait_ge(dt_a, 2)
            e, w, msk = dt_tmp[1], dt_tmp[2], dt_tmp[3]
            chain(nc.vector.tensor_scalar(w[:], e[:], 1.0, None, ALU.add))
            chain(nc.vector.tensor_scalar(dtT[:, 0, :], w[:], -1.0, None, ALU.add))
            chain(nc.vector.tensor_scalar(msk[:], dtT[:, 0, :], 0.0, None, ALU.is_equal))
            chain(nc.vector.tensor_tensor(dtT[:, 0, :], dtT[:, 0, :], msk[:], ALU.add))
            nc.vector.reciprocal(dtT[:, 0, :], dtT[:, 0, :]).then_inc(dt_b, 1)
            dve.wait_ge(dt_b, 1)
            dve.wait_ge(dt_a, 3)
            chain(nc.vector.tensor_tensor(w[:], w[:], msk[:], ALU.add))
            chain(nc.vector.tensor_tensor(w[:], w[:], dtT[:, 0, :], ALU.mult))
            chain(nc.vector.tensor_tensor(w[:], w[:], e[:], ALU.mult))
            chain(nc.vector.scalar_tensor_tensor(out=dtT[:, 0, :], in0=dt_tmp[0][:], scalar=0.0, in1=w[:],
                                                 op0=ALU.max, op1=ALU.add))
            nc.vector.tensor_copy(hs_rhs[:, 0:NS], dtT[:, 0, SEQ:TT])
            nc.vector.tensor_scalar(dtT[:, 1, :], dtT[:, 0, :], hcol[:, 2:3], -1.0, ALU.mult, ALU.mult).then_inc(dt_b, 1)
            dve.wait_ge(dt_tr, 1)
            nc.vector.tensor_copy(dtk[:].rearrange("p j c h -> p (j c h)"), aux[:, 2, 0:2 * P]).then_inc(dt_trv, 1)
            dve.wait_ge(cs_mm, 1)
            fl = "p c h -> p (c h)"
            chain(nc.vector.tensor_scalar(ncs[:].rearrange(fl), aux[:, 0, 0:P], -1.0, None, ALU.mult))
            nc.vector.tensor_tensor(dtd[:].rearrange(fl), aux[:, 0, P:2 * P], ncs[:].rearrange(fl), ALU.add).then_inc(cs_v, 1)
            dve.wait_ge(dt_a, 6)
            nc.vector.tensor_tensor(dtd[:], dtd[:], dtk[:, 0], ALU.mult).then_inc(cs_v, 1)

            def conv_front(t, dst, done, i=0):
                dve.wait_ge(evacuated[t % 2], t // 2 + 2 + i * 4)
                b = cbuf[t % 2]
                f = t + i * 8
                nc.vector.tensor_copy(xedge[:, f, :], b[:, SEQ:SEQ + EDGE])
                h = hbuf[t % 2][:]
                chain(nc.vector.tensor_scalar(h, b[:, 0:SEQ], cols[:, bass.ds(C_CW + f, 1)], cols[:, bass.ds(C_CB + f, 1)],
                                              ALU.mult, ALU.add))
                for k in range(1, TAPS):
                    ins = nc.vector.scalar_tensor_tensor(out=h, in0=b[:, k:k + SEQ], scalar=cols[:, bass.ds(C_CW + CT * k + f, 1)],
                                                         in1=h, op0=ALU.mult, op1=ALU.add)
                    if k < TAPS - 1:
                        chain(ins)
                    else:
                        ins.then_inc(conv_done, 1)
                split_lo(dve, t + 2, i, 8)
                dve.wait_ge(tanh_done, t + 1 + i * 8)
                nc.vector.scalar_tensor_tensor(out=dst, in0=tbuf[:], scalar=1.0, in1=h, op0=ALU.add,
                                               op1=ALU.mult).then_inc(done, 1)

            conv_front(0, abuf[0][:], act_ready)
            with dve.Fori(0, 2) as i:
                chain.loop(i, 24)
                for t in range(8):
                    conv_front(t + 1, abuf[(t + 1) % 2][:], act_ready, i)
                chain.end(2)
            dve.wait_ge(act_ready, 17)
            nc.vector.tensor_copy(bc[:, 0, 0:SEQ], abuf[0][:]).then_inc(bc_ready, 1)
            for t in range(17, 24):
                conv_front(t, bc[:, t - 16, 0:SEQ], bc_ready)

            def heads(t):
                return t.rearrange("p (h d) -> p h d", h=HPG)

            def prep(c, gr):
                hd = slice(gr * HPG, (gr + 1) * HPG)
                xs = heads(xs_tok[:, c, gr * GW:(gr + 1) * GW])
                nc.vector.tensor_tensor(heads(xdt[:]), xs, dtk[:, 0, c, hd].unsqueeze(2).to_broadcast([P, HPG, HD]), ALU.mult)
                nc.vector.tensor_tensor(heads(xdd[:]), xs, dtd[:, c, hd].unsqueeze(2).to_broadcast([P, HPG, HD]),
                                        ALU.mult).then_inc(x_prep, 1)

            def weights_a(s):
                dve.wait_ge(cb_ready, s)
                chain(nc.vector.tensor_tensor(cbm[:], aux[:, 1, 0:P], triu[:], ALU.mult))
                dve.wait_ge(exp_a, s)
                nc.vector.tensor_tensor(decay[:, 0:4, :], decay[:, 0:4, :], cbm[:].unsqueeze(1).to_broadcast([P, 4, P]), ALU.mult)

            def carry(s, c, gr):
                hd = slice(gr * HPG, (gr + 1) * HPG)
                dve.wait_ge(off_ready, s)
                nc.vector.tensor_tensor(heads(yacc[:]), heads(aux[:, 2, :]), ecs[:, c, hd].unsqueeze(2).to_broadcast([P, HPG, HD]), ALU.mult)
                chain(nc.vector.tensor_tensor(heads(state[:, gr, :]), heads(state[:, gr, :]),
                                              cdec[:, c, hd].unsqueeze(2).to_broadcast([P, HPG, HD]), ALU.mult))
                nc.vector.tensor_tensor(state[:, gr, :], state[:, gr, :], aux[:, 3, :], ALU.add)
                dve.wait_ge(exp_b, s)
                nc.vector.tensor_tensor(decay[:, 4:8, :], decay[:, 4:8, :], cbm[:].unsqueeze(1).to_broadcast([P, 4, P]),
                                        ALU.mult).then_inc(m_ready, 1)

            def finish_y(s, c, gr):
                dve.wait_ge(y_mm, s)
                chain(nc.vector.tensor_tensor(yacc[:], yacc[:], aux[:, 2, :], ALU.add))
                dve.wait_ge(skip_ready, s)
                nc.vector.tensor_tensor(xs_tok[:, c, gr * GW:(gr + 1) * GW], yacc[:], xskip[:], ALU.add).then_inc(y_ready, 1)

            def z_tile(t, k, i):
                split_lo(dve, t + 2, i, 8)
                dve.wait_ge(tz_ready, k + 1 + i * 8)
                nc.vector.scalar_tensor_tensor(out=halves(zs[:, k + i * 8, :]), in0=halves(tz[t % 2][:]), scalar=1.0,
                                               in1=in_slot(t % 2), op0=ALU.add, op1=ALU.mult).then_inc(evacuated[t % 2], 1)

            dve.wait_ge(xtr2_evac, 18)
            dve.wait_ge(bc_ready, 8)
            dve.wait_ge(spilled, 16)
            dve.wait_ge(st_zero, 1)
            dve.wait_ge(cs_v, 2)
            with dve.Fori(0, 2) as i:
                chain.loop(i, 12)
                for gr in range(GROUPS):
                    s = 4 * i + gr + 1
                    prep(i, gr)
                    weights_a(s)
                    z_tile(T_Z + 2 * gr, 2 * gr, i)
                    carry(s, i, gr)
                    z_tile(T_Z + 2 * gr + 1, 2 * gr + 1, i)
                    finish_y(s, i, gr)
                chain.end(2)
            with dve.Fori(0, 2) as i:
                chain.loop(i, 12)
                for gr in range(GROUPS):
                    s = 8 + 4 * i + gr + 1
                    prep(2 + i, gr)
                    weights_a(s)
                    carry(s, 2 + i, gr)
                    split_lo(dve, T_PU + gr + 2, i, 4)
                    finish_y(s, 2 + i, gr)
                chain.end(2)

            for n in range(4):
                dve.wait_ge(pre_tr, n + 1)
                nc.vector.tensor_copy(state_out[:, 4 * n:4 * n + 4, :], aux[:, n, :].rearrange("p (t n) -> p t n", t=4)).then_inc(pre_ev, 1)
            for n in range(2):
                dve.wait_ge(pre_tr, 5 + n)
                nc.vector.tensor_copy(pool_edge[:, n * 512:(n + 1) * 512], aux[0:PEDGE, n, :]).then_inc(pre_ev, 1)
            for n in range(6):
                dve.wait_ge(pre_tr, 7 + n)
                nc.vector.tensor_copy(conv_edge[:, n * 512:(n + 1) * 512], aux[0:EDGE, (2 + n) % 4, :]).then_inc(pre_ev, 1)
            for n in range(2):
                dve.wait_ge(pre_tr, 13 + n)
                nc.vector.tensor_copy(sp_cols[:, 4 * n:4 * n + 4, :],
                                      aux[:, n, 0:480].rearrange("p (k b) -> p k b", k=4)).then_inc(pre_ev, 1)
            for n in range(2):
                dve.wait_ge(pre_tr, 15 + n)
                nc.vector.tensor_copy(st_cols[:, 12 * n:12 * n + 12, :],
                                      aux[:, 2 + n, 0:288].rearrange("p (k b) -> p k b", k=12)).then_inc(pre_ev, 1)
            dve.wait_ge(pre_ev, 16)
            nc.vector.tensor_copy(spread[:].rearrange("h t (j d) -> h (t j) d", j=2),
                                  ident[0:HEADS, 0:HEADS].unsqueeze(2).to_broadcast([HEADS, HEADS, HD])).then_inc(pre_ev, 1)
            for k in range(KT):
                w = WINDOWS[k // 2]
                old = sp_cols[:, k, :].rearrange("p (b j) -> p b j", b=NS)[:, :, PBUF - w + 1:PBUF]
                ins = nc.vector.tensor_reduce(y_s[:, k, :], old, AX.X, ALU.add)
            chain(ins)
            chain(nc.vector.tensor_tensor(y_s[:, 0:KT, :], y_s[:, 0:KT, :], pu[:, :, SEQ:TT], ALU.add))
            for gi, w in enumerate(WINDOWS):
                two = slice(2 * gi, 2 * gi + 2)
                ins = nc.vector.scalar_tensor_tensor(out=pu[:, two, SEQ:TT], in0=y_s[:, two, :], scalar=1.0 / w,
                                                     in1=pu[:, two, SEQ:TT], op0=ALU.mult, op1=ALU.subtract)
            ins.then_inc(pool_sum_s, 1)
            def wcol(k):
                return cols[:, C_CW + CT * k:C_CW + CT * (k + 1)].unsqueeze(2).to_broadcast([P, CT, NS])
            old = st_cols[:].rearrange("p f (b k) -> p f k b", k=3)
            chain(nc.vector.tensor_tensor(tmp_s[:], xedge[:, :, TAPS - 1:EDGE], wcol(3), ALU.mult))
            chain(nc.vector.tensor_tensor(tmp_s[:], tmp_s[:], cols[:, C_CB:C_CB + CT].unsqueeze(2).to_broadcast([P, CT, NS]), ALU.add))
            for k in range(3):
                chain(nc.vector.tensor_tensor(acts_s[:], old[:, :, k, :], wcol(k), ALU.mult))
                ins = nc.vector.tensor_tensor(tmp_s[:], tmp_s[:], acts_s[:], ALU.add)
                if k < 2:
                    chain(ins)
                else:
                    ins.then_inc(smp_v, 1)
            dve.wait_ge(smp_a, 1)
            nc.vector.scalar_tensor_tensor(out=acts_s[:], in0=acts_s[:], scalar=1.0, in1=tmp_s[:], op0=ALU.add,
                                           op1=ALU.mult).then_inc(smp_v, 1)
            dve.wait_ge(smp_mm, 1)
            chain(nc.vector.tensor_copy(exp_s[:].rearrange("p t j -> p (t j)"), aux[:, 0, 0:16 * 17]))
            nc.vector.tensor_tensor(xdt_s[:], acts_s[:, 0:16, :], exp_s[:, :, 0:NS], ALU.mult).then_inc(smp_v, 1)
            dve.wait_ge(smp_mm, 2)
            nc.vector.tensor_copy(bc_s[:, :].rearrange("p (j n) -> p j n", j=2), aux[0:NS, 1:3, :]).then_inc(smp_v, 1)

            for k in range(8):
                split_lo(dve, T_GA + k + 2)
                for j in range(2):
                    n = 2 * k + j
                    dve.wait_ge(st_dec, n + 1)
                    if j == 0:
                        dve.wait_ge(bc_mm, k + 1)
                        dve.wait_ge(smp_v, 4)
                    for t in range(8):
                        tt = 8 * j + t
                        gg = tt // 4
                        S = sring[n % 3][:, t, :]
                        ins = nc.vector.scalar_tensor_tensor(out=S, in0=aux[:, 0, gg * P:(gg + 1) * P],
                                                             scalar=xdt_s[:, tt, k:k + 1], in1=S, op0=ALU.mult, op1=ALU.add)
                    ins.then_inc(st_new, 1)
                    dve.wait_ge(st_new, n + 1)
                    for t in range(8):
                        tt = 8 * j + t
                        gg = tt // 4
                        ins = nc.vector.tensor_tensor_reduce(junk_s[:, t, :], sring[n % 3][:, t, :], aux[:, 1, gg * P:(gg + 1) * P],
                                                             1.0, 0.0, ALU.mult, ALU.add, y_s[:, tt, k:k + 1])
                    ins.then_inc(bc_used, 1)
            dve.wait_ge(bc_used, 16)
            chain(nc.vector.tensor_tensor(tmp_s[:, 0:16, :], acts_s[:, 0:16, :], exp_s[:, :, 16:17].to_broadcast([P, 16, NS]), ALU.mult))
            chain(nc.vector.tensor_tensor(y_s[:], y_s[:], tmp_s[:, 0:16, :], ALU.add))
            nc.vector.tensor_tensor(zs[:, :, SEQ:TT], zs[:, :, SEQ:TT], y_s[:], ALU.mult)
            for k in range(8):
                split_lo(dve, T_GB + k + 2)
                for j in range(2):
                    f = 2 * k + j
                    dve.wait_ge(yt_mm, f + 1)
                    nc.vector.tensor_tensor(zs[:, f, 0:SEQ], aux[:, f % 2, :], zs[:, f, 0:SEQ], ALU.mult).then_inc(yt_ev, 1)
            dve.wait_ge(yt_ev, 16)
            dve.wait_ge(evacuated[0], uses(T_POOL) + 1)
            dve.wait_ge(evacuated[1], uses(T_POOL) + 1)
            nc.vector.tensor_scalar(gate_b[:], gate_b[:], 1.0, None, ALU.add)
            nc.vector.tensor_scalar(gate_a[:], gate_a[:], 1.0, None, ALU.add).then_inc(yt_ev, 1)
            for k in range(KT):
                dve.wait_ge(pool_hi, k + 1)
                nc.vector.tensor_tensor(b_lo[:, k, :], pu[:, k, :], b_hi[:, k, :].bitcast(F32), ALU.subtract).then_inc(pool_lo, 1)

            def y_half(gr):
                dst = (a_hi, a_lo) if gr < 2 else (b_hi, b_lo)
                norm_scale(8, 1 + gr, lambda k: zs[:, k, :], C_SSD, lambda k: (dst[0][:, k % 8, :], dst[1][:, k % 8, :]), 4, 4 * gr)

            y_half(0)
            y_half(1)
            for n in range(8):
                m, gi = n // 4, n % 4
                f = 2 * gi + m
                dve.wait_ge(pool_mm, n + 1)
                nc.vector.scalar_tensor_tensor(out=halves(gate_b[:, f, :]), in0=aux[:, 2 * (n % 2):2 * (n % 2) + 2, 0:HALF],
                                               scalar=cols[:, C_PS + f:C_PS + f + 1], in1=halves(gate_b[:, f, :]),
                                               op0=ALU.mult, op1=ALU.mult).then_inc(pool_ev, 1)
            split_lo(dve, T_POOL + 2)
            split_lo(dve, T_POOL + 3)
            y_half(2)
            y_half(3)

            for c4 in range(4):
                for m in range(2):
                    split_lo(dve, T_SSD + 4 * c4 + m + 2)
                for m in range(2):
                    k = 2 * c4 + m
                    t = T_SSD + 4 * c4 + 2 + m
                    split_lo(dve, t + 2)
                    dve.wait_ge(gemm_done, t + 1)
                    if k >= 2:
                        dve.wait_ge(mgl_ready, k - 1)
                    nc.vector.tensor_tensor(halves(ut[k % 2][:]), in_slot(m), halves(gate_a[:, k, :]), ALU.mult).then_inc(evacuated[m], 1)
                    dve.wait_ge(evacuated[m], uses(T_SSD + 4 * c4 + m) + 2)
                    nc.vector.tensor_tensor(ut[k % 2][:], ut[k % 2][:], gate_b[:, k, :], ALU.add).then_inc(mg_ready, 1)
                    dve.wait_ge(mgh_ready, k + 1)
                    nc.vector.tensor_tensor(c_lo[:, k, :], ut[k % 2][:], c_hi[:, k, :].bitcast(F32), ALU.subtract).then_inc(mgl_ready, 1)

            def residual(t, k, i=0, step=0):
                split_lo(dve, t + 2, i, step)
                dve.wait_ge(gemm_done, t + 1 + i * step)
                nc.vector.tensor_tensor(halves(x[:, k, :]), in_slot(t % 2), halves(x[:, k, :]),
                                        ALU.add).then_inc(evacuated[t % 2], 1)

            dve.wait_ge(reloaded, 16)
            for k in range(KT):
                residual(T_O + k, k)
            for n in range(4):
                dve.wait_ge(mem_hi_s, n + 1)
                nc.vector.tensor_tensor(mem_lo[:, 2 * n:2 * n + 2, :], aux[:, n % 2, :].rearrange("p (k m) -> p k m", k=2),
                                        mem_hi[:, 2 * n:2 * n + 2, :].bitcast(F32), ALU.subtract).then_inc(mem_lo_s, 1)
            norm_scale(24, 5, lambda k: x[:, k, :], CN_X, lambda k: (a_hi[:, k, :], a_lo[:, k, :]))
            for k in range(16):
                split_lo(dve, T_K + k + 2)
            for n in range(4):
                dve.wait_ge(kt_mm, n + 1)
                nc.vector.tensor_copy(kT[:, 2 * n:2 * n + 2, :], aux[:, n, :].rearrange("p (k m) -> p k m", k=2)).then_inc(kt_ev, 1)
            for k in range(8):
                split_lo(dve, T_Q + k + 2)
            dve.wait_ge(qt_mm, 1)
            nc.vector.tensor_copy(q_tok[:].rearrange("p (j n) -> p j n", j=2), aux[0:NS, 0:2, :]).then_inc(qt_ev, 1)
            for b in range(NS):
                dve.wait_ge(qb_mm, b + 1)
                dve.wait_ge(cache_in[b % 4], 16 * (b // 4 + 1))
                if b >= 1:
                    dve.wait_ge(cache_used, b)
                for m in range(2):
                    for h in range(XH):
                        c = m * 32 + b * XH + h
                        ins = nc.vector.tensor_tensor_reduce(junk[:, m, h, :], cache[b % 4][:, m, h * XD:(h + 1) * XD],
                                                             slot[b % 2][:, h // 2, h % 2 * XD:(h % 2 + 1) * XD], 1.0, 0.0,
                                                             ALU.mult, ALU.add, s_cols[:, c:c + 1])
                ins.then_inc(cache_used, 1)
            dve.wait_ge(sm_a, 1)
            chain(nc.vector.tensor_reduce(stats[0:32, 0:1], aux[0:32, 0, 0:MEM], AX.X, ALU.max))
            nc.vector.tensor_scalar(stats[0:32, 1:2], stats[0:32, 0:1], -(XD ** -0.5), None, ALU.mult).then_inc(sm_b, 1)
            dve.wait_ge(sm_c, 1)
            chain(nc.vector.reciprocal(stats[0:32, 3:4], stats[0:32, 2:3]))
            nc.vector.tensor_scalar(prob_s[:], prob_s[:], stats[0:32, 3:4], None, ALU.mult).then_inc(sm_d, 1)
            dve.wait_ge(sm_e, 1)
            nc.vector.tensor_copy(pT_s[:], aux[:, 1, 0:64]).then_inc(sm_f, 1)
            for n in range(16):
                h = n // 4
                dve.wait_ge(score_mm, n + 1)
                chain(nc.vector.tensor_reduce(stats[:, 48 + n:49 + n], aux[:, n % 2, 0:MEM], AX.X, ALU.max))
                nc.vector.tensor_scalar(stats[:, 16 + n:17 + n], stats[:, 48 + n:49 + n], -(XD ** -0.5), None, ALU.mult).then_inc(negmax, 1)
                dve.wait_ge(prob_exp, n + 1)
                chain(nc.vector.reciprocal(stats[:, 64 + n % 16:65 + n % 16], stats[:, 32 + n:33 + n]))
                nc.vector.tensor_scalar(prob[n % 2][:], prob[n % 2][:], stats[:, 64 + n % 16:65 + n % 16], None, ALU.mult).then_inc(prob_n, 1)
                if n % 4 == 3:
                    for dt in range(2):
                        k = 2 * h + dt
                        dve.wait_ge(pv_hi, k + 1)
                        nc.vector.tensor_tensor(c_lo[:, k, 0:SEQ], slot[dt][:, 0, :], c_hi[:, k, 0:SEQ].bitcast(F32),
                                                ALU.subtract).then_inc(pv_lo, 1)
            dve.wait_ge(o_s_hi, 1)
            nc.vector.tensor_tensor(c_lo[:, :, SEQ:TT], aux[:, 0, 0:64].rearrange("p (k b) -> p k b", k=KT),
                                    c_hi[:, :, SEQ:TT].bitcast(F32), ALU.subtract).then_inc(o_s_lo, 1)
            for k in range(KT):
                residual(T_XO + k, k)
            norm_scale(32, 6, lambda k: x[:, k, :], CN_MLP, lambda k: (a_hi[:, k, :], a_lo[:, k, :]))

            def ff_up(t, k, n, i=0):
                split_lo(dve, t + 2, i, 16)
                dve.wait_ge(evacuated[t % 2], uses(t) + 2 + i * 8)
                if k >= 2:
                    dve.wait_ge(ff_lo, n - 1 + i * 8)
                nc.vector.tensor_tensor(ut[k % 2][:], rt[k % 2][:], rt[k % 2][:], ALU.mult).then_inc(ff_sq, 1)
                dve.wait_ge(ff_hi, n + 1 + i * 8)
                nc.vector.tensor_tensor(c_lo[:, k, :], ut[k % 2][:], c_hi[:, k, :].bitcast(F32), ALU.subtract).then_inc(ff_lo, 1)

            with dve.Fori(0, FF_CHUNKS - 1) as i:
                for k in range(8):
                    ff_up(T_MLP + k, k, k, i)
                for k in range(8):
                    residual(T_MLP + 8 + k, k, i, 16)
            T_LAST = T_MLP + 16 * (FF_CHUNKS - 1)
            for k in range(8):
                ff_up(T_LAST + k, k, 8 * (FF_CHUNKS - 1) + k)
            for k in range(8):
                residual(T_LAST + 8 + k, k)
            dve.wait_ge(std_ready, 8)
            chain(nc.vector.reciprocal(rstd[:], std[:]))
            for k in range(KT):
                nc.vector.scalar_tensor_tensor(out=x[:, k, :], in0=x[:, k, :], scalar=cols[:, CN_FIN + k:CN_FIN + k + 1],
                                               in1=rstd[:], op0=ALU.mult, op1=ALU.mult).then_inc(fin_n, 1)
            for n in range(2):
                dve.wait_ge(fin_mm, n + 1)
                nc.vector.tensor_copy(ys_tok[:, n * 512:(n + 1) * 512], aux[0:NS, n, :]).then_inc(fin_ev, 1)
            for n in range(8):
                dve.wait_ge(fin_mm, n + 3)
                nc.vector.tensor_copy(y_tok[:, n // 2, n % 2 * 512:(n % 2 + 1) * 512], aux[:, n % 4, :]).then_inc(fin_ev, 1)

        @block.tensor
        def _(pe):
            pe.wait_ge(consts, 5)
            pe.wait_ge(s_in, 16)
            for k in range(KT):
                last = nc.tensor.transpose(aux[:, 0, NS * k:NS * k + NS], xs_row[:, k * P:(k + 1) * P], ident[0:NS, 0:NS])
            last.then_inc(xtr_done, 1)
            pe.wait_ge(vec_in, 16 * 8)
            nc.tensor.transpose(aux[:, 1, 0:56], vr1[:], ident[0:56, 0:56])
            nc.tensor.transpose(aux[:, 1, 56:176], vr2[:], ident[0:120, 0:120]).then_inc(xtr_done, 1)
            pe.wait_ge(x_in, 16)
            for k in range(KT):
                pe.wait_ge(xtr_evac, k + 1)
                for c in range(NCH):
                    last = nc.tensor.transpose(aux[:, k % 2, c * P:(c + 1) * P], x_tok[:, c, k * P:(k + 1) * P], ident[:])
                last.then_inc(xtr_done, 1)

            def norm_tile(q, k, first, last_one):
                pe.wait_ge(sq_ready, q + k + 1)
                for h in range(2):
                    ins = nc.tensor.matmul(aux[:, 2 + h, 0:HALF], ones[:], sq[k % 2][:, h * HALF:(h + 1) * HALF],
                                           start=first, stop=last_one)
                ins.then_inc(sq_used, 1)
                return ins

            def norm_pe(q, n=KT, first=0, m=0):
                if m:
                    pe.wait_ge(std_ready, m)
                for k in range(first, first + n):
                    norm_tile(q, k, k == first, k == first + n - 1)

            norm_pe(0)
            pe.wait_ge(u_ready, KT)
            pe.wait_ge(dtw_lo_s, 1)
            for k in range(KT):
                for n, (w, u) in enumerate(((dtw_hi, a_hi), (dtw_hi, a_lo), (dtw_lo, a_hi))):
                    for h in range(2):
                        last = nc.tensor.matmul(aux[0:HEADS, h, 0:HALF], w[:, k, :], u[:, k, h * HALF:(h + 1) * HALF],
                                                start=(k == 0 and n == 0), stop=(k == KT - 1 and n == 2))
            last.then_inc(dt_mm, 1)
            gemm(pe, 0, a_hi, a_lo)
            pe.wait_ge(dt_b, 2)
            for j in range(2):
                for c in range(NCH):
                    last = nc.tensor.transpose(aux[:, 2, (j * NCH + c) * HEADS:(j * NCH + c + 1) * HEADS],
                                               dtT[:, j, c * P:(c + 1) * P], ident[0:HEADS, 0:HEADS])
            last.then_inc(dt_tr, 1)
            pe.wait_ge(dt_trv, 1)
            rhs = dtk[:, 1].rearrange("p c h -> p (c h)")
            nc.tensor.matmul(aux[:, 0, 0:P], triu[:], rhs, start=True, stop=True)
            nc.tensor.matmul(aux[:, 0, P:2 * P], ones[:], rhs, start=True, stop=True).then_inc(cs_mm, 1)
            pe.wait_ge(dt_a, 6)
            with pe.Fori(0, 2) as i:
                for t in range(8):
                    gemm(pe, t + 1, a_hi, a_lo, i, 8)
                    pe.wait_ge(act_ready, t + 1 + i * 8)
                    pe.wait_ge(xtr2_evac, t + 1 + i * 8)
                    for c in range(NCH):
                        last = nc.tensor.transpose(aux[:, t % 2, c * P:(c + 1) * P], abuf[t % 2][:, c * P:(c + 1) * P], ident[:])
                    last.then_inc(xtr2_done, 1)
            for t in range(17, 24):
                gemm(pe, t, a_hi, a_lo)
            pe.wait_ge(xtr2_evac, 18)
            pe.wait_ge(bc_ready, 8)

            def rows_of_cs(c, gr, j0):
                nc.tensor.matmul(aux[:, 0, :], identb[:], maskneg[:].unsqueeze(1).to_broadcast([P, 4, P]), start=True, stop=False)
                for j in range(4):
                    h = gr * HPG + j0 + j
                    last = nc.tensor.matmul(aux[:, 0, j * P:(j + 1) * P], dtk[:, 1, c, h:h + 1].to_broadcast([P, P]),
                                            triu[:], start=False, stop=(j == 3))
                return last

            def step_a(c, gr):
                ch = slice(c * P, (c + 1) * P)
                nc.tensor.matmul(aux[:, 1, 0:P], bc[:, gr, ch], bc[:, GROUPS + gr, ch], start=True, stop=True)
                nc.tensor.transpose(aux[:, 3, 0:P], bc[:, gr, ch], ident[:])
                rows_of_cs(c, gr, 0).then_inc(cb_ready, 1)

            def step_b(c, gr, s):
                pe.wait_ge(exp_a, s)
                pe.wait_ge(x_prep, s)
                rows_of_cs(c, gr, 4)
                nc.tensor.matmul(aux[:, 2, :], bc[:, GROUPS + gr, c * P:(c + 1) * P], state[:, gr, :], start=True, stop=True)
                nc.tensor.matmul(aux[:, 3, :], b_tok[:], xdd[:], start=True, stop=True).then_inc(off_ready, 1)

            def step_c(s):
                pe.wait_ge(m_ready, s)
                for j in range(HPG):
                    last = nc.tensor.matmul(aux[:, 2, j * HD:(j + 1) * HD], decay[:, j, :], xdt[:, j * HD:(j + 1) * HD],
                                            start=(j == 0), stop=(j == HPG - 1), skip_group_check=True)
                last.then_inc(y_mm, 1)

            for c in range(NCH):
                for gr in range(GROUPS):
                    s = GROUPS * c + gr + 1
                    step_a(c, gr)
                    if c < 2:
                        gemm(pe, T_Z + 8 * c + 2 * gr, a_hi, a_lo)
                        step_b(c, gr, s)
                        gemm(pe, T_Z + 8 * c + 2 * gr + 1, a_hi, a_lo)
                    else:
                        gemm(pe, T_PU + 4 * (c - 2) + gr, a_hi, a_lo, kts=range(0, 4))
                        step_b(c, gr, s)
                        gemm(pe, T_PU + 4 * (c - 2) + gr, a_hi, a_lo, kts=range(4, 8))
                    step_c(s)

            pe.wait_ge(y_ready, 16)
            for n in range(4):
                for j in range(4):
                    last = nc.tensor.transpose(aux[:, n, j * P:(j + 1) * P], state[:, n, j * P:(j + 1) * P], ident[:])
                last.then_inc(pre_tr, 1)
            pe.wait_ge(evacuated[0], uses(T_GA) + 1)
            pe.wait_ge(evacuated[1], uses(T_GA) + 1)
            for n in range(2):
                pe.wait_ge(pre_ev, n + 1)
                for j in range(4):
                    last = nc.tensor.transpose(aux[0:PEDGE, n, j * P:(j + 1) * P], pu[:, 4 * n + j, SEQ - PBUF:TT], ident[:])
                last.then_inc(pre_tr, 1)
            for n in range(6):
                pe.wait_ge(pre_ev, n + 3)
                for j in range(4):
                    last = nc.tensor.transpose(aux[0:EDGE, (2 + n) % 4, j * P:(j + 1) * P], xedge[:, 4 * n + j, :], ident[:])
                last.then_inc(pre_tr, 1)
            pe.wait_ge(pre_in, 32)
            for n in range(2):
                pe.wait_ge(pre_ev, 9 + n)
                for j in range(4):
                    last = nc.tensor.transpose(aux[:, n, j * 120:(j + 1) * 120], pool_rows[:, (4 * n + j) * P:(4 * n + j + 1) * P],
                                               ident[0:120, 0:120])
                last.then_inc(pre_tr, 1)
            for n in range(2):
                pe.wait_ge(pre_ev, 11 + n)
                for j in range(12):
                    last = nc.tensor.transpose(aux[:, 2 + n, j * 24:(j + 1) * 24], conv_rows[:, (12 * n + j) * P:(12 * n + j + 1) * P],
                                               ident[0:24, 0:24])
                last.then_inc(pre_tr, 1)
            pe.wait_ge(pre_ev, 17)
            for t in range(16):
                last = nc.tensor.matmul(aux[:, 0, t * 17:(t + 1) * 17],
                                        spread[:, t, :],
                                        hs_rhs[:], start=True, stop=True)
            last.then_inc(smp_mm, 1)
            pe.wait_ge(smp_v, 2)
            for j in range(8):
                last = nc.tensor.transpose(aux[0:NS, 1 + j // 4, j % 4 * P:(j % 4 + 1) * P], acts_s[:, 16 + j, :], ident[:])
            last.then_inc(smp_mm, 1)
            pe.wait_ge(smp_v, 4)
            for k in range(8):
                if k >= 1:
                    pe.wait_ge(bc_used, 2 * k)
                for j in range(2):
                    last = nc.tensor.matmul(aux[:, j, :], ident[0:NS, k:k + 1].to_broadcast([NS, P]),
                                            bc_s[:, j * 512:(j + 1) * 512], start=True, stop=True)
                last.then_inc(bc_mm, 1)
                gemm(pe, T_GA + k, a_hi, a_lo)
            pe.wait_ge(bc_used, 16)
            for k in range(8):
                for j in range(2):
                    f = 2 * k + j
                    if f >= 2:
                        pe.wait_ge(yt_ev, f - 1)
                    for c in range(NCH):
                        last = nc.tensor.transpose(aux[:, f % 2, c * P:(c + 1) * P], xs_tok[:, c, f * P:(f + 1) * P], ident[:])
                    last.then_inc(yt_mm, 1)
                gemm(pe, T_GB + k, a_hi, a_lo)
            for gr in range(2):
                norm_pe(8, 4, 4 * gr, 1 + gr)
                if gr == 0:
                    pe.wait_ge(pool_lo, KT)
            pe.wait_ge(u_ready, 8 + 8)
            for n in range(8):
                m, gi = n // 4, n % 4
                t = T_POOL + m
                if gi == 0:
                    pe.wait_ge(lo_ready, t + 1)
                if n >= 2:
                    pe.wait_ge(pool_ev, n - 1)
                for kk in range(2):
                    k = 2 * gi + kk
                    for q, (w, u) in enumerate(((w_hi, b_hi), (w_hi, b_lo), (w_lo, b_hi))):
                        for h in range(2):
                            last = nc.tensor.matmul(aux[:, 2 * (n % 2) + h, 0:HALF], w[:, m, k, :], u[:, k, h * HALF:(h + 1) * HALF],
                                                    start=(kk == 0 and q == 0), stop=(kk == 1 and q == 2))
                last.then_inc(pool_mm, 1)
                if gi == 3:
                    pe.wait_ge(pool_mm, n + 1)
                    pe.sem_inc(gemm_done, 1)
            pe.wait_ge(pool_ev, 8)
            for gr in range(2, 4):
                norm_pe(8, 4, 4 * gr, 1 + gr)
            for c4 in range(4):
                for half in range(2):
                    if half:
                        pe.wait_ge(u_ready, 8 + 16)
                    for m in range(2):
                        gemm(pe, T_SSD + 4 * c4 + 2 * half + m, *((a_hi, a_lo) if half == 0 else (b_hi, b_lo)),
                             start=(half == 0), stop=(half == 1))
            for k in range(8):
                gemm(pe, T_O + k, c_hi, c_lo, ktwait=(lambda kk: pe.wait_ge(mgl_ready, kk + 1)) if k == 0 else None)
                if k >= 1:
                    norm_tile(24, k - 1, k == 1, False)
            norm_tile(24, 7, False, True)
            pe.wait_ge(mem_in, 16)
            for n in range(4):
                if n >= 2:
                    pe.wait_ge(mem_lo_s, n - 1)
                for kk in range(2):
                    for m in range(2):
                        last = nc.tensor.transpose(aux[:, n % 2, kk * MEM + m * P:kk * MEM + (m + 1) * P],
                                                   mem_tok[:, m, (2 * n + kk) * P:(2 * n + kk + 1) * P], ident[:])
                last.then_inc(mem_tr, 1)
            pe.wait_ge(mem_lo_s, 4)
            for k in range(16):
                t = T_K + k
                pe.wait_ge(lo_ready, t + 1)
                pe.wait_ge(evacuated[t % 2], uses(t) + 1)
                for m in range(2):
                    for kk in range(KT):
                        for q, (w, u) in enumerate(((w_hi, mem_hi), (w_hi, mem_lo), (w_lo, mem_hi))):
                            last = nc.tensor.matmul(slot[t % 2][:, 0, m * P:(m + 1) * P], u[:, kk, m * P:(m + 1) * P],
                                                    w[:, t % 2, kk, :], start=(kk == 0 and q == 0 and m == 0),
                                                    stop=(kk == KT - 1 and q == 2 and m == 1), skip_group_check=True)
                last.then_inc(gemm_done, 1)
            pe.wait_ge(evacuated[0], uses(T_V) + 1)
            pe.wait_ge(evacuated[1], uses(T_V) + 1)
            for n in range(4):
                for kk in range(2):
                    for m in range(2):
                        last = nc.tensor.transpose(aux[:, n, kk * MEM + m * P:kk * MEM + (m + 1) * P],
                                                   k_tok[:, m, (2 * n + kk) * P:(2 * n + kk + 1) * P], ident[:])
                last.then_inc(kt_mm, 1)
            for k in range(8):
                gemm(pe, T_Q + k, a_hi, a_lo, ktwait=(lambda kk: pe.wait_ge(u_ready, 24 + kk + 1)) if k == 0 else None)
            pe.wait_ge(evacuated[0], uses(T_XO) + 1)
            pe.wait_ge(evacuated[1], uses(T_XO) + 1)
            pe.wait_ge(kt_ev, 4)
            for k in range(KT):
                last = nc.tensor.transpose(aux[0:NS, k // 4, k % 4 * P:(k % 4 + 1) * P], qT[:, k, SEQ:TT], ident[:])
            last.then_inc(qt_mm, 1)
            pe.wait_ge(qt_ev, 1)
            for b in range(NS):
                if b >= 2:
                    pe.wait_ge(cache_used, b - 1)
                for j in range(2):
                    last = nc.tensor.matmul(slot[b % 2][:, j, :], ident[0:NS, b:b + 1].to_broadcast([NS, P]),
                                            q_tok[:, j * 512:(j + 1) * 512], start=True, stop=True)
                last.then_inc(qb_mm, 1)
            pe.wait_ge(cache_used, NS)
            for m in range(2):
                last = nc.tensor.transpose(aux[0:32, 0, m * P:(m + 1) * P], s_cols[:, m * 32:(m + 1) * 32], ident[:])
            last.then_inc(sm_a, 1)
            pe.wait_ge(sm_d, 1)
            for m in range(2):
                last = nc.tensor.transpose(aux[:, 1, m * 32:(m + 1) * 32], prob_s[:, m * P:(m + 1) * P], ident[0:32, 0:32])
            last.then_inc(sm_e, 1)
            pe.wait_ge(sm_f, 1)

            def scores(n):
                h, tq = n // 4, n % 4
                if n >= 2:
                    pe.wait_ge(prob_exp, n - 1)
                for kk in range(2):
                    last = nc.tensor.matmul(aux[:, n % 2, 0:MEM], qT[:, 2 * h + kk, tq * P:(tq + 1) * P], kT[:, 2 * h + kk, :],
                                            start=(kk == 0), stop=(kk == 1))
                last.then_inc(score_mm, 1)

            def turn(n):
                pe.wait_ge(prob_n, n + 1)
                if n >= 2:
                    pe.wait_ge(pt_ev, n - 1)
                for m in range(2):
                    last = nc.tensor.transpose(aux[:, 2 + n % 2, m * P:(m + 1) * P], prob[n % 2][:, m * P:(m + 1) * P], ident[:])
                last.then_inc(pt_mm, 1)

            def values(h):
                pe.wait_ge(pt_ev, 4 * h + 4)
                for dt in range(2):
                    if h >= 1:
                        pe.wait_ge(pv_lo, 2 * h + dt - 1)
                    for m in range(2):
                        last = nc.tensor.matmul(slot[dt][:, 0, :], v_tok[:, m, h * XD + dt * P:h * XD + (dt + 1) * P],
                                                probT[h % 2][:, m, :], start=(m == 0), stop=(m == 1))
                    last.then_inc(pv_mm, 1)

            scores(0)
            for n in range(16):
                if n + 1 < 16:
                    scores(n + 1)
                turn(n)
                if n % 4 == 3:
                    values(n // 4)
            for b in range(NS):
                n = NS + b
                pe.wait_ge(cache_in[n % 4], 16 * (n // 4 + 1))
                for h in range(XH):
                    for dt in range(2):
                        for m in range(2):
                            last = nc.tensor.matmul(aux[:, 0, (2 * h + dt) * NS + b:(2 * h + dt) * NS + b + 1],
                                                    cache[n % 4][:, m, h * XD + dt * P:h * XD + (dt + 1) * P],
                                                    pT_s[:, m * 32 + b * XH + h:m * 32 + b * XH + h + 1], start=(m == 0), stop=(m == 1))
                last.then_inc(cache_used, 1)
            pe.wait_ge(pv_lo, 8)
            pe.wait_ge(o_s_lo, 1)
            for k in range(8):
                gemm(pe, T_XO + k, c_hi, c_lo)
                if k >= 1:
                    norm_tile(32, k - 1, k == 1, False)
            norm_tile(32, 7, False, True)
            with pe.Fori(0, FF_CHUNKS - 1) as i:
                for k in range(8):
                    gemm(pe, T_MLP + k, a_hi, a_lo, i, 16, ktwait=(lambda kk: pe.wait_ge(u_ready, 32 + kk + 1)) if k == 0 else None)
                for k in range(8):
                    gemm(pe, T_MLP + 8 + k, c_hi, c_lo, i, 16,
                         ktwait=(lambda kk: pe.wait_ge(ff_lo, kk + 1 + i * 8)) if k == 0 else None)
            T_LAST = T_MLP + 16 * (FF_CHUNKS - 1)
            n0 = 8 * (FF_CHUNKS - 1)
            for k in range(8):
                gemm(pe, T_LAST + k, a_hi, a_lo)
            for k in range(8):
                gemm(pe, T_LAST + 8 + k, c_hi, c_lo, ktwait=(lambda kk: pe.wait_ge(ff_lo, n0 + kk + 1)) if k == 0 else None)
                if k >= 1:
                    norm_tile(40, k - 1, k == 1, False)
            norm_tile(40, 7, False, True)
            pe.wait_ge(fin_n, KT)
            for n in range(2):
                for j in range(4):
                    k = 4 * n + j
                    last = nc.tensor.transpose(aux[0:NS, n, j * P:(j + 1) * P], x[:, k, SEQ:TT], ident[:])
                last.then_inc(fin_mm, 1)
            for n in range(8):
                if n < 2 or n >= 4:
                    pe.wait_ge(fin_ev, n + 1 if n < 2 else n - 1)
                for j in range(4):
                    k = n % 2 * 4 + j
                    last = nc.tensor.transpose(aux[:, n % 4, j * P:(j + 1) * P], x[:, k, n // 2 * P:(n // 2 + 1) * P], ident[:])
                last.then_inc(fin_mm, 1)


_INS = ["x_prompt", "x_sample", "mem_prompt", "state_ssm", "state_conv", "state_pool", "cache_mem_k", "cache_mem_v",
        "norm_mix", "w_in", "conv_w", "conv_b", "dt_bias", "a_log", "d_skip", "ssd_norm", "w_ssd_proj", "pool_w",
        "pool_scale", "w_o", "norm_x", "w_xq", "w_xk", "w_xv", "w_xo", "norm_mlp", "w_up", "w_down", "norm_final"]
_OUTS = [("y_prompt", (1, SEQ, D)), ("y_sample", (NS, 1, D)),
         ("ssm_prompt", (1, 1, HEADS, HD, N_STATE)), ("conv_prompt", (1, 1, 3, CONV_DIM)), ("pool_prompt", (1, 1, PBUF, D)),
         ("memk_prompt", (1, 1, MEM, XH, XD)), ("memv_prompt", (1, 1, MEM, XH, XD)),
         ("ssm_sample", (1, NS, HEADS, HD, N_STATE)), ("conv_sample", (1, NS, 3, CONV_DIM)), ("pool_sample", (1, NS, PBUF, D))]


def kernel(**inputs):
    import numpy as _np
    import concourse.bacc as _bacc
    from concourse.bass_utils import run_bass_kernel_spmd as _run

    nc = _bacc.Bacc("TRN2", target_bir_lowering=False, num_devices=1)
    arrays, ins, outs = {}, {}, {}
    for name in _INS:
        v = _np.ascontiguousarray(inputs[name])
        arrays[f"in_{name}"] = v
        ins[name] = nc.dram_tensor(f"in_{name}", v.shape, F32, kind="ExternalInput").ap()
    for name, shape in _OUTS:
        outs[name] = nc.dram_tensor(f"out_{name}", shape, F32, kind="ExternalOutput").ap()
    build(nc, ins, outs)
    r = _run(nc, [arrays], core_ids=[0])
    return tuple(r.results[0][f"out_{name}"] for name, _ in _OUTS)
```

```python
from contextlib import ExitStack

import concourse.bass as bass
from concourse import mybir

P = 128
D = 1024
KT = D // P
SEQ = 512
NS = 8
TT = SEQ + NS
HALF = TT // 2
NCH = SEQ // P
HEADS, HD, N_STATE, GROUPS = 32, 64, 128, 4
HPG = HEADS // GROUPS
GW = HPG * HD
D_INNER = HEADS * HD
CONV_DIM = D_INNER + 2 * GROUPS * N_STATE
CT = CONV_DIM // P
XT_TILES = D_INNER // P
TAPS = 4
EDGE = TAPS - 1 + NS
OFF_XBC, OFF_DT = D_INNER, D_INNER + CONV_DIM
OFF_POOL = OFF_DT + HEADS
OFF_GA, OFF_GB = OFF_POOL + D, OFF_POOL + 2 * D
IN_DIM = OFF_GB + D
PBUF = 15
PEDGE = PBUF + NS
WINDOWS = (2, 4, 8, 16)
MEM = 256
XH, XD = 4, 256
D_FF = 4 * D
EPS = 1e-6
CR = 4
SR = 4
UW = 256
NEG = -1.0e30

F32 = mybir.dt.float32
R32 = mybir.dt.float32r
BF16 = mybir.dt.bfloat16
ALU = mybir.AluOpType
ACT = mybir.ActivationFunctionType
AX = mybir.AxisListType

T_XBC = 0
T_Z = T_XBC + CT
T_PU = T_Z + 16
T_GA = T_PU + 8
T_GB = T_GA + 8
T_POOL = T_GB + 8
T_SSD = T_POOL + 2
T_O = T_SSD + 16
T_K = T_O + 8
T_Q = T_K + 8
T_V = T_Q + 8
T_XO = T_V + 8
T_MLP = T_XO + 8
FF_CHUNKS = D_FF // D
T_END = T_MLP + 16 * FF_CHUNKS


class Chain:

    def __init__(self, eng, sem):
        self.eng, self.sem, self.n, self.extra = eng, sem, 0, 0

    def __call__(self, ins):
        self.n += 1
        ins.then_inc(self.sem, 1)
        self.eng.wait_ge(self.sem, self.n + self.extra)

    def loop(self, i, per):
        self.start, self.per, self.extra = self.n, per, i * per

    def end(self, times):
        assert self.n - self.start == self.per, (self.n - self.start, self.per)
        self.n, self.extra = self.start + self.per * times, 0


def build(nc, a, o):
    win = a["w_in"][0].rearrange("(k p) m -> p k m", p=P)
    x_dram = nc.dram_tensor("residual_spill", (P, KT * TT), F32, kind="Internal").ap()

    with ExitStack() as ctx:
        base = (nc.sbuf_base + 63) // 32 * 32
        R_RING = base
        R_A = R_RING + 32768
        R_1 = R_A + 2 * KT * TT * 4
        R_2 = R_1 + 2 * KT * TT * 4
        R_3 = R_2 + 2 * KT * TT * 4
        R_4 = R_3 + KT * TT * 4
        R_4N = R_4 + 2 * KT * TT * 4
        R_4S = R_4N + 12480
        R_5 = R_4N + 18720

        def at(name, shape, off, dt=F32):
            return nc.alloc_sbuf_tensor_at(name, shape, dt, offset=off)

        cur = [R_5 // 32 * 32]

        def const(name, shape, dt=F32):
            n = 1
            for d in shape[1:]:
                n *= d
            n *= 2 if dt == BF16 else 4
            t = at(name, shape, cur[0], dt)
            cur[0] += (n + 31) // 32 * 32
            return t

        w_raw = at("w_raw", [P, 2, KT, UW], R_RING)
        w_hi = at("w_hi", [P, 2, KT, P], R_RING + 16384, R32)
        w_lo = at("w_lo", [P, 2, KT, P], R_RING + 24576, R32)
        SZ = KT * TT * 4
        a_hi, a_lo = (at(n, [P, KT, TT], R_A + k * SZ, R32) for k, n in enumerate(("a_hi", "a_lo")))
        x0 = at("x0", [P, KT, TT], R_1)
        zs = at("zs", [P, 16, TT], R_1)
        c_hi, c_lo = (at(n, [P, KT, TT], R_1 + k * SZ, R32) for k, n in enumerate(("c_hi", "c_lo")))
        x_tok = at("x_tok", [P, NCH, D], R_2)
        xs_tok = at("xs_tok", [P, NCH, D_INNER], R_2)
        b_hi, b_lo = (at(n, [P, KT, TT], R_2 + k * SZ, R32) for k, n in enumerate(("b_hi", "b_lo")))
        qT = at("qT", [P, KT, TT], R_2)
        v_tok = at("v_tok", [P, 2, D], R_2 + SZ)
        kT = at("kT", [P, KT, MEM], R_2 + SZ + 8192)
        pu = at("pu", [P, KT, TT], R_3)
        x = at("x", [P, KT, TT], R_3)
        bc = at("bc", [P, 8, TT], R_4)
        gate_a = at("gate_a", [P, KT, TT], R_4)
        conv_rows = at("conv_rows", [NS * 3, CONV_DIM], R_1)
        pool_rows = at("pool_rows", [NS * PBUF, D], R_1 + 12288)
        spread = at("spread", [HEADS, 16, P], R_1 + 16384)
        mem_hi = at("mem_hi", [P, KT, MEM], R_4, R32)
        mem_lo = at("mem_lo", [P, KT, MEM], R_4 + 8192, R32)
        y_tok = at("y_tok", [P, NCH, D], R_4)
        g = R_4 + SZ
        cbuf = [at(f"cbuf{k}", [P, TAPS - 1 + TT], g + 2112 * k) for k in range(2)]
        hbuf = [at(f"hbuf{k}", [P, SEQ], g + 4224 + 2048 * k) for k in range(2)]
        tbuf = at("tbuf", [P, SEQ], g + 8320)
        abuf = [at(f"abuf{k}", [P, SEQ], g + 10368 + 2048 * k) for k in range(2)]
        decay = at("decay", [P, HPG, P], g)
        xdt = at("xdt", [P, GW], g + 4096)
        xdd = at("xdd", [P, GW], g + 6144)
        xskip = at("xskip", [P, GW], g + 8192)
        yacc = at("yacc", [P, GW], g + 10240)
        b_tok = at("b_tok", [P, N_STATE], g + 12288)
        cbm = at("cbm", [P, P], g + 12800)
        gate_b = at("gate_b", [P, KT, TT], g)
        state_out = at("state_out", [P, 16, N_STATE], g)
        pool_edge = at("pool_edge", [PEDGE, D], g + 8192)
        bc_s = at("bc_s", [NS, 8 * N_STATE], g + 12544)
        mem_tok = at("mem_tok", [P, 2, D], g)
        k_tok = at("k_tok", [P, 2, D], g + 8192)
        ys_tok = at("ys_tok", [NS, D], g)
        vT = at("vT", [P, KT, MEM], g)
        cache = [at(f"cache{k}", [P, 2, D], R_1 + 8192 * k) for k in range(CR)]
        sq = [at(f"sq{k}", [P, TT], R_4N + 2080 * k) for k in range(2)]
        ut = [at(f"ut{k}", [P, TT], R_4N + 4160 + 2080 * k) for k in range(2)]
        std = at("std", [P, TT], R_4N + 8320)
        rstd = at("rstd", [P, TT], R_4N + 10400)
        state = at("state", [P, GROUPS, GW], R_4N)
        tz = [at(f"tz{k}", [P, TT], R_4N + 8192 + 2080 * k) for k in range(2)]
        conv_edge = at("conv_edge", [EDGE, CONV_DIM], R_3 + 3072)
        sring = [at(f"sring{k}", [P, 8, N_STATE], R_4N + 4096 * k) for k in range(SR)]
        sp_cols = at("sp_cols", [P, KT, NS * PBUF], R_4N + 12480)
        ysq = [at(f"ysq{k}", [P, SEQ], R_2 + 2048 * k) for k in range(2)]
        ystd = at("ystd", [P, SEQ], R_2 + 4096)
        yrstd = at("yrstd", [P, SEQ], R_2 + 6144)
        win_sum = [at(f"win_sum{k}", [P, SEQ], R_2 + 8192 + 2048 * k) for k in range(2)]
        win_sum_a = [at(f"win_sum_a{k}", [P, SEQ], g + 2048 * k) for k in range(2)]
        st_cols = at("st_cols", [P, CT, NS * 3], R_4N + 16384)
        junk_s = at("junk_s", [P, 8, N_STATE], R_4N + 16384, BF16)
        prob = [at(f"prob{k}", [P, MEM], R_4N + 1024 * k) for k in range(2)]
        probT = [at(f"probT{k}", [P, 2, SEQ], R_4N + 2048 + 4096 * k) for k in range(2)]
        q_tok = at("q_tok", [NS, D], R_4N + 10240)
        junk = at("junk", [P, 2, XH, XD], R_4N + 2048, BF16)
        prob_s = at("prob_s", [32, MEM], R_4N + 15360)
        s_cols = at("s_cols", [P, 64], R_4N + 16384)
        pT_s = at("pT_s", [P, 64], R_4N + 16640)
        stats = at("stats", [P, 80], R_4N + 16896)
        rt = [at(f"rt{k}", [P, TT], R_4N + 2080 * k) for k in range(2)]
        dtw = at("dtw", [P, KT, HEADS], R_3)
        dtw_hi = at("dtw_hi", [P, KT, HEADS], R_3 + 1024, R32)
        dtw_lo = at("dtw_lo", [P, KT, HEADS], R_3 + 2048, R32)
        dtT = at("dtT", [HEADS, 2, TT], R_3 + 3072)
        dt_tmp = [at(f"dt_tmp{k}", [HEADS, TT], R_3 + 7232 + 2080 * k) for k in range(4)]
        xs_row = at("xs_row", [NS, D], R_4)
        vr1 = at("vr1", [56, P], R_4 + 4096)
        vr2 = at("vr2", [120, P], R_4 + 4608)

        ident = const("ident", [P, P])
        identb = const("identb", [P, P], BF16)
        triu = const("triu", [P, P])
        ones = const("ones", [P, P])
        maskneg = const("maskneg", [P, P], BF16)
        cols = const("cols", [P, 176])
        CN_MIX, CN_X, CN_MLP, CN_FIN, C_PS, C_SSD, C_CW, C_CB = 0, 8, 16, 24, 32, 40, 56, 152
        dtk = const("dtk", [P, 2, NCH, HEADS])
        ncs = const("ncs", [P, NCH, HEADS])
        ecs = const("ecs", [P, NCH, HEADS])
        cdec = const("cdec", [P, NCH, HEADS])
        dtd = const("dtd", [P, NCH, HEADS])
        dskip = const("dskip", [P, HEADS])
        rcount = const("rcount", [P, 16])
        xedge = const("xedge", [P, CT, EDGE])
        hcol = const("hcol", [HEADS, 4])
        hs_rhs = const("hs_rhs", [HEADS, 17])
        acts_s = const("acts_s", [P, CT, NS])
        exp_s = const("exp_s", [P, 16, 17])
        xdt_s = const("xdt_s", [P, 16, NS])
        y_s = const("y_s", [P, 16, NS])
        eps_col = const("eps_col", [P, 1])
        tmp_s = const("tmp_s", [P, CT, NS])
        y_sq = xdt_s
        y_std = const("y_std", [P, GROUPS, NS])
        assert cur[0] <= nc.sbuf_usable_end, (cur[0], nc.sbuf_usable_end)

        slot = [ctx.enter_context(nc.psum_tensor(f"slot{k}", [P, 2, 512], F32)) for k in range(2)]
        aux = ctx.enter_context(nc.psum_tensor("aux", [P, 4, 512], F32))

        names = {}

        def sem(name):
            names[name] = ctx.enter_context(nc.semaphore(name))
            return names[name]

        raw_landed = [sem(f"raw_landed{k}") for k in range(2)]
        hi_ready, lo_ready, gemm_done = sem("hi_ready"), sem("lo_ready"), sem("gemm_done")
        evacuated = [sem(f"evacuated{k}") for k in range(2)]
        v_step, a_step, p_step = sem("v_step"), sem("a_step"), sem("p_step")
        consts, x_in, s_in, vec_in, small_in = (sem(n) for n in ("consts", "x_in", "s_in", "vec_in", "small_in"))
        xtr_done, xtr_evac = sem("xtr_done"), sem("xtr_evac")
        sq_ready, sq_used, std_ready = (sem(n) for n in ("sq_ready", "sq_used", "std_ready"))
        ut_ready, uh_ready, u_ready = sem("ut_ready"), sem("uh_ready"), sem("u_ready")
        spilled, reloaded = sem("spilled"), sem("reloaded")
        dtw_hi_s, dtw_lo_s, dt_mm, dt_evac = (sem(n) for n in ("dtw_hi_s", "dtw_lo_s", "dt_mm", "dt_evac"))
        dt_a, dt_b, dt_tr, dt_trv, cs_mm, cs_v = (sem(n) for n in ("dt_a", "dt_b", "dt_tr", "dt_trv", "cs_mm", "cs_v"))
        conv_done, tanh_done, act_ready = sem("conv_done"), sem("tanh_done"), sem("act_ready")
        xtr2_done, xtr2_evac = sem("xs_turned"), sem("xs_stored")
        bc_ready = sem("bc_ready")
        cb_ready, exp_a, exp_b, x_prep, m_ready = (sem(n) for n in ("cb_ready", "exp_a", "exp_b", "x_prep", "m_ready"))
        off_ready, y_mm, skip_ready, y_ready, tz_ready = (sem(n) for n in ("off_ready", "y_mm", "skip_ready", "y_ready", "tz_ready"))
        st_zero = sem("st_zero")
        old_in, old_tr, old_ev = sem("old_in"), sem("old_tr"), sem("old_ev")
        edge_tr, edge_ev, end_tr, end_ev = (sem(n) for n in ("edge_tr", "edge_ev", "end_tr", "end_ev"))
        out_ssm, out_edge, out_pool, out_sst, out_kv, out_y = (sem(n) for n in ("out_ssm", "out_edge", "out_pool", "out_sst", "out_kv", "out_y"))
        smp_a, smp_mm, smp_v = sem("smp_a"), sem("smp_mm"), sem("smp_v")
        st_in = [sem(f"st_in{k}") for k in range(SR)]
        st_out = [sem(f"st_out{k}") for k in range(SR)]
        st_dec, st_new, bc_mm, bc_used = sem("st_dec"), sem("st_new"), sem("bc_mm"), sem("bc_used")
        ys_ready, ys_sq, ys_mm, ys_sum, ys_std, ys_n, ys_hi, ys_lo = (
            sem(n) for n in ("ys_ready", "ys_sq", "ys_mm", "ys_sum", "ys_std", "ys_n", "ys_hi", "ys_lo"))
        pool_sum, pool_sum_s, pool_hi, pool_lo, pool_mm, pool_ev = (sem(n) for n in ("pool_sum", "pool_sum_s", "pool_hi", "pool_lo", "pool_mm", "pool_ev"))
        yt_mm, yt_ev = sem("yt_mm"), sem("yt_ev")
        mg_ready, mgh_ready, mgl_ready = sem("mg_ready"), sem("mgh_ready"), sem("mgl_ready")
        mem_in, mem_tr, mem_hi_s, mem_lo_s = (sem(n) for n in ("mem_in", "mem_tr", "mem_hi_s", "mem_lo_s"))
        kt_mm, kt_ev, vt_mm, vt_ev = sem("kt_mm"), sem("kt_ev"), sem("vt_mm"), sem("vt_ev")
        cache_in = [sem(f"cache_in{k}") for k in range(CR)]
        cache_used = sem("cache_used")
        qt_mm, qt_ev, qb_mm, sc_s = (sem(n) for n in ("qt_mm", "qt_ev", "qb_mm", "sc_s"))
        sm_a, sm_b, sm_c, sm_d, sm_e, sm_f = (sem(f"sm_{n}") for n in "abcdef")
        score_mm, negmax, prob_exp, prob_n, pt_mm, pt_ev, pv_mm, pv_hi, pv_lo = (
            sem(n) for n in ("score_mm", "negmax", "prob_exp", "prob_n", "pt_mm", "pt_ev", "pv_mm", "pv_hi", "pv_lo"))
        o_s_hi, o_s_lo = sem("o_s_hi"), sem("o_s_lo")
        relu_done, ff_sq, ff_hi, ff_lo = (sem(n) for n in ("relu_done", "ff_sq", "ff_hi", "ff_lo"))
        fin_n, fin_mm, fin_ev = sem("fin_n"), sem("fin_mm"), sem("fin_ev")

        block = ctx.enter_context(nc.Block())

        def halves(t):
            return t.rearrange("p (h n) -> p h n", h=2)

        def in_slot(k):
            return slot[k][:, :, 0:HALF]

        def q_bank(b):
            return aux[:, 2:4, :] if b % 2 == 0 else aux[:, 0:2, :]

        def uses(t):
            if t <= T_POOL:
                return t // 2
            if t < T_O:
                return T_POOL // 2 + (t - T_SSD) // 4
            return T_POOL // 2 + 4 + (t - T_O) // 2

        def load_unit(sp, u, src, i=0, step=0):
            if u >= 2:
                sp.wait_ge(lo_ready, 2 * u - 2 + i * step)
            sp.dma_start(w_raw[:, u % 2], src).then_inc(raw_landed[u % 2], 16)

        def split_hi(act, t, i=0, step=0):
            if t >= T_END:
                return
            if t % 2 == 0:
                act.wait_ge(raw_landed[t // 2 % 2], 16 * (t // 4 + 1) + i * (4 * step))
            if t >= 2:
                act.wait_ge(gemm_done, t - 1 + i * step)
            nc.scalar.activation(w_hi[:, t % 2], w_raw[:, t // 2 % 2, :, t % 2 * P:t % 2 * P + P],
                                 ACT.Copy).then_inc(hi_ready, 1)

        def split_lo(dve, t, i=0, step=0):
            if t >= T_END:
                return
            dve.wait_ge(hi_ready, t + 1 + i * step)
            nc.vector.tensor_tensor(w_lo[:, t % 2], w_raw[:, t // 2 % 2, :, t % 2 * P:t % 2 * P + P],
                                    w_hi[:, t % 2].bitcast(F32), ALU.subtract).then_inc(lo_ready, 1)

        def gemm(pe, t, hi, lo, i=0, step=0, kts=range(KT), ktwait=None, start=True, stop=True):
            k0 = kts[0] == 0
            if k0:
                pe.wait_ge(lo_ready, t + 1 + i * step)
                if start:
                    pe.wait_ge(evacuated[t % 2], uses(t) + 1 + i * (step // 2))
            for k in kts:
                if ktwait is not None:
                    ktwait(k)
                for n, (w, act) in enumerate(((w_hi, hi), (w_hi, lo), (w_lo, hi))):
                    for h in range(2):
                        last = nc.tensor.matmul(slot[t % 2][:, h, 0:HALF], w[:, t % 2, k, :],
                                                act[:, k, h * HALF:(h + 1) * HALF],
                                                start=(start and k == 0 and n == 0),
                                                stop=(stop and k == KT - 1 and n == 2))
            if kts[-1] == KT - 1:
                last.then_inc(gemm_done, 1)

        def unit_src(name, cb, row=0):
            return a[name][0][row:row + D].rearrange("(k p) m -> p k m", p=P)[:, :, cb * UW:(cb + 1) * UW]

        @block.sync
        def _(sp):
            for u in range(4):
                load_unit(sp, u, win[:, :, OFF_XBC + u * UW:OFF_XBC + (u + 1) * UW])
            with sp.Fori(0, 2) as i:
                for u in range(4):
                    load_unit(sp, 4 + u, win[:, :, bass.ds(OFF_XBC + D + u * UW + i * D, UW)], i, 8)
            with sp.Fori(0, 2) as i:
                for u in range(4):
                    load_unit(sp, T_Z // 2 + u, win[:, :, bass.ds(u * UW + i * D, UW)], i, 8)
            for u in range(4):
                load_unit(sp, T_PU // 2 + u, win[:, :, OFF_POOL + u * UW:OFF_POOL + (u + 1) * UW])
            s_dram = a["state_ssm"][0].rearrange("b (j t h) p n -> b j (h p) t n", j=2, h=2)

            def load_state(n):
                if n >= SR:
                    sp.wait_ge(st_out[n % SR], 16 * (n // SR))
                    sp.wait_ge(bc_used, n - SR + 1)
                elif n < 2:
                    sp.wait_ge(end_tr, 4)
                elif n == 3:
                    sp.wait_ge(pool_sum_s, 1)
                sp.dma_start(sring[n % SR][:], s_dram[n // 2, n % 2]).then_inc(st_in[n % SR], 16)

            for u in range(8):
                load_unit(sp, T_GA // 2 + u, win[:, :, OFF_GA + u * UW:OFF_GA + (u + 1) * UW])
                if u == 1:
                    for n in (2, 0, 1, 3):
                        load_state(n)
                elif u >= 2:
                    load_state(2 * u)
                    load_state(2 * u + 1)
            load_unit(sp, T_POOL // 2, a["pool_w"][0].rearrange("g (k p) d -> p (g k) d", p=P))
            for u in range(8):
                load_unit(sp, T_SSD // 2 + u, unit_src("w_ssd_proj", u // 2, D * (1 - u % 2)))
            def load_cache(n):
                if n >= CR:
                    sp.wait_ge(cache_used, n - CR + 1)
                elif n == 0:
                    sp.wait_ge(gemm_done, T_O + 8)
                src = a["cache_mem_k" if n < NS else "cache_mem_v"][0, n % NS]
                sp.dma_start(cache[n % CR][:], src.rearrange("(m p) h d -> p m (h d)", p=P)).then_inc(cache_in[n % CR], 16)

            for n, name in enumerate(("w_o", "w_xk", "w_xq", "w_xv", "w_xo")):
                for u in range(4):
                    load_unit(sp, T_O // 2 + 4 * n + u, unit_src(name, u))
                    for c in {("w_xq", 0): (0, 1), ("w_xq", 1): (2, 3), ("w_xv", 2): (4, 5), ("w_xv", 3): (6, 7),
                              ("w_xo", 0): (8, 9, 10), ("w_xo", 1): (11, 12, 13, 14, 15)}.get((name, u), ()):
                        load_cache(c)
            up = a["w_up"][0].rearrange("(k p) m -> p k m", p=P)
            down = a["w_down"][0].rearrange("(j k p) m -> p j k m", p=P, k=KT)
            with sp.Fori(0, FF_CHUNKS) as i:
                for u in range(4):
                    load_unit(sp, T_MLP // 2 + u, up[:, :, bass.ds(i * D + u * UW, UW)], i, 16)
                for u in range(4):
                    load_unit(sp, T_MLP // 2 + 4 + u, down[:, i, :, u * UW:(u + 1) * UW], i, 16)

        @block.gpsimd
        def _(pool):
            chain = Chain(pool, p_step)
            nc.gpsimd.memset(ident[:], 0.0)
            nc.gpsimd.memset(identb[:], 0.0)
            nc.gpsimd.memset(ones[:], 1.0)
            nc.gpsimd.memset(triu[:], 1.0)
            nc.gpsimd.memset(maskneg[:], 0.0)
            for k in range(2):
                nc.gpsimd.memset(cbuf[k][:, 0:TAPS - 1], 0.0)
            for j in range(16):
                ins = nc.gpsimd.memset(rcount[:, j:j + 1], 1.0 / (j + 1))
            chain(ins)
            nc.gpsimd.affine_select(out=ident[:], in_=ident[:], compare_op=ALU.not_equal, fill=1.0, base=0,
                                    pattern=[[-1, P]], channel_multiplier=1).then_inc(consts, 1)
            nc.gpsimd.affine_select(out=identb[:], in_=identb[:], compare_op=ALU.not_equal, fill=1.0, base=0,
                                    pattern=[[-1, P]], channel_multiplier=1).then_inc(consts, 1)
            nc.gpsimd.affine_select(out=triu[:], in_=triu[:], compare_op=ALU.is_ge, fill=0.0, base=0,
                                    pattern=[[1, P]], channel_multiplier=-1).then_inc(consts, 1)
            nc.gpsimd.affine_select(out=maskneg[:], in_=maskneg[:], compare_op=ALU.is_ge, fill=NEG, base=0,
                                    pattern=[[1, P]], channel_multiplier=-1).then_inc(consts, 1)
            pool.dma_start(o["conv_sample"][0, :, 0:2, :], a["state_conv"][0, :, 1:3, :]).then_inc(out_edge, 16)
            pool.dma_start(o["pool_sample"][0, :, 0:PBUF - 1, :], a["state_pool"][0, :, 1:PBUF, :]).then_inc(out_pool, 16)
            pool.wait_ge(xtr_evac, 10)
            pool.dma_start(x_dram, x0[:].rearrange("p k n -> p (k n)")).then_inc(spilled, 16)
            pool.wait_ge(spilled, 16)
            pool.wait_ge(u_ready, KT)
            pool.dma_start(conv_rows[:], a["state_conv"][0].rearrange("b k c -> (b k) c")).then_inc(old_in, 16)
            pool.dma_start(pool_rows[:], a["state_pool"][0].rearrange("b k c -> (b k) c")).then_inc(old_in, 16)
            nc.gpsimd.memset(state[:], 0.0).then_inc(st_zero, 1)

            def skip_term(c, gr, s):
                pool.wait_ge(x_prep, s)
                nc.gpsimd.tensor_tensor(
                    xskip[:].rearrange("p (h d) -> p h d", h=HPG),
                    xs_tok[:, c, gr * GW:(gr + 1) * GW].rearrange("p (h d) -> p h d", h=HPG),
                    dskip[:, gr * HPG:(gr + 1) * HPG].unsqueeze(2).to_broadcast([P, HPG, HD]),
                    ALU.mult).then_inc(skip_ready, 1)

            pool.wait_ge(edge_ev, 6)
            pool.dma_start(o["conv_prompt"][0, 0], conv_edge[0:3, :]).then_inc(out_edge, 16)
            pool.dma_start(o["conv_sample"][0, :, 2, :], conv_edge[3:EDGE, :]).then_inc(out_edge, 16)
            with pool.Fori(0, NCH) as i:
                for gr in range(GROUPS):
                    skip_term(i, gr, 4 * i + gr + 1)

            pool.wait_ge(end_ev, 4)
            pool.dma_start(o["ssm_prompt"][0, 0].rearrange("(t h) p n -> (h p) t n", h=2), state_out[:]).then_inc(out_ssm, 16)

            def decay_state(n):
                b, j = n // 2, n % 2
                pool.wait_ge(st_in[n % SR], 16 * (n // SR + 1))
                nc.gpsimd.tensor_tensor(sring[n % SR][:], sring[n % SR][:],
                                        exp_s[:, 8 * j:8 * j + 8, NS + b:NS + b + 1].to_broadcast([P, 8, N_STATE]),
                                        ALU.mult).then_inc(st_dec, 1)

            decay_state(0)
            pool.wait_ge(end_ev, 7)
            pool.dma_start(o["pool_prompt"][0, 0], pool_edge[0:PBUF, :]).then_inc(out_pool, 16)
            pool.dma_start(o["pool_sample"][0, :, PBUF - 1, :], pool_edge[PBUF:PEDGE, :]).then_inc(out_pool, 16)
            def windows(k, buffers):
                w = WINDOWS[k // 2]
                if k >= 1:
                    pool.wait_ge(pool_sum, k)
                src, span = pu[:, k, 0:SEQ], 1
                bufs = list(buffers)
                while span < w:
                    dst = bufs[0]
                    nc.gpsimd.tensor_copy(dst[:, 0:span], src[:, 0:span])
                    chain(nc.gpsimd.tensor_tensor(dst[:, span:SEQ], src[:, span:SEQ], src[:, 0:SEQ - span], ALU.add))
                    src, span = dst[:, 0:SEQ], span * 2
                    bufs.reverse()
                dst = bufs[0]
                nc.gpsimd.tensor_scalar(dst[:, w:SEQ], src[:, w:SEQ], 1.0 / w, 1.0, ALU.mult, ALU.mult)
                chain(nc.gpsimd.tensor_tensor(dst[:, 0:w], src[:, 0:w], rcount[:, 0:w], ALU.mult))
                nc.gpsimd.tensor_tensor(pu[:, k, 0:SEQ], dst[:, 0:SEQ], pu[:, k, 0:SEQ], ALU.subtract).then_inc(pool_sum, 1)

            pool.wait_ge(out_ssm, 16)
            for n in range(1, 9):
                decay_state(n)
                if 3 <= n <= 6:
                    windows(n - 3, win_sum_a)
            pool.wait_ge(yt_ev, 16)
            for k in range(4, KT):
                for n in range(2 * k + 1, min(2 * k + 3, 2 * NS)):
                    decay_state(n)
                windows(k, win_sum)

            pool.wait_ge(pool_ev, 8)
            pool.wait_ge(spilled, 16)
            pool.dma_start(x[:].rearrange("p k n -> p (k n)"), x_dram).then_inc(reloaded, 16)
            pool.wait_ge(mgl_ready, KT)
            pool.dma_start(mem_tok[:], a["mem_prompt"][0].rearrange("(m p) d -> p m d", p=P)).then_inc(mem_in, 16)
            pool.wait_ge(kt_ev, 4)
            pool.dma_start(o["memk_prompt"][0, 0].rearrange("(m p) h d -> p m (h d)", p=P), k_tok[:]).then_inc(out_kv, 16)
            pool.wait_ge(vt_ev, 4)
            pool.dma_start(o["memv_prompt"][0, 0].rearrange("(m p) h d -> p m (h d)", p=P), v_tok[:]).then_inc(out_kv, 16)
            pool.wait_ge(fin_ev, 2)
            pool.dma_start(o["y_sample"].rearrange("b s d -> (b s) d"), ys_tok[:]).then_inc(out_y, 16)
            for c in range(NCH):
                pool.wait_ge(fin_ev, 4 + 2 * c)
                pool.dma_start(o["y_prompt"][0, c * P:(c + 1) * P, :], y_tok[:, c, :]).then_inc(out_y, 16)
            pool.wait_ge(out_y, 16 * (NCH + 1))
            pool.wait_ge(out_kv, 32)
            pool.wait_ge(out_ssm, 16)
            pool.wait_ge(out_pool, 48)
            pool.wait_ge(out_edge, 48)
            for k in range(SR):
                pool.wait_ge(st_out[k], 16 * len(range(k, 2 * NS, SR)))

        @block.scalar
        def _(act):
            chain = Chain(act, a_step)
            act.dma_start(xs_row[:], a["x_sample"].rearrange("b s d -> (b s) d")).then_inc(s_in, 16)
            for n, name in enumerate(("norm_mix", "norm_x", "norm_mlp", "norm_final", "pool_scale")):
                src = a[name] if name == "norm_final" else a[name][0]
                act.dma_start(vr1[8 * n:8 * n + 8, :], src.rearrange("(k p) -> k p", p=P)).then_inc(vec_in, 16)
            act.dma_start(vr1[40:56, :], a["ssd_norm"][0].rearrange("(k p) -> k p", p=P)).then_inc(vec_in, 16)
            act.dma_start(vr2[0:96, :], a["conv_w"][0].rearrange("w (k p) -> (w k) p", p=P)).then_inc(vec_in, 16)
            act.dma_start(vr2[96:120, :], a["conv_b"][0].rearrange("(k p) -> k p", p=P)).then_inc(vec_in, 16)
            act.dma_start(x_tok[:], a["x_prompt"][0].rearrange("(c p) d -> p c d", p=P)).then_inc(x_in, 16)
            act.dma_start(dtw[:], win[:, :, OFF_DT:OFF_DT + HEADS]).then_inc(small_in, 16)
            act.dma_start(hcol[:, 0:1], a["dt_bias"].rearrange("o h -> h o")).then_inc(small_in, 16)
            act.dma_start(hcol[:, 1:2], a["a_log"].rearrange("o h -> h o")).then_inc(small_in, 16)
            act.dma_start(hs_rhs[:, 16:17], a["d_skip"].rearrange("o h -> h o")).then_inc(small_in, 16)
            act.dma_start(dskip[:], a["d_skip"].to_broadcast([P, HEADS])).then_inc(small_in, 16)

            def norm_sum(q, src, ready, n=KT, first=0):
                for k in range(first, first + n):
                    ready(k)
                    if q + k >= 2:
                        act.wait_ge(sq_used, q + k - 1)
                    nc.scalar.activation(sq[k % 2][:], src(k), ACT.Square).then_inc(sq_ready, 1)

            def norm_std(used, scale):
                act.wait_ge(sq_used, used)
                nc.scalar.activation(halves(std[:]), aux[:, 2:4, 0:HALF], ACT.Sqrt, bias=eps_col[:, 0:1],
                                     scale=scale).then_inc(std_ready, 1)

            def norm_hi(q, dst, n=KT):
                for k in range(n):
                    act.wait_ge(ut_ready, q + k + 1)
                    nc.scalar.activation(dst[:, k, :], ut[k % 2][:], ACT.Copy).then_inc(uh_ready, 1)

            norm_sum(0, lambda k: x0[:, k, :], lambda k: act.wait_ge(xtr_evac, 3 + k))
            split_hi(act, 0)
            split_hi(act, 1)
            act.wait_ge(small_in, 80)
            nc.scalar.activation(dtw_hi[:], dtw[:], ACT.Copy).then_inc(dtw_hi_s, 1)
            norm_std(8, 1.0 / D)
            norm_hi(0, a_hi)
            act.wait_ge(dt_evac, 1)
            chain(nc.scalar.activation(dt_tmp[1][:], dt_tmp[0][:], ACT.Abs))
            nc.scalar.activation(dt_tmp[1][:], dt_tmp[1][:], ACT.Exp, scale=-1.0).then_inc(dt_a, 1)
            nc.scalar.activation(hcol[:, 2:3], hcol[:, 1:2], ACT.Exp).then_inc(dt_a, 1)
            act.wait_ge(dt_b, 1)
            nc.scalar.activation(dt_tmp[2][:], dt_tmp[2][:], ACT.Ln).then_inc(dt_a, 1)
            act.wait_ge(cs_mm, 1)
            act.wait_ge(cs_v, 1)
            nc.scalar.activation(ecs[:].rearrange("p c h -> p (c h)"), aux[:, 0, 0:P], ACT.Exp).then_inc(dt_a, 1)
            nc.scalar.activation(cdec[:].rearrange("p c h -> p (c h)"), aux[:, 0, P:2 * P], ACT.Exp).then_inc(dt_a, 1)
            nc.scalar.activation(dtd[:].rearrange("p c h -> p (c h)"), dtd[:].rearrange("p c h -> p (c h)"),
                                 ACT.Exp).then_inc(dt_a, 1)
            nc.scalar.activation(hs_rhs[:, NS:2 * NS], dtT[:, 1, SEQ:TT], ACT.Exp).then_inc(dt_a, 1)

            def conv_front(t, i=0):
                act.wait_ge(gemm_done, t + 1 + i * 8)
                nc.scalar.activation(halves(cbuf[t % 2][:, TAPS - 1:TAPS - 1 + TT]), in_slot(t % 2),
                                     ACT.Copy).then_inc(evacuated[t % 2], 1)
                split_hi(act, t + 2, i, 8)
                act.wait_ge(conv_done, t + 1 + i * 8)
                nc.scalar.activation(tbuf[:], hbuf[t % 2][:], ACT.Tanh).then_inc(tanh_done, 1)

            conv_front(0)
            with act.Fori(0, 2) as i:
                for t in range(8):
                    conv_front(t + 1, i)
                    act.wait_ge(xtr2_done, t + 1 + i * 8)
                    nc.scalar.activation(xs_tok[:, :, bass.ds(i * D + t * P, P)],
                                         aux[:, t % 2, :].rearrange("p (c f) -> p c f", c=NCH),
                                         ACT.Copy).then_inc(xtr2_evac, 1)
            for t in range(17, 24):
                conv_front(t)
                for n in {17: (0,), 18: (1,), 19: (2,), 20: (3,), 22: (4,), 23: (5,)}.get(t, ()):
                    act.wait_ge(edge_tr, n + 1)
                    nc.scalar.activation(conv_edge[:, n * 512:(n + 1) * 512], aux[0:EDGE, 1 + 2 * (n % 2), :],
                                         ACT.Copy).then_inc(edge_ev, 1)

            def decays(sem_in, s, c, gr, j0, sem_out):
                act.wait_ge(sem_in, s)
                for j in range(j0, j0 + 4):
                    last = nc.scalar.activation(decay[:, j, :], aux[:, 0, (j - j0) * P:(j - j0 + 1) * P], ACT.Exp,
                                                bias=ncs[:, c, gr * HPG + j:gr * HPG + j + 1])
                last.then_inc(sem_out, 1)

            def z_tile(t, i):
                act.wait_ge(gemm_done, t + 1 + i * 8)
                split_hi(act, t + 2, i, 8)
                nc.scalar.activation(halves(tz[t % 2][:]), in_slot(t % 2), ACT.Tanh, scale=0.5).then_inc(tz_ready, 1)

            def b_turned(s):
                act.wait_ge(cb_ready, s)
                nc.scalar.activation(b_tok[:], aux[:, 3, 0:P], ACT.Copy)

            with act.Fori(0, 2) as i:
                for gr in range(GROUPS):
                    s = 4 * i + gr + 1
                    b_turned(s)
                    decays(cb_ready, s, i, gr, 0, exp_a)
                    z_tile(T_Z + 2 * gr, i)
                    decays(off_ready, s, i, gr, 4, exp_b)
                    z_tile(T_Z + 2 * gr + 1, i)
            act.wait_ge(smp_v, 1)
            nc.scalar.activation(acts_s[:], tmp_s[:], ACT.Tanh).then_inc(smp_a, 1)
            act.wait_ge(out_edge, 48)
            with act.Fori(0, 2) as i:
                for gr in range(GROUPS):
                    s = 8 + 4 * i + gr + 1
                    t = T_PU + gr
                    b_turned(s)
                    decays(cb_ready, s, 2 + i, gr, 0, exp_a)
                    decays(off_ready, s, 2 + i, gr, 4, exp_b)
                    act.wait_ge(gemm_done, t + 1 + i * 4)
                    split_hi(act, t + 2, i, 4)
                    nc.scalar.activation(halves(pu[:, 4 * i + gr, :]), in_slot(t % 2),
                                         ACT.Copy).then_inc(evacuated[t % 2], 1)

            so_dram = o["ssm_sample"][0].rearrange("b (j t h) p n -> b j (h p) t n", j=2, h=2)

            def store_state(n):
                act.wait_ge(st_new, n + 1)
                act.dma_start(so_dram[n // 2, n % 2], sring[n % SR][:]).then_inc(st_out[n % SR], 16)

            for k in range(8):
                t = T_GA + k
                act.wait_ge(gemm_done, t + 1)
                split_hi(act, t + 2)
                nc.scalar.activation(halves(gate_a[:, k, :]), in_slot(t % 2), ACT.Tanh, scale=0.5).then_inc(evacuated[t % 2], 1)
                store_state(k)
            act.wait_ge(pool_sum, 4)
            act.wait_ge(out_pool, 48)
            act.wait_ge(yt_ev, 16)
            for k in range(8):
                t = T_GB + k
                act.wait_ge(gemm_done, t + 1)
                split_hi(act, t + 2)
                nc.scalar.activation(halves(gate_b[:, k, :]), in_slot(t % 2), ACT.Tanh, scale=0.5).then_inc(evacuated[t % 2], 1)
                store_state(8 + k)
                for f in (2 * k, 2 * k + 1):
                    act.wait_ge(sq_used, 8 + f - 1)
                    nc.scalar.activation(ysq[f % 2][:], zs[:, f, 0:SEQ], ACT.Square).then_inc(sq_ready, 1)
                if k % 2:
                    act.wait_ge(sq_used, 8 + 2 * k + 2)
                    if k >= 3:
                        act.wait_ge(ut_ready, 8 + 2 * k - 5)
                    nc.scalar.activation(ystd[:], aux[:, 2 + k // 2 % 2, :], ACT.Sqrt, bias=eps_col[:, 0:1],
                                         scale=1.0 / (4 * GW)).then_inc(std_ready, 1)
            act.wait_ge(pool_sum_s, 1)
            for k in range(KT):
                act.wait_ge(pool_sum, k + 1)
                nc.scalar.activation(a_hi[:, k, :], pu[:, k, :], ACT.Copy).then_inc(pool_hi, 1)
            act.wait_ge(ys_ready, 1)
            nc.scalar.activation(y_sq[:], y_s[:], ACT.Square).then_inc(ys_sq, 1)
            act.wait_ge(ut_ready, 8 + 16)
            for k in range(8, 16):
                nc.scalar.activation(b_hi[:, k - 8, 0:SEQ], zs[:, k, 0:SEQ], ACT.Copy).then_inc(uh_ready, 1)
            act.wait_ge(ys_sum, 1)
            nc.scalar.activation(y_std[:], y_std[:], ACT.Sqrt, bias=eps_col[:, 0:1], scale=1.0 / (4 * GW)).then_inc(ys_std, 1)
            split_hi(act, T_POOL + 2)
            act.wait_ge(ys_n, 1)
            nc.scalar.activation(b_hi[:, :, SEQ:TT], y_s[:, 8:16, :], ACT.Copy).then_inc(ys_hi, 1)
            act.wait_ge(pool_mm, 8)
            split_hi(act, T_POOL + 3)
            for k in range(8):
                nc.scalar.activation(a_hi[:, k, 0:SEQ], zs[:, k, 0:SEQ], ACT.Copy).then_inc(uh_ready, 1)
            nc.scalar.activation(a_hi[:, :, SEQ:TT], y_s[:, 0:8, :], ACT.Copy).then_inc(ys_hi, 1)
            for c4 in range(4):
                for m in range(2):
                    split_hi(act, T_SSD + 4 * c4 + m + 2)
                for m in range(2):
                    k = 2 * c4 + m
                    split_hi(act, T_SSD + 4 * c4 + m + 4)
                    act.wait_ge(mg_ready, k + 1)
                    nc.scalar.activation(c_hi[:, k, :], ut[k % 2][:], ACT.Copy).then_inc(mgh_ready, 1)

            def res_tile(q, t, k):
                act.wait_ge(gemm_done, t + 1)
                split_hi(act, t + 2)
                act.wait_ge(evacuated[t % 2], uses(t) + 2)
                act.wait_ge(sq_used, q + k - 1)
                nc.scalar.activation(sq[k % 2][:], x[:, k, :], ACT.Square).then_inc(sq_ready, 1)

            def turned(t):
                return t.rearrange("p (k m d) -> p m k d", k=2, m=2)

            for k in range(KT):
                res_tile(24, T_O + k, k)
                if 3 <= k < 7:
                    n = k - 3
                    act.wait_ge(mem_tr, n + 1)
                    nc.scalar.activation(mem_hi[:, 2 * n:2 * n + 2, :], aux[:, n % 2, :].rearrange("p (k m) -> p k m", k=2),
                                         ACT.Copy).then_inc(mem_hi_s, 1)
            norm_std(32, 1.0 / D)
            for k in range(KT):
                t = T_K + k
                act.wait_ge(gemm_done, t + 1)
                split_hi(act, t + 2)
                nc.scalar.activation(kT[:, k, :], slot[t % 2][:, 0, 0:MEM], ACT.Copy).then_inc(evacuated[t % 2], 1)
                act.wait_ge(ut_ready, 24 + k + 1)
                nc.scalar.activation(a_hi[:, k, :], ut[k % 2][:], ACT.Copy).then_inc(uh_ready, 1)
            for k in range(8):
                t = T_Q + k
                act.wait_ge(gemm_done, t + 1)
                split_hi(act, t + 2)
                nc.scalar.activation(halves(qT[:, k, :]), in_slot(t % 2), ACT.Copy).then_inc(evacuated[t % 2], 1)
                if k % 2:
                    n = k // 2
                    act.wait_ge(kt_mm, n + 1)
                    nc.scalar.activation(k_tok[:, :, n * 256:(n + 1) * 256].rearrange("p m (k d) -> p m k d", k=2),
                                         turned(aux[:, n % 2, :]), ACT.Copy).then_inc(kt_ev, 1)

            def v_turned(n):
                act.wait_ge(vt_mm, n + 1)
                nc.scalar.activation(v_tok[:, :, n * 256:(n + 1) * 256].rearrange("p m (k d) -> p m k d", k=2),
                                     turned(slot[n % 2][:, 1, :]), ACT.Copy).then_inc(vt_ev, 1)

            for k in range(8):
                t = T_V + k
                act.wait_ge(gemm_done, t + 1)
                split_hi(act, t + 2)
                nc.scalar.activation(vT[:, k, :], slot[t % 2][:, 0, 0:MEM], ACT.Copy).then_inc(evacuated[t % 2], 1)
                if k == 0:
                    act.wait_ge(qt_mm, 1)
                    nc.scalar.activation(q_tok[:].rearrange("p (j n) -> p j n", j=2), aux[0:NS, 0:2, :], ACT.Copy).then_inc(qt_ev, 1)
                if k >= 3 and k % 2:
                    v_turned((k - 3) // 2)
            v_turned(3)
            act.wait_ge(sm_b, 1)
            nc.scalar.activation(prob_s[:], slot[0][0:32, 1, 0:MEM], ACT.Exp, bias=stats[0:32, 1:2], scale=XD ** -0.5,
                                 accum_out=stats[0:32, 2:3]).then_inc(sm_c, 1)
            for n in range(16):
                h, tq = n // 4, n % 4
                act.wait_ge(negmax, n + 1)
                nc.scalar.activation(prob[n % 2][:], aux[:, n % 2, 0:MEM], ACT.Exp, bias=stats[:, 16 + n:17 + n],
                                     scale=XD ** -0.5, accum_out=stats[:, 32 + n:33 + n]).then_inc(prob_exp, 1)
                act.wait_ge(pt_mm, n + 1)
                nc.scalar.activation(probT[h % 2][:, :, tq * P:(tq + 1) * P],
                                     aux[:, 2 + n % 2, 0:MEM].rearrange("p (m l) -> p m l", m=2), ACT.Copy).then_inc(pt_ev, 1)
                if tq == 3:
                    for dt in range(2):
                        act.wait_ge(pv_mm, 2 * h + dt + 1)
                        nc.scalar.activation(a_hi[:, 2 * h + dt, 0:SEQ], slot[dt][:, 0, :], ACT.Copy).then_inc(pv_hi, 1)
            act.wait_ge(cache_used, 2 * NS)
            nc.scalar.activation(a_hi[:, :, SEQ:TT], slot[0][:, 1, 0:64].rearrange("p (k b) -> p k b", k=KT),
                                 ACT.Copy).then_inc(o_s_hi, 1)
            for k in range(KT):
                res_tile(32, T_XO + k, k)
            norm_std(40, 1.0 / D)
            norm_hi(32, a_hi)

            def ff_up(t, k, n, i=0):
                act.wait_ge(gemm_done, t + 1 + i * 16)
                split_hi(act, t + 2, i, 16)
                nc.scalar.activation(halves(rt[k % 2][:]), in_slot(t % 2), ACT.Relu).then_inc(evacuated[t % 2], 1)
                act.wait_ge(ff_sq, n + 1 + i * 8)
                nc.scalar.activation(c_hi[:, k, :], ut[k % 2][:], ACT.Copy).then_inc(ff_hi, 1)

            with act.Fori(0, FF_CHUNKS - 1) as i:
                for k in range(8):
                    ff_up(T_MLP + k, k, k, i)
                for k in range(8):
                    split_hi(act, T_MLP + 8 + k + 2, i, 16)
            T_LAST = T_MLP + 16 * (FF_CHUNKS - 1)
            for k in range(8):
                ff_up(T_LAST + k, k, 8 * (FF_CHUNKS - 1) + k)
            for k in range(8):
                res_tile(40, T_LAST + 8 + k, k)
            norm_std(48, 1.0 / D)

        @block.vector
        def _(dve):
            chain = Chain(dve, v_step)
            dve.sem_inc(evacuated[0], 1)
            dve.sem_inc(evacuated[1], 1)
            dve.sem_inc(xtr2_evac, 2)
            nc.vector.memset(eps_col[:], EPS).then_inc(consts, 1)

            def norm_scale(q, m, src, gain, dst, n=KT, first=0, between=None):
                dve.wait_ge(std_ready, m + 1)
                chain(nc.vector.reciprocal(rstd[:], std[:]))

                def lo(k):
                    dve.wait_ge(uh_ready, q + k + 1)
                    d = dst(k)
                    nc.vector.tensor_tensor(d[1], ut[k % 2][:], d[0].bitcast(F32), ALU.subtract).then_inc(u_ready, 1)

                for k in range(first, first + n):
                    if between is not None:
                        between(k)
                    if k >= first + 2:
                        lo(k - 2)
                        dve.wait_ge(u_ready, q + k - 1)
                    nc.vector.scalar_tensor_tensor(out=ut[k % 2][:], in0=src(k), scalar=cols[:, gain + k:gain + k + 1],
                                                   in1=rstd[:], op0=ALU.mult, op1=ALU.mult).then_inc(ut_ready, 1)
                lo(first + n - 2)
                lo(first + n - 1)

            dve.wait_ge(xtr_done, 1)
            nc.vector.tensor_copy(x0[:, :, SEQ:TT], aux[:, 0, 0:64].rearrange("p (k b) -> p k b", k=KT)).then_inc(xtr_evac, 1)
            dve.wait_ge(xtr_done, 2)
            nc.vector.tensor_copy(cols[:, 0:C_PS], aux[:, 1, 0:C_PS])
            nc.vector.tensor_scalar(cols[:, C_PS:C_SSD], aux[:, 1, C_PS:C_SSD], 0.5, None, ALU.mult)
            nc.vector.tensor_scalar(cols[:, C_SSD:C_CW], aux[:, 1, C_SSD:C_CW], 0.25, None, ALU.mult)
            nc.vector.tensor_scalar(cols[:, C_CW:176], aux[:, 1, C_CW:176], 0.5, None, ALU.mult).then_inc(xtr_evac, 1)
            for k in range(KT):
                dve.wait_ge(xtr_done, 3 + k)
                nc.vector.tensor_copy(x0[:, k, 0:SEQ], aux[:, k % 2, :]).then_inc(xtr_evac, 1)
            split_lo(dve, 0)
            split_lo(dve, 1)
            dve.wait_ge(dtw_hi_s, 1)
            nc.vector.tensor_tensor(dtw_lo[:], dtw[:], dtw_hi[:].bitcast(F32), ALU.subtract).then_inc(dtw_lo_s, 1)
            norm_scale(0, 0, lambda k: x0[:, k, :], CN_MIX, lambda k: (a_hi[:, k, :], a_lo[:, k, :]))

            dve.wait_ge(dt_mm, 1)
            nc.vector.tensor_scalar(halves(dt_tmp[0][:]), aux[0:HEADS, 0:2, 0:HALF], hcol[:, 0:1], None, ALU.add).then_inc(dt_evac, 1)
            dve.wait_ge(dt_a, 2)
            e, w, msk = dt_tmp[1], dt_tmp[2], dt_tmp[3]
            chain(nc.vector.tensor_scalar(w[:], e[:], 1.0, None, ALU.add))
            chain(nc.vector.tensor_scalar(dtT[:, 0, :], w[:], -1.0, None, ALU.add))
            chain(nc.vector.tensor_scalar(msk[:], dtT[:, 0, :], 0.0, None, ALU.is_equal))
            chain(nc.vector.tensor_tensor(dtT[:, 0, :], dtT[:, 0, :], msk[:], ALU.add))
            nc.vector.reciprocal(dtT[:, 0, :], dtT[:, 0, :]).then_inc(dt_b, 1)
            dve.wait_ge(dt_b, 1)
            dve.wait_ge(dt_a, 3)
            chain(nc.vector.tensor_tensor(w[:], w[:], msk[:], ALU.add))
            chain(nc.vector.tensor_tensor(w[:], w[:], dtT[:, 0, :], ALU.mult))
            chain(nc.vector.tensor_tensor(w[:], w[:], e[:], ALU.mult))
            chain(nc.vector.scalar_tensor_tensor(out=dtT[:, 0, :], in0=dt_tmp[0][:], scalar=0.0, in1=w[:],
                                                 op0=ALU.max, op1=ALU.add))
            nc.vector.tensor_copy(hs_rhs[:, 0:NS], dtT[:, 0, SEQ:TT])
            nc.vector.tensor_scalar(dtT[:, 1, :], dtT[:, 0, :], hcol[:, 2:3], -1.0, ALU.mult, ALU.mult).then_inc(dt_b, 1)
            dve.wait_ge(dt_tr, 1)
            nc.vector.tensor_copy(dtk[:].rearrange("p j c h -> p (j c h)"), aux[:, 2, 0:2 * P]).then_inc(dt_trv, 1)
            dve.wait_ge(cs_mm, 1)
            fl = "p c h -> p (c h)"
            chain(nc.vector.tensor_scalar(ncs[:].rearrange(fl), aux[:, 0, 0:P], -1.0, None, ALU.mult))
            nc.vector.tensor_tensor(dtd[:].rearrange(fl), aux[:, 0, P:2 * P], ncs[:].rearrange(fl), ALU.add).then_inc(cs_v, 1)
            dve.wait_ge(dt_a, 6)
            nc.vector.tensor_tensor(dtd[:], dtd[:], dtk[:, 0], ALU.mult).then_inc(cs_v, 1)
            dve.wait_ge(spilled, 16)
            nc.vector.tensor_copy(spread[:].rearrange("h t (j d) -> h (t j) d", j=2),
                                  ident[0:HEADS, 0:HEADS].unsqueeze(2).to_broadcast([HEADS, HEADS, HD])).then_inc(old_ev, 1)

            def conv_front(t, dst, done, i=0):
                dve.wait_ge(evacuated[t % 2], t // 2 + 2 + i * 4)
                b = cbuf[t % 2]
                f = t + i * 8
                nc.vector.tensor_copy(xedge[:, f, :], b[:, SEQ:SEQ + EDGE])
                h = hbuf[t % 2][:]
                chain(nc.vector.tensor_scalar(h, b[:, 0:SEQ], cols[:, bass.ds(C_CW + f, 1)], cols[:, bass.ds(C_CB + f, 1)],
                                              ALU.mult, ALU.add))
                for k in range(1, TAPS):
                    ins = nc.vector.scalar_tensor_tensor(out=h, in0=b[:, k:k + SEQ], scalar=cols[:, bass.ds(C_CW + CT * k + f, 1)],
                                                         in1=h, op0=ALU.mult, op1=ALU.add)
                    if k < TAPS - 1:
                        chain(ins)
                    else:
                        ins.then_inc(conv_done, 1)
                split_lo(dve, t + 2, i, 8)
                dve.wait_ge(tanh_done, t + 1 + i * 8)
                nc.vector.scalar_tensor_tensor(out=dst, in0=tbuf[:], scalar=1.0, in1=h, op0=ALU.add,
                                               op1=ALU.mult).then_inc(done, 1)

            conv_front(0, abuf[0][:], act_ready)
            with dve.Fori(0, 2) as i:
                chain.loop(i, 24)
                for t in range(8):
                    conv_front(t + 1, abuf[(t + 1) % 2][:], act_ready, i)
                chain.end(2)
            dve.wait_ge(act_ready, 17)
            nc.vector.tensor_copy(bc[:, 0, 0:SEQ], abuf[0][:]).then_inc(bc_ready, 1)
            for t in range(17, 24):
                conv_front(t, bc[:, t - 16, 0:SEQ], bc_ready)
                m = t - 17
                if m < 5:
                    dve.wait_ge(old_tr, m + 1)
                    src = aux[:, 2 * (m % 2), :]
                    if m < 2:
                        ins = nc.vector.tensor_copy(sp_cols[:, 4 * m:4 * m + 4, :], src[:, 0:480].rearrange("p (k b) -> p k b", k=4))
                    elif m < 4:
                        ins = nc.vector.tensor_copy(st_cols[:, 12 * m - 24:12 * m - 12, :],
                                                    src[:, 0:288].rearrange("p (k b) -> p k b", k=12))
                    else:
                        ins = nc.vector.tensor_copy(exp_s[:].rearrange("p t j -> p (t j)"), src[:, 0:16 * 17])
                    ins.then_inc(old_ev, 1)

            def heads(t):
                return t.rearrange("p (h d) -> p h d", h=HPG)

            def prep(c, gr):
                hd = slice(gr * HPG, (gr + 1) * HPG)
                xs = heads(xs_tok[:, c, gr * GW:(gr + 1) * GW])
                nc.vector.tensor_tensor(heads(xdt[:]), xs, dtk[:, 0, c, hd].unsqueeze(2).to_broadcast([P, HPG, HD]), ALU.mult)
                nc.vector.tensor_tensor(heads(xdd[:]), xs, dtd[:, c, hd].unsqueeze(2).to_broadcast([P, HPG, HD]),
                                        ALU.mult).then_inc(x_prep, 1)

            def weights_a(s):
                dve.wait_ge(cb_ready, s)
                chain(nc.vector.tensor_tensor(cbm[:], aux[:, 1, 0:P], triu[:], ALU.mult))
                dve.wait_ge(exp_a, s)
                nc.vector.tensor_tensor(decay[:, 0:4, :], decay[:, 0:4, :], cbm[:].unsqueeze(1).to_broadcast([P, 4, P]), ALU.mult)

            def carry(s, c, gr):
                hd = slice(gr * HPG, (gr + 1) * HPG)
                dve.wait_ge(off_ready, s)
                nc.vector.tensor_tensor(heads(yacc[:]), heads(aux[:, 2, :]), ecs[:, c, hd].unsqueeze(2).to_broadcast([P, HPG, HD]), ALU.mult)
                chain(nc.vector.tensor_tensor(heads(state[:, gr, :]), heads(state[:, gr, :]),
                                              cdec[:, c, hd].unsqueeze(2).to_broadcast([P, HPG, HD]), ALU.mult))
                nc.vector.tensor_tensor(state[:, gr, :], state[:, gr, :], aux[:, 3, :], ALU.add)
                dve.wait_ge(exp_b, s)
                nc.vector.tensor_tensor(decay[:, 4:8, :], decay[:, 4:8, :], cbm[:].unsqueeze(1).to_broadcast([P, 4, P]),
                                        ALU.mult).then_inc(m_ready, 1)

            def finish_y(s, c, gr):
                dve.wait_ge(y_mm, s)
                chain(nc.vector.tensor_tensor(yacc[:], yacc[:], aux[:, 2, :], ALU.add))
                dve.wait_ge(skip_ready, s)
                nc.vector.tensor_tensor(xs_tok[:, c, gr * GW:(gr + 1) * GW], yacc[:], xskip[:], ALU.add).then_inc(y_ready, 1)

            def z_tile(t, k, i):
                split_lo(dve, t + 2, i, 8)
                dve.wait_ge(tz_ready, k + 1 + i * 8)
                nc.vector.scalar_tensor_tensor(out=halves(zs[:, k + i * 8, :]), in0=halves(tz[t % 2][:]), scalar=1.0,
                                               in1=in_slot(t % 2), op0=ALU.add, op1=ALU.mult).then_inc(evacuated[t % 2], 1)

            dve.wait_ge(xtr2_evac, 18)
            dve.wait_ge(bc_ready, 8)
            dve.wait_ge(spilled, 16)
            dve.wait_ge(st_zero, 1)
            dve.wait_ge(cs_v, 2)
            with dve.Fori(0, 2) as i:
                chain.loop(i, 12)
                for gr in range(GROUPS):
                    s = 4 * i + gr + 1
                    prep(i, gr)
                    weights_a(s)
                    z_tile(T_Z + 2 * gr, 2 * gr, i)
                    carry(s, i, gr)
                    z_tile(T_Z + 2 * gr + 1, 2 * gr + 1, i)
                    finish_y(s, i, gr)
                chain.end(2)
            def wcol(k):
                return cols[:, C_CW + CT * k:C_CW + CT * (k + 1)].unsqueeze(2).to_broadcast([P, CT, NS])
            old = st_cols[:].rearrange("p f (b k) -> p f k b", k=3)
            chain(nc.vector.tensor_tensor(tmp_s[:], xedge[:, :, TAPS - 1:EDGE], wcol(3), ALU.mult))
            chain(nc.vector.tensor_tensor(tmp_s[:], tmp_s[:], cols[:, C_CB:C_CB + CT].unsqueeze(2).to_broadcast([P, CT, NS]), ALU.add))
            for k in range(3):
                chain(nc.vector.tensor_tensor(acts_s[:], old[:, :, k, :], wcol(k), ALU.mult))
                ins = nc.vector.tensor_tensor(tmp_s[:], tmp_s[:], acts_s[:], ALU.add)
                if k < 2:
                    chain(ins)
                else:
                    ins.then_inc(smp_v, 1)
            with dve.Fori(0, 2) as i:
                chain.loop(i, 12)
                for gr in range(GROUPS):
                    s = 8 + 4 * i + gr + 1
                    prep(2 + i, gr)
                    weights_a(s)
                    carry(s, 2 + i, gr)
                    split_lo(dve, T_PU + gr + 2, i, 4)
                    finish_y(s, 2 + i, gr)
                chain.end(2)

            dve.wait_ge(smp_a, 1)
            nc.vector.scalar_tensor_tensor(out=acts_s[:], in0=acts_s[:], scalar=1.0, in1=tmp_s[:], op0=ALU.add,
                                           op1=ALU.mult).then_inc(smp_v, 1)
            for n in range(4):
                dve.wait_ge(end_tr, n + 1)
                nc.vector.tensor_copy(state_out[:, 4 * n:4 * n + 4, :], aux[:, n, :].rearrange("p (t n) -> p t n", t=4)).then_inc(end_ev, 1)
            dve.wait_ge(end_tr, 5)
            nc.vector.tensor_copy(bc_s[:, :].rearrange("p (j n) -> p j n", j=2), aux[0:NS, 0:2, :]).then_inc(end_ev, 1)
            dve.wait_ge(smp_v, 2)
            nc.vector.tensor_tensor(xdt_s[:], acts_s[:, 0:16, :], exp_s[:, :, 0:NS], ALU.mult).then_inc(smp_v, 1)
            for n in range(2):
                dve.wait_ge(end_tr, 6 + n)
                nc.vector.tensor_copy(pool_edge[:, n * 512:(n + 1) * 512], aux[0:PEDGE, 2 + n, :]).then_inc(end_ev, 1)
            new = tmp_s[:, 16:24, :]
            for k in range(KT):
                w = WINDOWS[k // 2]
                old = sp_cols[:, k, :].rearrange("p (b j) -> p b j", b=NS)[:, :, PBUF - w + 1:PBUF]
                ins = nc.vector.tensor_reduce(new[:, k, :], old, AX.X, ALU.add)
            chain(ins)
            chain(nc.vector.tensor_tensor(new, new, pu[:, :, SEQ:TT], ALU.add))
            for gi, w in enumerate(WINDOWS):
                two = slice(2 * gi, 2 * gi + 2)
                ins = nc.vector.scalar_tensor_tensor(out=pu[:, two, SEQ:TT], in0=new[:, two, :], scalar=1.0 / w,
                                                     in1=pu[:, two, SEQ:TT], op0=ALU.mult, op1=ALU.subtract)
            ins.then_inc(pool_sum_s, 1)

            def recurrence_s(n):
                b, j = n // 2, n % 2
                dve.wait_ge(st_dec, n + 1)
                dve.wait_ge(bc_mm, b + 1)
                for t in range(8):
                    tt = 8 * j + t
                    gg = tt // 4
                    S = sring[n % SR][:, t, :]
                    ins = nc.vector.scalar_tensor_tensor(out=S, in0=aux[:, 0, gg * P:(gg + 1) * P],
                                                         scalar=xdt_s[:, tt, b:b + 1], in1=S, op0=ALU.mult, op1=ALU.add)
                ins.then_inc(st_new, 1)
                dve.wait_ge(st_new, n + 1)
                for t in range(8):
                    tt = 8 * j + t
                    gg = tt // 4
                    ins = nc.vector.tensor_tensor_reduce(junk_s[:, t, :], sring[n % SR][:, t, :], aux[:, 1, gg * P:(gg + 1) * P],
                                                         1.0, 0.0, ALU.mult, ALU.add, y_s[:, tt, b:b + 1])
                ins.then_inc(bc_used, 1)

            def scale_y(f):
                if f % 4 == 0:
                    dve.wait_ge(std_ready, 2 + f // 4)
                    chain(nc.vector.reciprocal(yrstd[:], ystd[:]))
                nc.vector.scalar_tensor_tensor(out=zs[:, f, 0:SEQ], in0=zs[:, f, 0:SEQ], scalar=cols[:, C_SSD + f:C_SSD + f + 1],
                                               in1=yrstd[:], op0=ALU.mult, op1=ALU.mult).then_inc(ut_ready, 1)

            dve.wait_ge(smp_v, 3)
            recurrence_s(0)
            for k in range(8):
                split_lo(dve, T_GA + k + 2)
                recurrence_s(k + 1)
                for f in (2 * k, 2 * k + 1):
                    dve.wait_ge(yt_mm, f + 1)
                    nc.vector.tensor_tensor(zs[:, f, 0:SEQ], aux[:, 2 + f % 2, :], zs[:, f, 0:SEQ], ALU.mult).then_inc(yt_ev, 1)
            dve.wait_ge(yt_ev, 16)
            for k in range(8):
                split_lo(dve, T_GB + k + 2)
                if k < 7:
                    recurrence_s(9 + k)
                if k >= 2:
                    scale_y(2 * k - 4)
                    scale_y(2 * k - 3)
            dve.wait_ge(bc_used, 16)
            chain(nc.vector.tensor_tensor(tmp_s[:, 0:16, :], acts_s[:, 0:16, :], exp_s[:, :, 16:17].to_broadcast([P, 16, NS]), ALU.mult))
            chain(nc.vector.tensor_tensor(y_s[:], y_s[:], tmp_s[:, 0:16, :], ALU.add))
            nc.vector.tensor_tensor(y_s[:], y_s[:], zs[:, :, SEQ:TT], ALU.mult).then_inc(ys_ready, 1)
            for k in range(KT):
                dve.wait_ge(pool_hi, k + 1)
                nc.vector.tensor_tensor(a_lo[:, k, :], pu[:, k, :], a_hi[:, k, :].bitcast(F32), ALU.subtract).then_inc(pool_lo, 1)
            for f in range(12, 16):
                scale_y(f)
            dve.wait_ge(ys_mm, 1)
            nc.vector.tensor_reduce(y_std[:], slot[0][:, 0, 0:P].rearrange("p (g k b) -> p g b k", g=GROUPS, b=NS), AX.X,
                                    ALU.add).then_inc(ys_sum, 1)
            for n in range(8):
                m, gi = n // 4, n % 4
                f = 2 * gi + m
                dve.wait_ge(pool_mm, n + 1)
                nc.vector.scalar_tensor_tensor(out=halves(gate_b[:, f, :]), in0=halves(gate_b[:, f, :]), scalar=1.0,
                                               in1=aux[:, 2 * (n % 2):2 * (n % 2) + 2, 0:HALF],
                                               op0=ALU.add, op1=ALU.mult).then_inc(pool_ev, 1)
                dve.wait_ge(uh_ready, 8 + n + 1)
                nc.vector.tensor_tensor(b_lo[:, n, 0:SEQ], zs[:, n + 8, 0:SEQ], b_hi[:, n, 0:SEQ].bitcast(F32),
                                        ALU.subtract).then_inc(u_ready, 1)
                if n == 3:
                    dve.wait_ge(ys_std, 1)
                    chain(nc.vector.reciprocal(y_std[:], y_std[:]))
                    chain(nc.vector.tensor_tensor(y_s[:], y_s[:], cols[:, C_SSD:C_SSD + 16].unsqueeze(2).to_broadcast([P, 16, NS]), ALU.mult))
                    nc.vector.tensor_tensor(y_s[:].rearrange("p (g k) b -> p g k b", g=GROUPS), y_s[:].rearrange("p (g k) b -> p g k b", g=GROUPS),
                                            y_std[:].unsqueeze(2).to_broadcast([P, GROUPS, 4, NS]), ALU.mult).then_inc(ys_n, 1)
                if n == 4:
                    split_lo(dve, T_POOL + 2)
                    dve.wait_ge(ys_hi, 1)
                    nc.vector.tensor_tensor(b_lo[:, :, SEQ:TT], y_s[:, 8:16, :], b_hi[:, :, SEQ:TT].bitcast(F32),
                                            ALU.subtract).then_inc(ys_lo, 1)
            split_lo(dve, T_POOL + 3)
            for k in range(8):
                dve.wait_ge(uh_ready, 16 + k + 1)
                nc.vector.tensor_tensor(a_lo[:, k, 0:SEQ], zs[:, k, 0:SEQ], a_hi[:, k, 0:SEQ].bitcast(F32),
                                        ALU.subtract).then_inc(u_ready, 1)
            dve.wait_ge(ys_hi, 2)
            nc.vector.tensor_tensor(a_lo[:, :, SEQ:TT], y_s[:, 0:8, :], a_hi[:, :, SEQ:TT].bitcast(F32),
                                    ALU.subtract).then_inc(ys_lo, 1)
            for k in range(SR):
                dve.wait_ge(st_out[k], 16 * len(range(k, 2 * NS, SR)))

            for c4 in range(4):
                for m in range(2):
                    split_lo(dve, T_SSD + 4 * c4 + m + 2)
                for m in range(2):
                    k = 2 * c4 + m
                    t = T_SSD + 4 * c4 + 2 + m
                    split_lo(dve, t + 2)
                    dve.wait_ge(gemm_done, t + 1)
                    if k >= 2:
                        dve.wait_ge(mgl_ready, k - 1)
                    nc.vector.scalar_tensor_tensor(out=halves(ut[k % 2][:]), in0=halves(gate_a[:, k, :]), scalar=1.0,
                                                   in1=in_slot(m), op0=ALU.add, op1=ALU.mult).then_inc(evacuated[m], 1)
                    dve.wait_ge(evacuated[m], uses(T_SSD + 4 * c4 + m) + 2)
                    nc.vector.scalar_tensor_tensor(out=ut[k % 2][:], in0=gate_b[:, k, :], scalar=cols[:, C_PS + k:C_PS + k + 1],
                                                   in1=ut[k % 2][:], op0=ALU.mult, op1=ALU.add).then_inc(mg_ready, 1)
                    dve.wait_ge(mgh_ready, k + 1)
                    nc.vector.tensor_tensor(c_lo[:, k, :], ut[k % 2][:], c_hi[:, k, :].bitcast(F32), ALU.subtract).then_inc(mgl_ready, 1)

            def residual(t, k, i=0, step=0):
                split_lo(dve, t + 2, i, step)
                dve.wait_ge(gemm_done, t + 1 + i * step)
                nc.vector.tensor_tensor(halves(x[:, k, :]), in_slot(t % 2), halves(x[:, k, :]),
                                        ALU.add).then_inc(evacuated[t % 2], 1)

            dve.wait_ge(reloaded, 16)
            for k in range(KT):
                residual(T_O + k, k)
                if 3 <= k < 7:
                    n = k - 3
                    dve.wait_ge(mem_hi_s, n + 1)
                    nc.vector.tensor_tensor(mem_lo[:, 2 * n:2 * n + 2, :], aux[:, n % 2, :].rearrange("p (k m) -> p k m", k=2),
                                            mem_hi[:, 2 * n:2 * n + 2, :].bitcast(F32), ALU.subtract).then_inc(mem_lo_s, 1)
            norm_scale(24, 5, lambda k: x[:, k, :], CN_X, lambda k: (a_hi[:, k, :], a_lo[:, k, :]),
                       between=lambda k: split_lo(dve, T_K + k + 2))
            for k in range(8):
                split_lo(dve, T_Q + k + 2)
            for b in range(NS):
                split_lo(dve, T_V + b + 2)
                dve.wait_ge(qb_mm, b + 1)
                dve.wait_ge(cache_in[b % CR], 16 * (b // CR + 1))
                if b >= 1:
                    dve.wait_ge(cache_used, b)
                for m in range(2):
                    for h in range(XH):
                        c = m * 32 + b * XH + h
                        ins = nc.vector.tensor_tensor_reduce(junk[:, m, h, :], cache[b % CR][:, m, h * XD:(h + 1) * XD],
                                                             q_bank(b)[:, h // 2, h % 2 * XD:(h % 2 + 1) * XD], 1.0, 0.0,
                                                             ALU.mult, ALU.add, s_cols[:, c:c + 1])
                ins.then_inc(cache_used, 1)
            dve.wait_ge(sm_a, 1)
            chain(nc.vector.tensor_reduce(stats[0:32, 0:1], slot[0][0:32, 1, 0:MEM], AX.X, ALU.max))
            nc.vector.tensor_scalar(stats[0:32, 1:2], stats[0:32, 0:1], -(XD ** -0.5), None, ALU.mult).then_inc(sm_b, 1)
            dve.wait_ge(sm_c, 1)
            chain(nc.vector.reciprocal(stats[0:32, 3:4], stats[0:32, 2:3]))
            nc.vector.tensor_scalar(prob_s[:], prob_s[:], stats[0:32, 3:4], None, ALU.mult).then_inc(sm_d, 1)
            dve.wait_ge(sm_e, 1)
            nc.vector.tensor_copy(pT_s[:], slot[1][:, 1, 0:64]).then_inc(sm_f, 1)

            def row_max(n):
                dve.wait_ge(score_mm, n + 1)
                chain(nc.vector.tensor_reduce(stats[:, 48 + n:49 + n], aux[:, n % 2, 0:MEM], AX.X, ALU.max))
                nc.vector.tensor_scalar(stats[:, 16 + n:17 + n], stats[:, 48 + n:49 + n], -(XD ** -0.5), None, ALU.mult).then_inc(negmax, 1)

            row_max(0)
            for n in range(16):
                h = n // 4
                if n + 1 < 16:
                    row_max(n + 1)
                dve.wait_ge(prob_exp, n + 1)
                chain(nc.vector.reciprocal(stats[:, 64 + n % 16:65 + n % 16], stats[:, 32 + n:33 + n]))
                nc.vector.tensor_scalar(prob[n % 2][:], prob[n % 2][:], stats[:, 64 + n % 16:65 + n % 16], None, ALU.mult).then_inc(prob_n, 1)
                if n % 4 == 3:
                    for dt in range(2):
                        k = 2 * h + dt
                        dve.wait_ge(pv_hi, k + 1)
                        nc.vector.tensor_tensor(a_lo[:, k, 0:SEQ], slot[dt][:, 0, :], a_hi[:, k, 0:SEQ].bitcast(F32),
                                                ALU.subtract).then_inc(pv_lo, 1)
            dve.wait_ge(o_s_hi, 1)
            nc.vector.tensor_tensor(a_lo[:, :, SEQ:TT], slot[0][:, 1, 0:64].rearrange("p (k b) -> p k b", k=KT),
                                    a_hi[:, :, SEQ:TT].bitcast(F32), ALU.subtract).then_inc(o_s_lo, 1)
            for k in range(KT):
                residual(T_XO + k, k)
            norm_scale(32, 6, lambda k: x[:, k, :], CN_MLP, lambda k: (a_hi[:, k, :], a_lo[:, k, :]))

            def ff_up(t, k, n, i=0):
                split_lo(dve, t + 2, i, 16)
                dve.wait_ge(evacuated[t % 2], uses(t) + 2 + i * 8)
                if k >= 2:
                    dve.wait_ge(ff_lo, n - 1 + i * 8)
                nc.vector.tensor_tensor(ut[k % 2][:], rt[k % 2][:], rt[k % 2][:], ALU.mult).then_inc(ff_sq, 1)
                dve.wait_ge(ff_hi, n + 1 + i * 8)
                nc.vector.tensor_tensor(c_lo[:, k, :], ut[k % 2][:], c_hi[:, k, :].bitcast(F32), ALU.subtract).then_inc(ff_lo, 1)

            with dve.Fori(0, FF_CHUNKS - 1) as i:
                for k in range(8):
                    ff_up(T_MLP + k, k, k, i)
                for k in range(8):
                    residual(T_MLP + 8 + k, k, i, 16)
            T_LAST = T_MLP + 16 * (FF_CHUNKS - 1)
            for k in range(8):
                ff_up(T_LAST + k, k, 8 * (FF_CHUNKS - 1) + k)
            for k in range(8):
                residual(T_LAST + 8 + k, k)
            dve.wait_ge(std_ready, 8)
            chain(nc.vector.reciprocal(rstd[:], std[:]))
            for k in range(KT):
                nc.vector.scalar_tensor_tensor(out=x[:, k, :], in0=x[:, k, :], scalar=cols[:, CN_FIN + k:CN_FIN + k + 1],
                                               in1=rstd[:], op0=ALU.mult, op1=ALU.mult).then_inc(fin_n, 1)
            for n in range(2):
                dve.wait_ge(fin_mm, n + 1)
                nc.vector.tensor_copy(ys_tok[:, n * 512:(n + 1) * 512], aux[0:NS, n, :]).then_inc(fin_ev, 1)
            for n in range(8):
                dve.wait_ge(fin_mm, n + 3)
                nc.vector.tensor_copy(y_tok[:, n // 2, n % 2 * 512:(n % 2 + 1) * 512], aux[:, n % 4, :]).then_inc(fin_ev, 1)

        @block.tensor
        def _(pe):
            pe.wait_ge(consts, 5)
            pe.wait_ge(s_in, 16)
            for k in range(KT):
                last = nc.tensor.transpose(aux[:, 0, NS * k:NS * k + NS], xs_row[:, k * P:(k + 1) * P], ident[0:NS, 0:NS])
            last.then_inc(xtr_done, 1)
            pe.wait_ge(vec_in, 16 * 8)
            nc.tensor.transpose(aux[:, 1, 0:56], vr1[:], ident[0:56, 0:56])
            nc.tensor.transpose(aux[:, 1, 56:176], vr2[:], ident[0:120, 0:120]).then_inc(xtr_done, 1)
            pe.wait_ge(x_in, 16)
            for k in range(KT):
                pe.wait_ge(xtr_evac, k + 1)
                for c in range(NCH):
                    last = nc.tensor.transpose(aux[:, k % 2, c * P:(c + 1) * P], x_tok[:, c, k * P:(k + 1) * P], ident[:])
                last.then_inc(xtr_done, 1)

            def norm_tile(q, k, first, last_one):
                pe.wait_ge(sq_ready, q + k + 1)
                for h in range(2):
                    ins = nc.tensor.matmul(aux[:, 2 + h, 0:HALF], ones[:], sq[k % 2][:, h * HALF:(h + 1) * HALF],
                                           start=first, stop=last_one)
                ins.then_inc(sq_used, 1)
                return ins

            def norm_pe(q, n=KT, first=0, m=0):
                if m:
                    pe.wait_ge(std_ready, m)
                for k in range(first, first + n):
                    norm_tile(q, k, k == first, k == first + n - 1)

            norm_pe(0)
            pe.wait_ge(u_ready, KT)
            pe.wait_ge(dtw_lo_s, 1)
            for k in range(KT):
                for n, (w, u) in enumerate(((dtw_hi, a_hi), (dtw_hi, a_lo), (dtw_lo, a_hi))):
                    for h in range(2):
                        last = nc.tensor.matmul(aux[0:HEADS, h, 0:HALF], w[:, k, :], u[:, k, h * HALF:(h + 1) * HALF],
                                                start=(k == 0 and n == 0), stop=(k == KT - 1 and n == 2))
            last.then_inc(dt_mm, 1)
            gemm(pe, 0, a_hi, a_lo)
            pe.wait_ge(dt_b, 2)
            for j in range(2):
                for c in range(NCH):
                    last = nc.tensor.transpose(aux[:, 2, (j * NCH + c) * HEADS:(j * NCH + c + 1) * HEADS],
                                               dtT[:, j, c * P:(c + 1) * P], ident[0:HEADS, 0:HEADS])
            last.then_inc(dt_tr, 1)
            pe.wait_ge(dt_trv, 1)
            rhs = dtk[:, 1].rearrange("p c h -> p (c h)")
            nc.tensor.matmul(aux[:, 0, 0:P], triu[:], rhs, start=True, stop=True)
            nc.tensor.matmul(aux[:, 0, P:2 * P], ones[:], rhs, start=True, stop=True).then_inc(cs_mm, 1)
            pe.wait_ge(dt_a, 6)
            with pe.Fori(0, 2) as i:
                for t in range(8):
                    gemm(pe, t + 1, a_hi, a_lo, i, 8)
                    pe.wait_ge(act_ready, t + 1 + i * 8)
                    pe.wait_ge(xtr2_evac, t + 1 + i * 8)
                    for c in range(NCH):
                        last = nc.tensor.transpose(aux[:, t % 2, c * P:(c + 1) * P], abuf[t % 2][:, c * P:(c + 1) * P], ident[:])
                    last.then_inc(xtr2_done, 1)
            for t in range(17, 24):
                gemm(pe, t, a_hi, a_lo)
                m = t - 17
                if m == 0:
                    pe.wait_ge(xtr2_evac, 18)
                    pe.wait_ge(old_in, 32)
                if m < 5:
                    bank = aux[:, 2 * (m % 2), :]
                    pe.wait_ge(old_ev, max(1, m))
                    if m < 2:
                        for j in range(4):
                            last = nc.tensor.transpose(bank[:, j * 120:(j + 1) * 120], pool_rows[:, (4 * m + j) * P:(4 * m + j + 1) * P],
                                                       ident[0:120, 0:120])
                    elif m < 4:
                        for j in range(12):
                            f = 12 * m - 24 + j
                            last = nc.tensor.transpose(bank[:, j * 24:(j + 1) * 24], conv_rows[:, f * P:(f + 1) * P], ident[0:24, 0:24])
                    else:
                        for j in range(16):
                            last = nc.tensor.matmul(bank[:, j * 17:(j + 1) * 17], spread[:, j, :], hs_rhs[:], start=True, stop=True)
                    last.then_inc(old_tr, 1)
                n = {0: 0, 1: 1, 2: 2, 3: 3, 5: 4, 6: 5}.get(m)
                if n is not None:
                    pe.wait_ge(conv_done, 4 * n + 4)
                    if n >= 2:
                        pe.wait_ge(edge_ev, n - 1)
                    for j in range(4):
                        last = nc.tensor.transpose(aux[0:EDGE, 1 + 2 * (n % 2), j * P:(j + 1) * P], xedge[:, 4 * n + j, :], ident[:])
                    last.then_inc(edge_tr, 1)
            pe.wait_ge(old_ev, 6)
            pe.wait_ge(edge_ev, 6)
            pe.wait_ge(bc_ready, 8)

            def rows_of_cs(c, gr, j0):
                nc.tensor.matmul(aux[:, 0, :], identb[:], maskneg[:].unsqueeze(1).to_broadcast([P, 4, P]), start=True, stop=False)
                for j in range(4):
                    h = gr * HPG + j0 + j
                    last = nc.tensor.matmul(aux[:, 0, j * P:(j + 1) * P], dtk[:, 1, c, h:h + 1].to_broadcast([P, P]),
                                            triu[:], start=False, stop=(j == 3))
                return last

            def step_a(c, gr):
                ch = slice(c * P, (c + 1) * P)
                nc.tensor.matmul(aux[:, 1, 0:P], bc[:, gr, ch], bc[:, GROUPS + gr, ch], start=True, stop=True)
                nc.tensor.transpose(aux[:, 3, 0:P], bc[:, gr, ch], ident[:])
                rows_of_cs(c, gr, 0).then_inc(cb_ready, 1)

            def step_b(c, gr, s):
                pe.wait_ge(exp_a, s)
                pe.wait_ge(x_prep, s)
                rows_of_cs(c, gr, 4)
                nc.tensor.matmul(aux[:, 2, :], bc[:, GROUPS + gr, c * P:(c + 1) * P], state[:, gr, :], start=True, stop=True)
                nc.tensor.matmul(aux[:, 3, :], b_tok[:], xdd[:], start=True, stop=True).then_inc(off_ready, 1)

            def step_c(s):
                pe.wait_ge(m_ready, s)
                for j in range(HPG):
                    last = nc.tensor.matmul(aux[:, 2, j * HD:(j + 1) * HD], decay[:, j, :], xdt[:, j * HD:(j + 1) * HD],
                                            start=(j == 0), stop=(j == HPG - 1), skip_group_check=True)
                last.then_inc(y_mm, 1)

            for c in range(NCH):
                for gr in range(GROUPS):
                    s = GROUPS * c + gr + 1
                    step_a(c, gr)
                    if c < 2:
                        gemm(pe, T_Z + 8 * c + 2 * gr, a_hi, a_lo)
                        step_b(c, gr, s)
                        gemm(pe, T_Z + 8 * c + 2 * gr + 1, a_hi, a_lo)
                    else:
                        gemm(pe, T_PU + 4 * (c - 2) + gr, a_hi, a_lo, kts=range(0, 4))
                        step_b(c, gr, s)
                        gemm(pe, T_PU + 4 * (c - 2) + gr, a_hi, a_lo, kts=range(4, 8))
                    step_c(s)

            pe.wait_ge(y_ready, 16)
            for n in range(4):
                for j in range(4):
                    last = nc.tensor.transpose(aux[:, n, j * P:(j + 1) * P], state[:, n, j * P:(j + 1) * P], ident[:])
                last.then_inc(end_tr, 1)
            pe.wait_ge(smp_v, 2)
            pe.wait_ge(end_ev, 2)
            for j in range(8):
                last = nc.tensor.transpose(aux[0:NS, j // 4, j % 4 * P:(j % 4 + 1) * P], acts_s[:, 16 + j, :], ident[:])
            last.then_inc(end_tr, 1)
            pe.wait_ge(evacuated[0], uses(T_GA) + 1)
            pe.wait_ge(evacuated[1], uses(T_GA) + 1)
            for n in range(2):
                pe.wait_ge(end_ev, n + 3)
                for j in range(4):
                    last = nc.tensor.transpose(aux[0:PEDGE, 2 + n, j * P:(j + 1) * P], pu[:, 4 * n + j, SEQ - PBUF:TT], ident[:])
                last.then_inc(end_tr, 1)
            pe.wait_ge(end_ev, 5)

            def spread_bc(b):
                if b >= 1:
                    pe.wait_ge(bc_used, 2 * b)
                for j in range(2):
                    last = nc.tensor.matmul(aux[:, j, :], ident[0:NS, b:b + 1].to_broadcast([NS, P]),
                                            bc_s[:, j * 512:(j + 1) * 512], start=True, stop=True)
                last.then_inc(bc_mm, 1)

            for k in range(8):
                if k % 2 == 0:
                    spread_bc(k // 2)
                gemm(pe, T_GA + k, a_hi, a_lo)
                for f in (2 * k, 2 * k + 1):
                    if f < 2:
                        pe.wait_ge(end_ev, 6 + f)
                    else:
                        pe.wait_ge(yt_ev, f - 1)
                    for c in range(NCH):
                        last = nc.tensor.transpose(aux[:, 2 + f % 2, c * P:(c + 1) * P], xs_tok[:, c, f * P:(f + 1) * P], ident[:])
                    last.then_inc(yt_mm, 1)

            def y_sums(k):
                for f in (2 * k, 2 * k + 1):
                    if f < 2:
                        pe.wait_ge(yt_ev, 16)
                    elif f % 4 == 0 and f >= 8:
                        pe.wait_ge(std_ready, f // 4)
                    pe.wait_ge(sq_ready, 8 + f + 1)
                    nc.tensor.matmul(aux[:, 2 + f // 4 % 2, :], ones[:], ysq[f % 2][:], start=(f % 4 == 0),
                                     stop=(f % 4 == 3)).then_inc(sq_used, 1)

            for k in range(8):
                if k % 2 == 0:
                    spread_bc(4 + k // 2)
                gemm(pe, T_GB + k, a_hi, a_lo)
                if k >= 1:
                    y_sums(k - 1)
            y_sums(7)
            pe.wait_ge(bc_used, 16)
            for n in range(8):
                m, gi = n // 4, n % 4
                t = T_POOL + m
                if gi == 0:
                    pe.wait_ge(lo_ready, t + 1)
                if n == 1:
                    pe.wait_ge(std_ready, 5)
                if n == 2:
                    pe.wait_ge(ys_sq, 1)
                    pe.wait_ge(evacuated[0], uses(T_POOL) + 1)
                    nc.tensor.matmul(slot[0][:, 0, 0:P], ones[:], y_sq[:].rearrange("p k b -> p (k b)"), start=True,
                                     stop=True).then_inc(ys_mm, 1)
                if n >= 2:
                    pe.wait_ge(pool_ev, n - 1)
                for kk in range(2):
                    k = 2 * gi + kk
                    if m == 0:
                        pe.wait_ge(pool_lo, k + 1)
                    for q, (w, u) in enumerate(((w_hi, a_hi), (w_hi, a_lo), (w_lo, a_hi))):
                        for h in range(2):
                            last = nc.tensor.matmul(aux[:, 2 * (n % 2) + h, 0:HALF], w[:, m, k, :], u[:, k, h * HALF:(h + 1) * HALF],
                                                    start=(kk == 0 and q == 0), stop=(kk == 1 and q == 2))
                last.then_inc(pool_mm, 1)
                if gi == 3:
                    pe.wait_ge(pool_mm, n + 1)
                    pe.sem_inc(gemm_done, 1)
            pe.wait_ge(ys_sum, 1)
            for c4 in range(4):
                for half in range(2):
                    pe.wait_ge(u_ready, 16 + 8 * half)
                    pe.wait_ge(ys_lo, 1 + half)
                    for m in range(2):
                        gemm(pe, T_SSD + 4 * c4 + 2 * half + m, *((b_hi, b_lo) if half == 0 else (a_hi, a_lo)),
                             start=(half == 0), stop=(half == 1))
            def turn_mem(n):
                if n == 0:
                    pe.wait_ge(mem_in, 16)
                if n >= 2:
                    pe.wait_ge(mem_lo_s, n - 1)
                for kk in range(2):
                    for m in range(2):
                        last = nc.tensor.transpose(aux[:, n % 2, kk * MEM + m * P:kk * MEM + (m + 1) * P],
                                                   mem_tok[:, m, (2 * n + kk) * P:(2 * n + kk + 1) * P], ident[:])
                last.then_inc(mem_tr, 1)

            def gemm_mem(t):
                pe.wait_ge(lo_ready, t + 1)
                pe.wait_ge(evacuated[t % 2], uses(t) + 1)
                for kk in range(KT):
                    for q, (w, u) in enumerate(((w_hi, mem_hi), (w_hi, mem_lo), (w_lo, mem_hi))):
                        last = nc.tensor.matmul(slot[t % 2][:, 0, 0:MEM], w[:, t % 2, kk, :], u[:, kk, :],
                                                start=(kk == 0 and q == 0), stop=(kk == KT - 1 and q == 2))
                last.then_inc(gemm_done, 1)

            def turn_kv(bank, src, n):
                for kk in range(2):
                    for m in range(2):
                        last = nc.tensor.transpose(bank[:, (kk * 2 + m) * P:(kk * 2 + m + 1) * P],
                                                   src[:, 2 * n + kk, m * P:(m + 1) * P], ident[:])
                return last

            for k in range(8):
                gemm(pe, T_O + k, c_hi, c_lo, ktwait=(lambda kk: pe.wait_ge(mgl_ready, kk + 1)) if k == 0 else None)
                if k >= 1:
                    norm_tile(24, k - 1, k == 1, False)
                if 3 <= k < 7:
                    turn_mem(k - 3)
            norm_tile(24, 7, False, True)
            pe.wait_ge(mem_lo_s, 4)
            for k in range(8):
                gemm_mem(T_K + k)
            for k in range(8):
                gemm(pe, T_Q + k, a_hi, a_lo, ktwait=(lambda kk: pe.wait_ge(u_ready, 24 + kk + 1)) if k == 0 else None)
                if k % 2 == 1:
                    n = k // 2
                    if n == 0:
                        pe.wait_ge(evacuated[0], uses(T_Q) + 1)
                        pe.wait_ge(evacuated[1], uses(T_Q) + 1)
                    if n >= 2:
                        pe.wait_ge(kt_ev, n - 1)
                    turn_kv(aux[:, n % 2, :], kT, n).then_inc(kt_mm, 1)

            def turn_v(n):
                pe.wait_ge(evacuated[0], uses(T_V) + n + 2)
                pe.wait_ge(evacuated[1], uses(T_V) + n + 2)
                if n >= 2:
                    pe.wait_ge(vt_ev, n - 1)
                turn_kv(slot[n % 2][:, 1, :], vT, n).then_inc(vt_mm, 1)

            for k in range(8):
                gemm_mem(T_V + k)
                if k == 0:
                    pe.wait_ge(evacuated[1], uses(T_V) + 1)
                    pe.wait_ge(kt_ev, 4)
                    for n in range(KT):
                        last = nc.tensor.transpose(aux[0:NS, n // 4, n % 4 * P:(n % 4 + 1) * P], qT[:, n, SEQ:TT], ident[:])
                    last.then_inc(qt_mm, 1)
                    pe.wait_ge(qt_ev, 1)
                if k >= 2:
                    pe.wait_ge(cache_used, k - 1)
                for j in range(2):
                    last = nc.tensor.matmul(q_bank(k)[:, j, :], ident[0:NS, k:k + 1].to_broadcast([NS, P]),
                                            q_tok[:, j * 512:(j + 1) * 512], start=True, stop=True)
                last.then_inc(qb_mm, 1)
                if k >= 2 and k % 2 == 0:
                    turn_v(k // 2 - 1)
            turn_v(3)
            pe.wait_ge(cache_used, NS)
            pe.wait_ge(vt_ev, 4)
            for m in range(2):
                last = nc.tensor.transpose(slot[0][0:32, 1, m * P:(m + 1) * P], s_cols[:, m * 32:(m + 1) * 32], ident[:])
            last.then_inc(sm_a, 1)

            def scores(n):
                h, tq = n // 4, n % 4
                if n >= 2:
                    pe.wait_ge(prob_exp, n - 1)
                for kk in range(2):
                    last = nc.tensor.matmul(aux[:, n % 2, 0:MEM], qT[:, 2 * h + kk, tq * P:(tq + 1) * P], kT[:, 2 * h + kk, :],
                                            start=(kk == 0), stop=(kk == 1))
                last.then_inc(score_mm, 1)

            def turn(n):
                pe.wait_ge(prob_n, n + 1)
                if n >= 2:
                    pe.wait_ge(pt_ev, n - 1)
                for m in range(2):
                    last = nc.tensor.transpose(aux[:, 2 + n % 2, m * P:(m + 1) * P], prob[n % 2][:, m * P:(m + 1) * P], ident[:])
                last.then_inc(pt_mm, 1)

            def values(h):
                pe.wait_ge(pt_ev, 4 * h + 4)
                for dt in range(2):
                    if h >= 1:
                        pe.wait_ge(pv_lo, 2 * h + dt - 1)
                    for m in range(2):
                        last = nc.tensor.matmul(slot[dt][:, 0, :], v_tok[:, m, h * XD + dt * P:h * XD + (dt + 1) * P],
                                                probT[h % 2][:, m, :], start=(m == 0), stop=(m == 1))
                    last.then_inc(pv_mm, 1)

            def values_s(b):
                n = NS + b
                pe.wait_ge(cache_in[n % CR], 16 * (n // CR + 1))
                for h in range(XH):
                    for dt in range(2):
                        for m in range(2):
                            last = nc.tensor.matmul(slot[0][:, 1, (2 * h + dt) * NS + b:(2 * h + dt) * NS + b + 1],
                                                    cache[n % CR][:, m, h * XD + dt * P:h * XD + (dt + 1) * P],
                                                    pT_s[:, m * 32 + b * XH + h:m * 32 + b * XH + h + 1], start=(m == 0), stop=(m == 1))
                last.then_inc(cache_used, 1)

            scores(0)
            pe.wait_ge(sm_d, 1)
            for m in range(2):
                last = nc.tensor.transpose(slot[1][:, 1, m * 32:(m + 1) * 32], prob_s[:, m * P:(m + 1) * P], ident[0:32, 0:32])
            last.then_inc(sm_e, 1)
            pe.wait_ge(sm_f, 1)
            for n in range(16):
                if n + 1 < 16:
                    scores(n + 1)
                if n % 2 == 1:
                    values_s(n // 2)
                turn(n)
                if n % 4 == 3:
                    values(n // 4)
            pe.wait_ge(pv_lo, 8)
            pe.wait_ge(o_s_lo, 1)
            for k in range(8):
                gemm(pe, T_XO + k, a_hi, a_lo)
                if k >= 1:
                    norm_tile(32, k - 1, k == 1, False)
            norm_tile(32, 7, False, True)
            with pe.Fori(0, FF_CHUNKS - 1) as i:
                for k in range(8):
                    gemm(pe, T_MLP + k, a_hi, a_lo, i, 16, ktwait=(lambda kk: pe.wait_ge(u_ready, 32 + kk + 1)) if k == 0 else None)
                for k in range(8):
                    gemm(pe, T_MLP + 8 + k, c_hi, c_lo, i, 16,
                         ktwait=(lambda kk: pe.wait_ge(ff_lo, kk + 1 + i * 8)) if k == 0 else None)
            T_LAST = T_MLP + 16 * (FF_CHUNKS - 1)
            n0 = 8 * (FF_CHUNKS - 1)
            for k in range(8):
                gemm(pe, T_LAST + k, a_hi, a_lo)
            for k in range(8):
                gemm(pe, T_LAST + 8 + k, c_hi, c_lo, ktwait=(lambda kk: pe.wait_ge(ff_lo, n0 + kk + 1)) if k == 0 else None)
                if k >= 1:
                    norm_tile(40, k - 1, k == 1, False)
            norm_tile(40, 7, False, True)
            pe.wait_ge(fin_n, KT)
            for n in range(2):
                for j in range(4):
                    k = 4 * n + j
                    last = nc.tensor.transpose(aux[0:NS, n, j * P:(j + 1) * P], x[:, k, SEQ:TT], ident[:])
                last.then_inc(fin_mm, 1)
            for n in range(8):
                if n < 2 or n >= 4:
                    pe.wait_ge(fin_ev, n + 1 if n < 2 else n - 1)
                for j in range(4):
                    k = n % 2 * 4 + j
                    last = nc.tensor.transpose(aux[:, n % 4, j * P:(j + 1) * P], x[:, k, n // 2 * P:(n // 2 + 1) * P], ident[:])
                last.then_inc(fin_mm, 1)


_INS = ["x_prompt", "x_sample", "mem_prompt", "state_ssm", "state_conv", "state_pool", "cache_mem_k", "cache_mem_v",
        "norm_mix", "w_in", "conv_w", "conv_b", "dt_bias", "a_log", "d_skip", "ssd_norm", "w_ssd_proj", "pool_w",
        "pool_scale", "w_o", "norm_x", "w_xq", "w_xk", "w_xv", "w_xo", "norm_mlp", "w_up", "w_down", "norm_final"]
_OUTS = [("y_prompt", (1, SEQ, D)), ("y_sample", (NS, 1, D)),
         ("ssm_prompt", (1, 1, HEADS, HD, N_STATE)), ("conv_prompt", (1, 1, 3, CONV_DIM)), ("pool_prompt", (1, 1, PBUF, D)),
         ("memk_prompt", (1, 1, MEM, XH, XD)), ("memv_prompt", (1, 1, MEM, XH, XD)),
         ("ssm_sample", (1, NS, HEADS, HD, N_STATE)), ("conv_sample", (1, NS, 3, CONV_DIM)), ("pool_sample", (1, NS, PBUF, D))]


def kernel(**inputs):
    import numpy as _np
    import concourse.bacc as _bacc
    from concourse.bass_utils import run_bass_kernel_spmd as _run

    nc = _bacc.Bacc("TRN2", target_bir_lowering=False, num_devices=1)
    arrays, ins, outs = {}, {}, {}
    for name in _INS:
        v = _np.ascontiguousarray(inputs[name])
        arrays[f"in_{name}"] = v
        ins[name] = nc.dram_tensor(f"in_{name}", v.shape, F32, kind="ExternalInput").ap()
    for name, shape in _OUTS:
        outs[name] = nc.dram_tensor(f"out_{name}", shape, F32, kind="ExternalOutput").ap()
    build(nc, ins, outs)
    r = _run(nc, [arrays], core_ids=[0])
    return tuple(r.results[0][f"out_{name}"] for name, _ in _OUTS)
```

```python
from contextlib import ExitStack

import concourse.bass as bass
from concourse import mybir

P = 128
D = 1024
KT = D // P
SEQ = 512
NS = 8
TT = SEQ + NS
HALF = TT // 2
NCH = SEQ // P
HEADS, HD, N_STATE, GROUPS = 32, 64, 128, 4
HPG = HEADS // GROUPS
GW = HPG * HD
D_INNER = HEADS * HD
CONV_DIM = D_INNER + 2 * GROUPS * N_STATE
CT = CONV_DIM // P
XT_TILES = D_INNER // P
TAPS = 4
EDGE = TAPS - 1 + NS
OFF_XBC, OFF_DT = D_INNER, D_INNER + CONV_DIM
OFF_POOL = OFF_DT + HEADS
OFF_GA, OFF_GB = OFF_POOL + D, OFF_POOL + 2 * D
IN_DIM = OFF_GB + D
PBUF = 15
PEDGE = PBUF + NS
WINDOWS = (2, 4, 8, 16)
MEM = 256
XH, XD = 4, 256
D_FF = 4 * D
EPS = 1e-6
CR = 5
SR = 4
UW = 256
NEG = -1.0e30

F32 = mybir.dt.float32
R32 = mybir.dt.float32r
BF16 = mybir.dt.bfloat16
ALU = mybir.AluOpType
ACT = mybir.ActivationFunctionType
AX = mybir.AxisListType

T_XBC = 0
T_Z = T_XBC + CT
T_PU = T_Z + 16
T_GA = T_PU + 8
T_GB = T_GA + 8
T_POOL = T_GB + 8
T_SSD = T_POOL + 2
T_O = T_SSD + 16
T_K = T_O + 8
T_Q = T_K + 8
T_V = T_Q + 8
T_XO = T_V + 8
T_MLP = T_XO + 8
FF_CHUNKS = D_FF // D
T_END = T_MLP + 16 * FF_CHUNKS


class Chain:

    def __init__(self, eng, sem):
        self.eng, self.sem, self.n, self.extra = eng, sem, 0, 0

    def __call__(self, ins):
        self.n += 1
        ins.then_inc(self.sem, 1)
        self.eng.wait_ge(self.sem, self.n + self.extra)

    def loop(self, i, per):
        self.start, self.per, self.extra = self.n, per, i * per

    def end(self, times):
        assert self.n - self.start == self.per, (self.n - self.start, self.per)
        self.n, self.extra = self.start + self.per * times, 0


def build(nc, a, o):
    win = a["w_in"][0].rearrange("(k p) m -> p k m", p=P)
    x_dram = nc.dram_tensor("residual_spill", (P, KT * TT), F32, kind="Internal").ap()

    with ExitStack() as ctx:
        base = (nc.sbuf_base + 63) // 32 * 32
        R_RING = base
        R_A = R_RING + 32768
        R_1 = R_A + 2 * KT * TT * 4
        R_2 = R_1 + 2 * KT * TT * 4
        R_3 = R_2 + 2 * KT * TT * 4
        R_4 = R_3 + KT * TT * 4
        R_4N = R_4 + 2 * KT * TT * 4
        R_5 = R_4N + 18720

        def at(name, shape, off, dt=F32):
            return nc.alloc_sbuf_tensor_at(name, shape, dt, offset=off)

        cur = [R_5 // 32 * 32]

        def const(name, shape, dt=F32):
            n = 1
            for d in shape[1:]:
                n *= d
            n *= 2 if dt == BF16 else 4
            t = at(name, shape, cur[0], dt)
            cur[0] += (n + 31) // 32 * 32
            return t

        w_raw = at("w_raw", [P, 2, KT, UW], R_RING)
        w_hi = at("w_hi", [P, 2, KT, P], R_RING + 16384, R32)
        w_lo = at("w_lo", [P, 2, KT, P], R_RING + 24576, R32)
        SZ = KT * TT * 4
        a_hi, a_lo = (at(n, [P, KT, TT], R_A + k * SZ, R32) for k, n in enumerate(("a_hi", "a_lo")))
        x0 = at("x0", [P, KT, TT], R_1)
        zs = at("zs", [P, 16, TT], R_1)
        c_hi, c_lo = (at(n, [P, KT, TT], R_1 + k * SZ, R32) for k, n in enumerate(("c_hi", "c_lo")))
        x_tok = at("x_tok", [P, NCH, D], R_2)
        xs_tok = at("xs_tok", [P, NCH, D_INNER], R_2)
        b_hi, b_lo = (at(n, [P, KT, TT], R_2 + k * SZ, R32) for k, n in enumerate(("b_hi", "b_lo")))
        qT = at("qT", [P, KT, TT], R_2)
        v_tok = at("v_tok", [P, 2, D], R_2 + SZ)
        kT = at("kT", [P, KT, MEM], R_2 + SZ + 8192)
        pu = at("pu", [P, KT, TT], R_3)
        x = at("x", [P, KT, TT], R_3)
        bc = at("bc", [P, 8, TT], R_4)
        gate_a = at("gate_a", [P, KT, TT], R_4)
        conv_rows = at("conv_rows", [NS * 3, CONV_DIM], R_1)
        pool_rows = at("pool_rows", [NS * PBUF, D], R_1 + 12288)
        spread = at("spread", [HEADS, 16, P], R_1 + 16384)
        mem_hi = at("mem_hi", [P, KT, MEM], R_4, R32)
        mem_lo = at("mem_lo", [P, KT, MEM], R_4 + 8192, R32)
        y_tok = at("y_tok", [P, NCH, D], R_4)
        gain_row = at("gain_row", [P, D], R_4 + SZ + 8192)
        g = R_4 + SZ
        cbuf = [at(f"cbuf{k}", [P, TAPS - 1 + TT], g + 2112 * k) for k in range(2)]
        hbuf = [at(f"hbuf{k}", [P, SEQ], g + 4224 + 2048 * k) for k in range(2)]
        tbuf = at("tbuf", [P, SEQ], g + 8320)
        abuf = [at(f"abuf{k}", [P, SEQ], g + 10368 + 2048 * k) for k in range(2)]
        decay = at("decay", [P, HPG, P], g)
        xdt = at("xdt", [P, GW], g + 4096)
        xdd = at("xdd", [P, GW], g + 6144)
        xskip = at("xskip", [P, GW], g + 8192)
        yacc = at("yacc", [P, GW], g + 10240)
        b_tok = at("b_tok", [P, N_STATE], g + 12288)
        cbm = at("cbm", [P, P], g + 12800)
        gate_b = at("gate_b", [P, KT, TT], g)
        state_out = at("state_out", [P, 16, N_STATE], g)
        pool_edge = at("pool_edge", [PEDGE, D], g + 8192)
        bc_s = at("bc_s", [2 * NS, 8 * N_STATE], g + 12544, R32)
        cs_rows = at("cs_rows", [64, 4 * P], g + 13824, R32)
        cs_split = at("cs_split", [P, 4, 2, 32], R_1 + 28416)
        bc_cols = at("bc_cols", [P, 8, 2 * NS], g + 13312)
        mem_tok = at("mem_tok", [P, 2, D], g)
        k_tok = at("k_tok", [P, 2, D], g + 8192)
        ys_tok = at("ys_tok", [NS, D], g)
        vT = at("vT", [P, KT, MEM], R_4N)
        cache = [at(f"cache{k}", [P, 2, D], R_1 + 8192 * k if k < 4 else g) for k in range(CR)]
        sq = [at(f"sq{k}", [P, TT], R_4N + 2080 * k) for k in range(2)]
        ut = [at(f"ut{k}", [P, TT], R_4N + 4160 + 2080 * k) for k in range(2)]
        std = at("std", [P, TT], R_4N + 8320)
        rstd = at("rstd", [P, TT], R_4N + 10400)
        sq_sum = at("sq_sum", [P, TT], R_4N + 12480)
        state = at("state", [P, GROUPS, GW], R_4N)
        tz = [at(f"tz{k}", [P, TT], R_4N + 8192 + 2080 * k) for k in range(2)]
        conv_edge = at("conv_edge", [EDGE, CONV_DIM], R_3 + 3072)
        sring = [at(f"sring{k}", [P, 8, N_STATE], R_4N + 4096 * k) for k in range(SR)]
        sp_cols = at("sp_cols", [P, KT, NS * PBUF], R_4N + 12480)
        ysq_buf = [at(f"ysq{k}", [P, SEQ], R_2 + 2048 * k) for k in range(4)]
        ysq_first = [at(f"ysq_first{k}", [P, SEQ], g + 4160 + 2048 * k) for k in range(2)]
        ysq = [ysq_first if q == 0 else ysq_buf[q % 2 * 2:q % 2 * 2 + 2] for q in range(8)]
        y_tok_sum = at("y_tok_sum", [P, GROUPS, NCH], R_4N + 18432)
        y_tok_std = at("y_tok_std", [P, GROUPS, NCH], R_4N + 18496)
        y_tok_inv = at("y_tok_inv", [P, GROUPS, NCH], R_4N + 18560)
        diag_junk = at("diag_junk", [P, GROUPS, NCH, P], R_2 + 12288, BF16)
        win_sum = [at(f"win_sum{k}", [P, SEQ], R_2 + 8192 + 2048 * k) for k in range(2)]
        win_sum_a = [at(f"win_sum_a{k}", [P, SEQ], g + 2048 * k) for k in range(2)]
        st_cols = at("st_cols", [P, CT, NS * 3], R_4N + 16384)
        junk_s = at("junk_s", [P, 8, N_STATE], R_4N + 16384, BF16)
        prob = [at(f"prob{k}", [P, MEM], R_4N + 1024 * k) for k in range(2)]
        probT = [at(f"probT{k}", [P, 2, SEQ], R_4N + 2048 + 4096 * k) for k in range(2)]
        q_tok = at("q_tok", [2 * NS, D], R_4N + 12288, R32)
        q_cols = at("q_cols", [P, KT, 2 * NS], R_4N + 17408)
        junk = at("junk", [P, 2, XH, XD], R_4N + 8192, BF16)
        prob_s = at("prob_s", [32, MEM], R_4N + 15360)
        s_cols = at("s_cols", [P, 64], R_4N + 16384)
        stats = at("stats", [P, 80], R_4N + 16896)
        p_diag = at("p_diag", [P, 2, NS, XH, NS], R_4 + 8192)
        o_tok = at("o_tok", [NS, D], R_4 + 10240)
        fin_junk = at("fin_junk", [P, 8, 512], R_4N, BF16)
        fin_junk_s = at("fin_junk_s", [NS, 2, 512], R_4N + 8192, BF16)
        rt = [at(f"rt{k}", [P, TT], R_4N + 2080 * k) for k in range(2)]
        dtw = at("dtw", [P, KT, HEADS], R_3)
        dtw_hi = at("dtw_hi", [P, KT, HEADS], R_3 + 1024, R32)
        dtw_lo = at("dtw_lo", [P, KT, HEADS], R_3 + 2048, R32)
        dt_raw = at("dt_raw", [HEADS, TT], R_3)
        dt_tmp = [at(f"dt_tmp{k}", [P, NCH + 1, HEADS], R_1 + 24576 + 640 * k) for k in range(6)]
        x_junk = [at(f"x_junk{k}", [P, D], R_4N + 2048 * k, BF16) for k in range(NCH + 1)]
        tok_sum = at("tok_sum", [P, NCH + 1], R_4N + 17408)
        tok_std = at("tok_std", [P, NCH + 1], R_4N + 17440)
        tok_inv = at("tok_inv", [P, NCH + 1], R_4N + 17472)
        xs_row = at("xs_row", [NS, D], R_4)
        vr1 = at("vr1", [56, P], R_4 + 4096)
        vr2 = at("vr2", [120, P], R_4 + 4608)

        ident = const("ident", [P, P])
        identb = const("identb", [P, P], BF16)
        triu = const("triu", [P, P])
        ones = const("ones", [P, P])
        maskneg = const("maskneg", [P, P], BF16)
        cols = const("cols", [P, 176])
        CN_MIX, CN_X, CN_MLP, C_PS, C_SSD, C_CW, C_CB = 0, 8, 16, 32, 40, 56, 152
        dtk = const("dtk", [P, 2, NCH + 1, HEADS])
        a_row = const("a_row", [P, HEADS])
        ncs = const("ncs", [P, NCH, HEADS])
        ecs = const("ecs", [P, NCH, HEADS])
        cdec = const("cdec", [P, NCH, HEADS])
        dtd = const("dtd", [P, NCH, HEADS])
        dskip = const("dskip", [P, HEADS])
        rcount = const("rcount", [P, 16])
        xedge = const("xedge", [P, CT, EDGE])
        hcol = const("hcol", [HEADS, 1])
        hs_rhs = const("hs_rhs", [HEADS, 17])
        acts_s = const("acts_s", [P, CT, NS])
        exp_s = const("exp_s", [P, 16, 17])
        xdt_s = const("xdt_s", [P, 16, NS])
        y_s = const("y_s", [P, 16, NS])
        pick_step = const("pick_step", [64, 32], R32)
        pick = const("pick", [2 * NS, NS], R32)
        eps_col = const("eps_col", [P, 1])
        tmp_s = const("tmp_s", [P, CT, NS])
        y_sq = xdt_s
        y_std = const("y_std", [P, GROUPS, NS])
        assert cur[0] <= nc.sbuf_usable_end, (cur[0], nc.sbuf_usable_end)

        slot = [ctx.enter_context(nc.psum_tensor(f"slot{k}", [P, 2, 512], F32)) for k in range(2)]
        aux = ctx.enter_context(nc.psum_tensor("aux", [P, 4, 512], F32))

        names = {}

        def sem(name):
            names[name] = ctx.enter_context(nc.semaphore(name))
            return names[name]

        raw_landed = [sem(f"raw_landed{k}") for k in range(2)]
        hi_ready, lo_ready, gemm_done = sem("hi_ready"), sem("lo_ready"), sem("gemm_done")
        evacuated = [sem(f"evacuated{k}") for k in range(2)]
        v_step, a_step, p_step = sem("v_step"), sem("a_step"), sem("p_step")
        x_in = [sem(f"x_in{c}") for c in range(NCH)]
        consts, s_in, vec_in, small_in = (sem(n) for n in ("consts", "s_in", "vec_in", "small_in"))
        xtr_done, xtr_evac, xtr_evac_a = sem("xtr_done"), sem("xtr_evac"), sem("xtr_evac_a")
        tok_a, tok_v, tok_mm = sem("tok_a"), sem("tok_v"), sem("tok_mm")
        sq_ready, sq_used, std_ready = (sem(n) for n in ("sq_ready", "sq_used", "std_ready"))
        ut_ready, uh_ready, u_ready = sem("ut_ready"), sem("uh_ready"), sem("u_ready")
        spilled, reloaded = sem("spilled"), sem("reloaded")
        dtw_hi_s, dtw_lo_s, dt_mm, dt_evac = (sem(n) for n in ("dtw_hi_s", "dtw_lo_s", "dt_mm", "dt_evac"))
        dt_a, dt_b, dt_tr, cs_mm, cs_v = (sem(n) for n in ("dt_a", "dt_b", "dt_tr", "cs_mm", "cs_v"))
        conv_done, tanh_done, act_ready = sem("conv_done"), sem("tanh_done"), sem("act_ready")
        xtr2_done, xtr2_evac = sem("xs_turned"), sem("xs_stored")
        bc_ready = sem("bc_ready")
        cb_ready, exp_a, exp_b, x_prep, m_ready = (sem(n) for n in ("cb_ready", "exp_a", "exp_b", "x_prep", "m_ready"))
        off_ready, y_mm, skip_ready, y_ready, tz_ready = (sem(n) for n in ("off_ready", "y_mm", "skip_ready", "y_ready", "tz_ready"))
        old_in, old_tr, old_ev = sem("old_in"), sem("old_tr"), sem("old_ev")
        edge_tr, edge_ev, end_tr, end_ev = (sem(n) for n in ("edge_tr", "edge_ev", "end_tr", "end_ev"))
        out_ssm, out_edge, out_pool, out_kv, out_y = (sem(n) for n in ("out_ssm", "out_edge", "out_pool", "out_kv", "out_y"))
        smp_a, smp_v = sem("smp_a"), sem("smp_v")
        st_in = [sem(f"st_in{k}") for k in range(SR)]
        st_out = [sem(f"st_out{k}") for k in range(SR)]
        st_dec, st_new, bc_mm, bc_used = sem("st_dec"), sem("st_new"), sem("bc_mm"), sem("bc_used")
        ysum_mm, diag_done, y_rms, y_inv, y_row = (sem(n) for n in ("ysum_mm", "diag_done", "y_rms", "y_inv", "y_row"))
        pool_lo_p, sq_added = sem("pool_lo_p"), sem("sq_added")
        ys_ready, ys_sq, ys_mm, ys_sum, ys_std, ys_n, ys_hi, ys_lo = (
            sem(n) for n in ("ys_ready", "ys_sq", "ys_mm", "ys_sum", "ys_std", "ys_n", "ys_hi", "ys_lo"))
        pool_sum, pool_sum_s, pool_hi, pool_lo, pool_mm, pool_ev = (sem(n) for n in ("pool_sum", "pool_sum_s", "pool_hi", "pool_lo", "pool_mm", "pool_ev"))
        yt_mm, yt_ev = sem("yt_mm"), sem("yt_ev")
        mg_ready, mgh_ready, mgl_ready = sem("mg_ready"), sem("mgh_ready"), sem("mgl_ready")
        mem_in, mem_tr, mem_hi_s, mem_lo_s = (sem(n) for n in ("mem_in", "mem_tr", "mem_hi_s", "mem_lo_s"))
        kt_mm, kt_ev, vt_mm, vt_ev = sem("kt_mm"), sem("kt_ev"), sem("vt_mm"), sem("vt_ev")
        cache_in = [sem(f"cache_in{k}") for k in range(CR)]
        cache_used = sem("cache_used")
        q_split, qt_mm, qt_ev, qb_mm = (sem(n) for n in ("q_split", "qt_mm", "qt_ev", "qb_mm"))
        sm_a, sm_b, sm_c, sm_d, sm_e, sm_f = (sem(f"sm_{n}") for n in "abcdef")
        score_mm, negmax, prob_exp, prob_n, pt_mm, pt_ev, pv_mm, pv_hi, pv_lo = (
            sem(n) for n in ("score_mm", "negmax", "prob_exp", "prob_n", "pt_mm", "pt_ev", "pv_mm", "pv_hi", "pv_lo"))
        p_zero, o_s_row, o_s_tr, o_s_hi, o_s_lo = (sem(n) for n in ("p_zero", "o_s_row", "o_s_tr", "o_s_hi", "o_s_lo"))
        ff_sq, ff_hi, ff_lo = (sem(n) for n in ("ff_sq", "ff_hi", "ff_lo"))
        gain_in, fin_mm, fin_copy, fin_sq, fin_sum, fin_std, fin_ev = (
            sem(n) for n in ("gain_in", "fin_mm", "fin_copy", "fin_sq", "fin_sum", "fin_std", "fin_ev"))

        D_ORDER = (0, 1, 4, 2, 5, 3, 6, 7)

        block = ctx.enter_context(nc.Block())

        def halves(t):
            return t.rearrange("p (h n) -> p h n", h=2)

        def in_slot(k):
            return slot[k][:, :, 0:HALF]

        def pool_bank(n):
            return aux[:, 0:2, 0:HALF] if n % 2 == 0 else in_slot(1)

        def pv_bank(h, dt):
            return aux[:, dt, :] if h == XH - 1 else slot[dt][:, 0, :]

        def q_bank(b):
            return aux[:, 2:4, :] if b % 2 else aux[:, 0:2, :]

        def uses(t):
            if t <= T_POOL:
                return t // 2
            if t < T_O:
                return T_POOL // 2 + (t - T_SSD) // 4
            return T_POOL // 2 + 4 + (t - T_O) // 2

        def load_unit(sp, u, src, i=0, step=0):
            if u >= 2:
                sp.wait_ge(lo_ready, 2 * u - 2 + i * step)
            sp.dma_start(w_raw[:, u % 2], src).then_inc(raw_landed[u % 2], 16)

        def split_hi(act, t, i=0, step=0):
            if t >= T_END:
                return
            if t % 2 == 0:
                act.wait_ge(raw_landed[t // 2 % 2], 16 * (t // 4 + 1) + i * (4 * step))
            if t >= 2:
                act.wait_ge(gemm_done, t - 1 + i * step)
            nc.scalar.activation(w_hi[:, t % 2], w_raw[:, t // 2 % 2, :, t % 2 * P:t % 2 * P + P],
                                 ACT.Copy).then_inc(hi_ready, 1)

        def split_lo(dve, t, i=0, step=0):
            if t >= T_END:
                return
            dve.wait_ge(hi_ready, t + 1 + i * step)
            nc.vector.tensor_tensor(w_lo[:, t % 2], w_raw[:, t // 2 % 2, :, t % 2 * P:t % 2 * P + P],
                                    w_hi[:, t % 2].bitcast(F32), ALU.subtract).then_inc(lo_ready, 1)

        def gemm(pe, t, hi, lo, i=0, step=0, kts=range(KT), ktwait=None, start=True, stop=True):
            k0 = kts[0] == 0
            if k0:
                pe.wait_ge(lo_ready, t + 1 + i * step)
                if start:
                    pe.wait_ge(evacuated[t % 2], uses(t) + 1 + i * (step // 2))
            for k in kts:
                if ktwait is not None:
                    ktwait(k)
                for n, (w, act) in enumerate(((w_hi, hi), (w_hi, lo), (w_lo, hi))):
                    for h in range(2):
                        last = nc.tensor.matmul(slot[t % 2][:, h, 0:HALF], w[:, t % 2, k, :],
                                                act[:, k, h * HALF:(h + 1) * HALF],
                                                start=(start and k == 0 and n == 0),
                                                stop=(stop and k == KT - 1 and n == 2))
            if kts[-1] == KT - 1:
                last.then_inc(gemm_done, 1)

        def unit_src(name, cb, row=0):
            return a[name][0][row:row + D].rearrange("(k p) m -> p k m", p=P)[:, :, cb * UW:(cb + 1) * UW]

        @block.sync
        def _(sp):
            for c in range(NCH):
                sp.dma_start(x_tok[:, c, :], a["x_prompt"][0, c * P:(c + 1) * P, :]).then_inc(x_in[c], 16)
            for n, name in enumerate(("norm_mix", "norm_x", "norm_mlp", "norm_final", "pool_scale")):
                src = a[name] if name == "norm_final" else a[name][0]
                sp.dma_start(vr1[8 * n:8 * n + 8, :], src.rearrange("(k p) -> k p", p=P)).then_inc(vec_in, 16)
            sp.dma_start(vr1[40:56, :], a["ssd_norm"][0].rearrange("(k p) -> k p", p=P)).then_inc(vec_in, 16)
            sp.dma_start(vr2[0:96, :], a["conv_w"][0].rearrange("w (k p) -> (w k) p", p=P)).then_inc(vec_in, 16)
            sp.dma_start(vr2[96:120, :], a["conv_b"][0].rearrange("(k p) -> k p", p=P)).then_inc(vec_in, 16)
            for u in range(4):
                load_unit(sp, u, win[:, :, OFF_XBC + u * UW:OFF_XBC + (u + 1) * UW])
            with sp.Fori(0, 2) as i:
                for u in range(4):
                    load_unit(sp, 4 + u, win[:, :, bass.ds(OFF_XBC + D + u * UW + i * D, UW)], i, 8)
            with sp.Fori(0, 2) as i:
                for u in range(4):
                    load_unit(sp, T_Z // 2 + u, win[:, :, bass.ds(u * UW + i * D, UW)], i, 8)
            for u in range(4):
                load_unit(sp, T_PU // 2 + u, win[:, :, OFF_POOL + u * UW:OFF_POOL + (u + 1) * UW])
            s_dram = a["state_ssm"][0].rearrange("b (j t h) p n -> b j (h p) t n", j=2, h=2)

            def load_state(n):
                if n >= SR:
                    sp.wait_ge(st_out[n % SR], 16 * (n // SR))
                    sp.wait_ge(bc_used, n - SR + 1)
                elif n < 2:
                    sp.wait_ge(end_tr, 4)
                elif n == 3:
                    sp.wait_ge(pool_sum_s, 1)
                sp.dma_start(sring[n % SR][:], s_dram[n // 2, n % 2]).then_inc(st_in[n % SR], 16)

            for u in range(8):
                load_unit(sp, T_GA // 2 + u, win[:, :, OFF_GA + u * UW:OFF_GA + (u + 1) * UW])
                if u == 1:
                    for n in (2, 0, 1, 3):
                        load_state(n)
                elif u >= 2:
                    load_state(2 * u)
                    load_state(2 * u + 1)
            load_unit(sp, T_POOL // 2, a["pool_w"][0].rearrange("g (k p) d -> p (g k) d", p=P))
            for u in range(8):
                load_unit(sp, T_SSD // 2 + u, unit_src("w_ssd_proj", u // 2, D * (1 - u % 2)))
            def load_cache(n):
                if n >= CR:
                    sp.wait_ge(cache_used, n - CR + 1)
                elif n == 0:
                    sp.wait_ge(gemm_done, T_O + 8)
                src = a["cache_mem_k" if n < NS else "cache_mem_v"][0, n % NS]
                sp.dma_start(cache[n % CR][:], src.rearrange("(m p) h d -> p m (h d)", p=P)).then_inc(cache_in[n % CR], 16)

            for n, name in enumerate(("w_o", "w_xk", "w_xq", "w_xv", "w_xo")):
                for u in range(4):
                    load_unit(sp, T_O // 2 + 4 * n + u, unit_src(name, u))
                    for c in {("w_xq", 0): (0, 1), ("w_xq", 1): (2, 3), ("w_xq", 2): (4,), ("w_xv", 2): (5, 6), ("w_xv", 3): (7, 8),
                              ("w_xo", 0): (9, 10), ("w_xo", 1): (11, 12, 13, 14, 15)}.get((name, u), ()):
                        load_cache(c)
            up = a["w_up"][0].rearrange("(k p) m -> p k m", p=P)
            down = a["w_down"][0].rearrange("(j k p) m -> p j k m", p=P, k=KT)
            with sp.Fori(0, FF_CHUNKS) as i:
                for u in range(4):
                    load_unit(sp, T_MLP // 2 + u, up[:, :, bass.ds(i * D + u * UW, UW)], i, 16)
                for u in range(4):
                    load_unit(sp, T_MLP // 2 + 4 + u, down[:, i, :, u * UW:(u + 1) * UW], i, 16)
            for c in range(NCH):
                sp.wait_ge(fin_ev, c + 1)
                sp.dma_start(o["y_prompt"][0, c * P:(c + 1) * P, :], y_tok[:, c, :]).then_inc(out_y, 16)

        @block.gpsimd
        def _(pool):
            chain = Chain(pool, p_step)
            nc.gpsimd.memset(ident[:], 0.0)
            nc.gpsimd.memset(identb[:], 0.0)
            nc.gpsimd.memset(ones[:], 1.0)
            nc.gpsimd.memset(triu[:], 1.0)
            nc.gpsimd.memset(maskneg[:], 0.0)
            for k in range(2):
                nc.gpsimd.memset(cbuf[k][:, 0:TAPS - 1], 0.0)
            for j in range(16):
                ins = nc.gpsimd.memset(rcount[:, j:j + 1], 1.0 / (j + 1))
            chain(ins)
            nc.gpsimd.affine_select(out=ident[:], in_=ident[:], compare_op=ALU.not_equal, fill=1.0, base=0,
                                    pattern=[[-1, P]], channel_multiplier=1).then_inc(consts, 1)
            nc.gpsimd.affine_select(out=identb[:], in_=identb[:], compare_op=ALU.not_equal, fill=1.0, base=0,
                                    pattern=[[-1, P]], channel_multiplier=1).then_inc(consts, 1)
            nc.gpsimd.affine_select(out=triu[:], in_=triu[:], compare_op=ALU.is_ge, fill=0.0, base=0,
                                    pattern=[[1, P]], channel_multiplier=-1).then_inc(consts, 1)
            nc.gpsimd.affine_select(out=maskneg[:], in_=maskneg[:], compare_op=ALU.is_ge, fill=NEG, base=0,
                                    pattern=[[1, P]], channel_multiplier=-1).then_inc(consts, 1)
            pool.dma_start(o["conv_sample"][0, :, 0:2, :], a["state_conv"][0, :, 1:3, :]).then_inc(out_edge, 16)
            pool.dma_start(o["pool_sample"][0, :, 0:PBUF - 1, :], a["state_pool"][0, :, 1:PBUF, :]).then_inc(out_pool, 16)
            pool.wait_ge(xtr_evac, 6)
            pool.wait_ge(xtr_evac_a, 4)
            pool.dma_start(x_dram, x0[:].rearrange("p k n -> p (k n)")).then_inc(spilled, 16)
            pool.wait_ge(spilled, 16)
            pool.wait_ge(u_ready, KT)
            pool.dma_start(conv_rows[:], a["state_conv"][0].rearrange("b k c -> (b k) c")).then_inc(old_in, 16)
            pool.dma_start(pool_rows[:], a["state_pool"][0].rearrange("b k c -> (b k) c")).then_inc(old_in, 16)
            nc.gpsimd.memset(state[:], 0.0).then_inc(consts, 1)

            def skip_term(c, gr, s):
                pool.wait_ge(x_prep, s)
                nc.gpsimd.tensor_tensor(
                    xskip[:].rearrange("p (h d) -> p h d", h=HPG),
                    xs_tok[:, c, gr * GW:(gr + 1) * GW].rearrange("p (h d) -> p h d", h=HPG),
                    dskip[:, gr * HPG:(gr + 1) * HPG].unsqueeze(2).to_broadcast([P, HPG, HD]),
                    ALU.mult).then_inc(skip_ready, 1)

            pool.wait_ge(edge_ev, 6)
            pool.dma_start(o["conv_prompt"][0, 0], conv_edge[0:3, :]).then_inc(out_edge, 16)
            pool.dma_start(o["conv_sample"][0, :, 2, :], conv_edge[3:EDGE, :]).then_inc(out_edge, 16)
            pool.wait_ge(old_ev, 6)
            def wcol(k):
                return cols[:, C_CW + CT * k:C_CW + CT * (k + 1)].unsqueeze(2).to_broadcast([P, CT, NS])
            old = st_cols[:].rearrange("p f (b k) -> p f k b", k=3)
            chain(nc.gpsimd.tensor_tensor(tmp_s[:], xedge[:, :, TAPS - 1:EDGE], wcol(3), ALU.mult))
            chain(nc.gpsimd.tensor_tensor(tmp_s[:], tmp_s[:], cols[:, C_CB:C_CB + CT].unsqueeze(2).to_broadcast([P, CT, NS]), ALU.add))
            for k in range(3):
                chain(nc.gpsimd.tensor_tensor(acts_s[:], old[:, :, k, :], wcol(k), ALU.mult))
                ins = nc.gpsimd.tensor_tensor(tmp_s[:], tmp_s[:], acts_s[:], ALU.add)
                if k < 2:
                    chain(ins)
                else:
                    ins.then_inc(smp_v, 1)
            with pool.Fori(0, NCH) as i:
                for gr in range(GROUPS):
                    skip_term(i, gr, 4 * i + gr + 1)

            pool.wait_ge(end_ev, 4)
            pool.dma_start(o["ssm_prompt"][0, 0].rearrange("(t h) p n -> (h p) t n", h=2), state_out[:]).then_inc(out_ssm, 16)

            def decay_state(n):
                b, j = n // 2, n % 2
                pool.wait_ge(st_in[n % SR], 16 * (n // SR + 1))
                nc.gpsimd.tensor_tensor(sring[n % SR][:], sring[n % SR][:],
                                        exp_s[:, 8 * j:8 * j + 8, NS + b:NS + b + 1].to_broadcast([P, 8, N_STATE]),
                                        ALU.mult).then_inc(st_dec, 1)

            decay_state(0)
            pool.wait_ge(end_ev, 7)
            pool.dma_start(o["pool_prompt"][0, 0], pool_edge[0:PBUF, :]).then_inc(out_pool, 16)
            pool.dma_start(o["pool_sample"][0, :, PBUF - 1, :], pool_edge[PBUF:PEDGE, :]).then_inc(out_pool, 16)
            def add_squares(q):
                pool.wait_ge(sq_ready, q + 1)
                pool.sem_inc(sq_used, 1)
                for k in range(1, KT - 1):
                    pool.wait_ge(sq_ready, q + k + 1)
                    if k >= 2:
                        pool.wait_ge(sq_used, q + k)
                    nc.gpsimd.tensor_tensor(sq_sum[:], sq_sum[:], sq[k % 2][:], ALU.add).then_inc(sq_used, 1)

            def windows(k, buffers):
                w = WINDOWS[k // 2]
                if k >= 1:
                    pool.wait_ge(pool_sum, k)
                src, span = pu[:, k, 0:SEQ], 1
                bufs = list(buffers)
                while span < w:
                    dst = bufs[0]
                    nc.gpsimd.tensor_copy(dst[:, 0:span], src[:, 0:span])
                    chain(nc.gpsimd.tensor_tensor(dst[:, span:SEQ], src[:, span:SEQ], src[:, 0:SEQ - span], ALU.add))
                    src, span = dst[:, 0:SEQ], span * 2
                    bufs.reverse()
                dst = bufs[0]
                nc.gpsimd.tensor_scalar(dst[:, w:SEQ], src[:, w:SEQ], 1.0 / w, 1.0, ALU.mult, ALU.mult)
                chain(nc.gpsimd.tensor_tensor(dst[:, 0:w], src[:, 0:w], rcount[:, 0:w], ALU.mult))
                nc.gpsimd.tensor_tensor(pu[:, k, 0:SEQ], dst[:, 0:SEQ], pu[:, k, 0:SEQ], ALU.subtract).then_inc(pool_sum, 1)

            pool.wait_ge(out_ssm, 16)
            for n in range(1, 9):
                decay_state(n)
                if 2 <= n <= 7:
                    windows(n - 2, win_sum_a)
            def add_pair(q):
                pool.wait_ge(sq_ready, 2 * q + 2)
                nc.gpsimd.tensor_tensor(ysq[q][0][:], ysq[q][0][:], ysq[q][1][:], ALU.add).then_inc(sq_added, 1)

            for k in range(8):
                if k < 7:
                    decay_state(9 + k)
                if k == 1:
                    pool.wait_ge(yt_ev, 16)
                if k in (1, 4):
                    windows(6 + k // 4, win_sum)
                add_pair(k)

            for k in range(4, KT):
                pool.wait_ge(pool_hi, D_ORDER.index(k) + 1)
                nc.gpsimd.tensor_tensor(a_lo[:, k, :], pu[:, k, :], a_hi[:, k, :].bitcast(F32), ALU.subtract).then_inc(pool_lo_p, 1)
            pool.wait_ge(pool_ev, 8)
            pool.wait_ge(spilled, 16)
            pool.dma_start(x[:].rearrange("p k n -> p (k n)"), x_dram).then_inc(reloaded, 16)
            pool.wait_ge(mgl_ready, KT)
            pool.dma_start(mem_tok[:], a["mem_prompt"][0].rearrange("(m p) d -> p m d", p=P)).then_inc(mem_in, 16)
            add_squares(16)
            pool.wait_ge(gemm_done, T_XO)
            nc.gpsimd.memset(p_diag[:], 0.0).then_inc(p_zero, 1)
            pool.wait_ge(kt_ev, 4)
            pool.dma_start(o["memk_prompt"][0, 0].rearrange("(m p) h d -> p m (h d)", p=P), k_tok[:]).then_inc(out_kv, 16)
            pool.wait_ge(vt_ev, 4)
            pool.dma_start(o["memv_prompt"][0, 0].rearrange("(m p) h d -> p m (h d)", p=P), v_tok[:]).then_inc(out_kv, 16)
            add_squares(24)
            pool.dma_start(gain_row[:], a["norm_final"].rearrange("(o d) -> o d", o=1).to_broadcast([P, D])).then_inc(gain_in, 16)
            pool.wait_ge(out_y, 16 * (NCH + 1))
            pool.wait_ge(out_kv, 32)
            pool.wait_ge(out_ssm, 16)
            pool.wait_ge(out_pool, 48)
            pool.wait_ge(out_edge, 48)
            for k in range(SR):
                pool.wait_ge(st_out[k], 16 * len(range(k, 2 * NS, SR)))

        @block.scalar
        def _(act):
            chain = Chain(act, a_step)
            act.dma_start(xs_row[:], a["x_sample"].rearrange("b s d -> (b s) d")).then_inc(s_in, 16)
            act.dma_start(dtw[:], win[:, :, OFF_DT:OFF_DT + HEADS]).then_inc(small_in, 16)
            act.dma_start(hcol[:, 0:1], a["dt_bias"].rearrange("o h -> h o")).then_inc(small_in, 16)
            act.dma_start(a_row[:], a["a_log"].to_broadcast([P, HEADS])).then_inc(small_in, 16)
            act.dma_start(hs_rhs[:, 16:17], a["d_skip"].rearrange("o h -> h o")).then_inc(small_in, 16)
            act.dma_start(dskip[:], a["d_skip"].to_broadcast([P, HEADS])).then_inc(small_in, 16)

            def norm_std(used):
                act.wait_ge(sq_used, used)
                nc.scalar.activation(halves(std[:]), aux[:, 2:4, 0:HALF], ACT.Sqrt, bias=eps_col[:, 0:1],
                                     scale=1.0 / D).then_inc(std_ready, 1)

            def turned_x(n):
                act.wait_ge(xtr_done, n + 2)
                nc.scalar.activation(x0[:, 4:8, n // 2 * P:n // 2 * P + P], aux[:, n % 4, :].rearrange("p (k t) -> p k t", k=4),
                                     ACT.Copy).then_inc(xtr_evac_a, 1)

            act.wait_ge(s_in, 16)
            act.wait_ge(tok_v, 1)
            nc.scalar.activation(x_junk[4][0:NS, :], xs_row[:], ACT.Square, accum_out=tok_sum[0:NS, 4:5])
            act.wait_ge(x_in[0], 16)
            nc.scalar.activation(x_junk[0][:], x_tok[:, 0, :], ACT.Square, accum_out=tok_sum[:, 0:1])
            turned_x(1)
            act.wait_ge(x_in[2], 16)
            chain(nc.scalar.activation(x_junk[2][:], x_tok[:, 2, :], ACT.Square, accum_out=tok_sum[:, 2:3]))
            turned_x(3)
            act.wait_ge(tok_v, 3)
            nc.scalar.activation(tok_std[:], tok_sum[:], ACT.Sqrt, bias=eps_col[:, 0:1], scale=1.0 / D).then_inc(tok_a, 1)
            turned_x(5)
            turned_x(7)
            act.wait_ge(tok_mm, 1)
            nc.scalar.activation(rstd[:, 0:SEQ], slot[1][:, 0, :], ACT.Copy)
            nc.scalar.activation(rstd[:, SEQ:TT], slot[1][:, 1, 0:NS], ACT.Copy).then_inc(std_ready, 1)
            split_hi(act, 0)
            act.wait_ge(small_in, 80)
            nc.scalar.activation(dtw_hi[:], dtw[:], ACT.Copy).then_inc(dtw_hi_s, 1)
            for k in range(KT):
                act.wait_ge(ut_ready, k + 1)
                nc.scalar.activation(a_hi[:, k, :], ut[k % 2][:], ACT.Copy).then_inc(uh_ready, 1)
                if k == 3:
                    split_hi(act, 1)

            def conv_front(t, i=0):
                act.wait_ge(gemm_done, t + 1 + i * 8)
                nc.scalar.activation(halves(cbuf[t % 2][:, TAPS - 1:TAPS - 1 + TT]), in_slot(t % 2),
                                     ACT.Copy).then_inc(evacuated[t % 2], 1)
                split_hi(act, t + 2, i, 8)
                act.wait_ge(conv_done, t + 1 + i * 8)
                nc.scalar.activation(tbuf[:], hbuf[t % 2][:], ACT.Tanh).then_inc(tanh_done, 1)

            conv_front(0)
            with act.Fori(0, 2) as i:
                for t in range(8):
                    conv_front(t + 1, i)
                    act.wait_ge(xtr2_done, t + 1 + i * 8)
                    nc.scalar.activation(xs_tok[:, :, bass.ds(i * D + t * P, P)],
                                         aux[:, t % 2, :].rearrange("p (c f) -> p c f", c=NCH),
                                         ACT.Copy).then_inc(xtr2_evac, 1)
            def dt_step(n):
                fl = "p c h -> p (c h)"
                if n == 0:
                    act.wait_ge(dt_b, 1)
                    nc.scalar.activation(dt_tmp[1][:], dt_tmp[1][:], ACT.Exp, scale=-1.0).then_inc(dt_a, 1)
                    nc.scalar.activation(a_row[:], a_row[:], ACT.Exp).then_inc(dt_a, 1)
                elif n == 1:
                    act.wait_ge(dt_b, 2)
                    nc.scalar.activation(dt_tmp[5][:], dt_tmp[2][:], ACT.Ln).then_inc(dt_a, 1)
                elif n == 4:
                    act.wait_ge(cs_v, 1)
                    nc.scalar.activation(hs_rhs[:, NS:2 * NS], aux[0:HEADS, 3, NS:2 * NS], ACT.Exp).then_inc(dt_a, 1)
                    nc.scalar.activation(ecs[:].rearrange(fl), aux[:, 2, 0:P], ACT.Exp).then_inc(dt_a, 1)
                    nc.scalar.activation(cdec[:].rearrange(fl), aux[:, 2, P:2 * P], ACT.Exp).then_inc(dt_a, 1)
                    nc.scalar.activation(dtd[:].rearrange(fl), dtd[:].rearrange(fl), ACT.Exp).then_inc(dt_a, 1)

            for t in range(17, 24):
                conv_front(t)
                for n in {17: (0,), 18: (1,), 19: (2,), 20: (3,), 22: (4,), 23: (5,)}.get(t, ()):
                    act.wait_ge(edge_tr, n + 1)
                    nc.scalar.activation(conv_edge[:, n * 512:(n + 1) * 512], aux[0:EDGE, 1 + 2 * (n % 2), :],
                                         ACT.Copy).then_inc(edge_ev, 1)
                dt_step(t - 17)

            def decays(sem_in, s, c, gr, j0, sem_out):
                act.wait_ge(sem_in, s)
                for j in range(j0, j0 + 4):
                    last = nc.scalar.activation(decay[:, j, :], aux[:, 0, (j - j0) * P:(j - j0 + 1) * P], ACT.Exp,
                                                bias=ncs[:, c, gr * HPG + j:gr * HPG + j + 1])
                last.then_inc(sem_out, 1)

            def z_tile(t, i):
                act.wait_ge(gemm_done, t + 1 + i * 8)
                split_hi(act, t + 2, i, 8)
                nc.scalar.activation(halves(tz[t % 2][:]), in_slot(t % 2), ACT.Tanh, scale=0.5).then_inc(tz_ready, 1)

            def b_turned(s):
                act.wait_ge(cb_ready, s)
                nc.scalar.activation(b_tok[:], aux[:, 3, 0:P], ACT.Copy)

            with act.Fori(0, 2) as i:
                for gr in range(GROUPS):
                    s = 4 * i + gr + 1
                    b_turned(s)
                    decays(cb_ready, s, i, gr, 0, exp_a)
                    z_tile(T_Z + 2 * gr, i)
                    decays(off_ready, s, i, gr, 4, exp_b)
                    z_tile(T_Z + 2 * gr + 1, i)
            act.wait_ge(smp_v, 1)
            nc.scalar.activation(acts_s[:], tmp_s[:], ACT.Tanh).then_inc(smp_a, 1)
            act.wait_ge(out_edge, 48)
            with act.Fori(0, 2) as i:
                for gr in range(GROUPS):
                    s = 8 + 4 * i + gr + 1
                    t = T_PU + gr
                    b_turned(s)
                    decays(cb_ready, s, 2 + i, gr, 0, exp_a)
                    decays(off_ready, s, 2 + i, gr, 4, exp_b)
                    act.wait_ge(gemm_done, t + 1 + i * 4)
                    split_hi(act, t + 2, i, 4)
                    nc.scalar.activation(halves(pu[:, 4 * i + gr, :]), in_slot(t % 2),
                                         ACT.Copy).then_inc(evacuated[t % 2], 1)

            so_dram = o["ssm_sample"][0].rearrange("b (j t h) p n -> b j (h p) t n", j=2, h=2)

            def store_state(n):
                act.wait_ge(st_new, n + 1)
                act.dma_start(so_dram[n // 2, n % 2], sring[n % SR][:]).then_inc(st_out[n % SR], 16)

            for k in range(8):
                t = T_GA + k
                act.wait_ge(gemm_done, t + 1)
                split_hi(act, t + 2)
                nc.scalar.activation(halves(gate_a[:, k, :]), in_slot(t % 2), ACT.Tanh, scale=0.5).then_inc(evacuated[t % 2], 1)
                store_state(k)

            def y_square(f):
                if f >= 6:
                    act.wait_ge(sq_used, f // 2 * 2 - 2)
                nc.scalar.activation(ysq[f // 2][f % 2][:], zs[:, f, 0:SEQ], ACT.Square).then_inc(sq_ready, 1)

            def y_root(gr):
                act.wait_ge(diag_done, gr + 1)
                nc.scalar.activation(y_tok_std[:, gr, :], y_tok_sum[:, gr, :], ACT.Sqrt, bias=eps_col[:, 0:1],
                                     scale=1.0 / (4 * GW)).then_inc(y_rms, 1)

            act.wait_ge(out_ssm, 16)
            act.wait_ge(out_pool, 48)
            act.wait_ge(yt_ev, 2)
            y_square(0)
            y_square(1)
            act.wait_ge(pool_sum, 6)
            act.wait_ge(yt_ev, 16)
            for k in range(8):
                t = T_GB + k
                act.wait_ge(gemm_done, t + 1)
                split_hi(act, t + 2)
                nc.scalar.activation(halves(gate_b[:, k, :]), in_slot(t % 2), ACT.Tanh, scale=0.5).then_inc(evacuated[t % 2], 1)
                store_state(8 + k)
                if k < 7:
                    y_square(2 * k + 2)
                    y_square(2 * k + 3)
                if k % 2 and k < 7:
                    y_root(k // 2)
            act.wait_ge(pool_sum_s, 1)
            act.wait_ge(pool_sum, KT)
            for n, k in enumerate(D_ORDER):
                nc.scalar.activation(a_hi[:, k, :], pu[:, k, :], ACT.Copy).then_inc(pool_hi, 1)
                if n == 2:
                    y_root(3)
            act.wait_ge(ys_ready, 1)
            nc.scalar.activation(y_sq[:], y_s[:], ACT.Square).then_inc(ys_sq, 1)
            for k in range(8, 16):
                act.wait_ge(ut_ready, 8 + (12 if k < 12 else 16))
                if k == 12:
                    act.wait_ge(ys_sum, 1)
                    nc.scalar.activation(y_std[:], y_std[:], ACT.Sqrt, bias=eps_col[:, 0:1], scale=1.0 / (4 * GW)).then_inc(ys_std, 1)
                nc.scalar.activation(b_hi[:, k - 8, 0:SEQ], zs[:, k, 0:SEQ], ACT.Copy).then_inc(uh_ready, 1)
            split_hi(act, T_POOL + 2)
            act.wait_ge(ys_n, 1)
            nc.scalar.activation(b_hi[:, :, SEQ:TT], y_s[:, 8:16, :], ACT.Copy).then_inc(ys_hi, 1)
            act.wait_ge(pool_mm, 8)
            split_hi(act, T_POOL + 3)
            for k in range(8):
                nc.scalar.activation(a_hi[:, k, 0:SEQ], zs[:, k, 0:SEQ], ACT.Copy).then_inc(uh_ready, 1)
            nc.scalar.activation(a_hi[:, :, SEQ:TT], y_s[:, 0:8, :], ACT.Copy).then_inc(ys_hi, 1)
            for c4 in range(4):
                for m in range(2):
                    split_hi(act, T_SSD + 4 * c4 + m + 2)
                for m in range(2):
                    k = 2 * c4 + m
                    split_hi(act, T_SSD + 4 * c4 + m + 4)
                    act.wait_ge(mg_ready, k + 1)
                    nc.scalar.activation(c_hi[:, k, :], ut[k % 2][:], ACT.Copy).then_inc(mgh_ready, 1)

            def res_tile(q, t, k, gain, hi):
                act.wait_ge(gemm_done, t + 1)
                split_hi(act, t + 2)
                act.wait_ge(evacuated[t % 2], uses(t) + 2)
                act.wait_ge(sq_used, q + k - 1)
                nc.scalar.activation(sq[k % 2][:] if k else sq_sum[:], x[:, k, :], ACT.Square).then_inc(sq_ready, 1)
                nc.scalar.activation(hi[:, k, :], x[:, k, :], ACT.Copy, scale=cols[:, gain + k:gain + k + 1]).then_inc(uh_ready, 1)

            def turned(t):
                return t.rearrange("p (k m d) -> p m k d", k=2, m=2)

            for k in range(KT):
                res_tile(16, T_O + k, k, CN_X, a_hi)
                if 3 <= k < 7:
                    n = k - 3
                    act.wait_ge(mem_tr, n + 1)
                    nc.scalar.activation(mem_hi[:, 2 * n:2 * n + 2, :], aux[:, n % 2, :].rearrange("p (k m) -> p k m", k=2),
                                         ACT.Copy).then_inc(mem_hi_s, 1)
            norm_std(24)
            for k in range(KT):
                t = T_K + k
                act.wait_ge(gemm_done, t + 1)
                split_hi(act, t + 2)
                nc.scalar.activation(kT[:, k, :], slot[t % 2][:, 0, 0:MEM], ACT.Copy).then_inc(evacuated[t % 2], 1)
            for k in range(8):
                t = T_Q + k
                act.wait_ge(gemm_done, t + 1)
                split_hi(act, t + 2)
                if k % 2:
                    n = k // 2
                    act.wait_ge(kt_mm, n + 1)
                    nc.scalar.activation(k_tok[:, :, n * 256:(n + 1) * 256].rearrange("p m (k d) -> p m k d", k=2),
                                         turned(aux[:, n % 2, :]), ACT.Copy).then_inc(kt_ev, 1)

            def v_turned(n):
                act.wait_ge(vt_mm, n + 1)
                nc.scalar.activation(v_tok[:, :, n * 256:(n + 1) * 256].rearrange("p m (k d) -> p m k d", k=2),
                                     turned(slot[n % 2][:, 1, :]), ACT.Copy).then_inc(vt_ev, 1)

            for k in range(8):
                t = T_V + k
                act.wait_ge(gemm_done, t + 1)
                split_hi(act, t + 2)
                nc.scalar.activation(vT[:, k, :], slot[t % 2][:, 0, 0:MEM], ACT.Copy).then_inc(evacuated[t % 2], 1)
                if k == 0:
                    act.wait_ge(qt_mm, 1)
                    nc.scalar.activation(q_tok[:].rearrange("p (j n) -> p j n", j=2), aux[0:2 * NS, 0:2, :], ACT.Copy).then_inc(qt_ev, 1)
                if k >= 3 and k % 2:
                    v_turned((k - 3) // 2)
            v_turned(3)
            act.wait_ge(sm_b, 1)
            nc.scalar.activation(prob_s[:], slot[0][0:32, 1, 0:MEM], ACT.Exp, bias=stats[0:32, 1:2], scale=XD ** -0.5,
                                 accum_out=stats[0:32, 2:3]).then_inc(sm_c, 1)
            for n in range(16):
                h, tq = n // 4, n % 4
                act.wait_ge(negmax, n + 1)
                nc.scalar.activation(prob[n % 2][:], aux[:, n % 2, 0:MEM], ACT.Exp, bias=stats[:, 16 + n:17 + n],
                                     scale=XD ** -0.5, accum_out=stats[:, 32 + n:33 + n]).then_inc(prob_exp, 1)
                if n == 15:
                    act.wait_ge(o_s_tr, 1)
                    nc.scalar.activation(a_hi[:, :, SEQ:TT], slot[0][:, 1, 0:64].rearrange("p (k b) -> p k b", k=KT),
                                         ACT.Copy).then_inc(o_s_hi, 1)
                act.wait_ge(pt_mm, n + 1)
                nc.scalar.activation(probT[h % 2][:, :, tq * P:(tq + 1) * P],
                                     aux[:, 2 + n % 2, 0:MEM].rearrange("p (m l) -> p m l", m=2), ACT.Copy).then_inc(pt_ev, 1)
                if tq == 3:
                    for dt in range(2):
                        act.wait_ge(pv_mm, 2 * h + dt + 1)
                        nc.scalar.activation(a_hi[:, 2 * h + dt, 0:SEQ], pv_bank(h, dt), ACT.Copy).then_inc(pv_hi, 1)
                if n == 14:
                    act.wait_ge(cache_used, 2 * NS)
                    for j in range(2):
                        nc.scalar.activation(o_tok[:, j * 512:(j + 1) * 512], slot[j][0:NS, 1, :], ACT.Copy).then_inc(o_s_row, 1)
            for k in range(KT):
                res_tile(24, T_XO + k, k, CN_MLP, b_hi)
            norm_std(32)

            def ff_up(t, k, n, i=0):
                act.wait_ge(gemm_done, t + 1 + i * 16)
                split_hi(act, t + 2, i, 16)
                act.wait_ge(evacuated[t % 2], uses(t) + 2 + i * 8)
                if k >= 2:
                    act.wait_ge(ff_lo, n - 1 + i * 8)
                nc.scalar.activation(ut[k % 2][:], rt[k % 2][:], ACT.Square).then_inc(ff_sq, 1)
                act.wait_ge(ff_sq, n + 1 + i * 8)
                nc.scalar.activation(c_hi[:, k, :], ut[k % 2][:], ACT.Copy).then_inc(ff_hi, 1)

            with act.Fori(0, FF_CHUNKS - 1) as i:
                for k in range(8):
                    ff_up(T_MLP + k, k, k, i)
                for k in range(8):
                    split_hi(act, T_MLP + 8 + k + 2, i, 16)
            T_LAST = T_MLP + 16 * (FF_CHUNKS - 1)
            for k in range(8):
                ff_up(T_LAST + k, k, 8 * (FF_CHUNKS - 1) + k)
            for k in range(4):
                split_hi(act, T_LAST + 8 + k + 2)
            for c in range(NCH):
                act.wait_ge(fin_mm, c + 1)
                nc.scalar.activation(fin_junk[:, c, :], aux[:, c, :], ACT.Square, accum_out=stats[:, c:c + 1])
                nc.scalar.activation(y_tok[:, c, 0:512], aux[:, c, :], ACT.Copy).then_inc(fin_copy, 1)
                if c == 1:
                    split_hi(act, T_LAST + 8 + 6)
                if c == 3:
                    split_hi(act, T_LAST + 8 + 7)
            for c in range(NCH):
                act.wait_ge(fin_mm, NCH + c + 1)
                ins = nc.scalar.activation(fin_junk[:, 4 + c, :], aux[:, c, :], ACT.Square, accum_out=stats[:, 4 + c:5 + c])
            ins.then_inc(fin_sq, 1)
            act.wait_ge(fin_sum, 1)
            nc.scalar.activation(stats[:, 16:20], stats[:, 12:16], ACT.Sqrt, bias=eps_col[:, 0:1], scale=1.0 / D).then_inc(fin_std, 1)
            act.wait_ge(fin_mm, 2 * NCH + 1)
            chain(nc.scalar.activation(fin_junk_s[:], slot[0][0:NS, :, :], ACT.Square, accum_out=stats[0:NS, 8:9]))
            nc.scalar.activation(stats[0:NS, 9:10], stats[0:NS, 8:9], ACT.Sqrt, bias=eps_col[0:NS, 0:1], scale=1.0 / D).then_inc(fin_std, 1)
            act.wait_ge(fin_ev, NCH + 1)
            act.dma_start(o["y_sample"].rearrange("b s d -> (b s) d"), ys_tok[:]).then_inc(out_y, 16)

        @block.vector
        def _(dve):
            chain = Chain(dve, v_step)
            dve.sem_inc(evacuated[0], 1)
            dve.sem_inc(evacuated[1], 1)
            dve.sem_inc(xtr2_evac, 2)
            nc.vector.memset(eps_col[:], EPS).then_inc(consts, 1)

            def turned_x(n):
                dve.wait_ge(xtr_done, n + 2)
                nc.vector.tensor_copy(x0[:, 0:4, n // 2 * P:n // 2 * P + P],
                                      aux[:, n % 4, :].rearrange("p (k t) -> p k t", k=4)).then_inc(xtr_evac, 1)

            def row_squares(c):
                dve.wait_ge(x_in[c], 16)
                nc.vector.tensor_tensor_reduce(x_junk[c][:], x_tok[:, c, :], x_tok[:, c, :], 1.0, 0.0, ALU.mult, ALU.add,
                                               tok_sum[:, c:c + 1]).then_inc(tok_v, 1)

            nc.vector.memset(tok_sum[:, 4:5], 1.0).then_inc(tok_v, 1)
            dve.wait_ge(xtr_done, 1)
            nc.vector.tensor_copy(x0[:, :, SEQ:TT], slot[0][:, 0, 0:64].rearrange("p (k b) -> p k b", k=KT)).then_inc(xtr_evac, 1)
            turned_x(0)
            row_squares(1)
            turned_x(2)
            row_squares(3)
            turned_x(4)
            turned_x(6)
            dve.wait_ge(tok_a, 1)
            nc.vector.reciprocal(tok_inv[:], tok_std[:]).then_inc(tok_v, 1)
            dve.wait_ge(xtr_done, 10)
            g_ps = slot[0][:, 1, :]
            nc.vector.tensor_copy(cols[:, 0:C_PS], g_ps[:, 0:C_PS])
            nc.vector.tensor_scalar(cols[:, C_PS:C_SSD], g_ps[:, C_PS:C_SSD], 0.5, None, ALU.mult)
            nc.vector.tensor_scalar(cols[:, C_SSD:C_CW], g_ps[:, C_SSD:C_CW], 0.25, None, ALU.mult)
            nc.vector.tensor_scalar(cols[:, C_CW:176], g_ps[:, C_CW:176], 0.5, None, ALU.mult).then_inc(xtr_evac, 1)
            dve.wait_ge(xtr_evac, 6)
            dve.wait_ge(xtr_evac_a, 4)
            dve.wait_ge(std_ready, 1)

            def u_lo(k):
                dve.wait_ge(uh_ready, k + 1)
                nc.vector.tensor_tensor(a_lo[:, k, :], ut[k % 2][:], a_hi[:, k, :].bitcast(F32), ALU.subtract).then_inc(u_ready, 1)

            for k in range(KT):
                if k >= 2:
                    u_lo(k - 2)
                    dve.wait_ge(u_ready, k - 1)
                nc.vector.scalar_tensor_tensor(out=ut[k % 2][:], in0=x0[:, k, :], scalar=cols[:, CN_MIX + k:CN_MIX + k + 1],
                                               in1=rstd[:], op0=ALU.mult, op1=ALU.mult).then_inc(ut_ready, 1)
                if k == 1:
                    split_lo(dve, 0)
                    dve.wait_ge(dtw_hi_s, 1)
                    nc.vector.tensor_tensor(dtw_lo[:], dtw[:], dtw_hi[:].bitcast(F32), ALU.subtract).then_inc(dtw_lo_s, 1)
            u_lo(6)
            u_lo(7)
            split_lo(dve, 1)
            dve.wait_ge(dt_mm, 1)
            nc.vector.tensor_scalar(halves(dt_raw[:]), aux[0:HEADS, 2:4, 0:HALF], hcol[:, 0:1], None, ALU.add).then_inc(dt_evac, 1)

            v, e, w, m_, msk, ln = dt_tmp

            def dt_step(n):
                fl = "p c h -> p (c h)"
                if n == 0:
                    dve.wait_ge(dt_tr, 1)
                    nc.vector.tensor_copy(v[:, 0:NCH, :], aux[:, 2, 0:P].rearrange("p (c h) -> p c h", c=NCH))
                    chain(nc.vector.tensor_copy(v[0:NS, NCH, :], aux[0:NS, 2, P:P + HEADS]))
                    nc.vector.scalar_tensor_tensor(out=e[:], in0=v[:], scalar=-1.0, in1=v[:], op0=ALU.mult, op1=ALU.max).then_inc(dt_b, 1)
                elif n == 1:
                    dve.wait_ge(dt_a, 2)
                    nc.vector.tensor_scalar(w[:], e[:], 1.0, None, ALU.add).then_inc(dt_b, 1)
                    dve.wait_ge(dt_b, 2)
                    chain(nc.vector.tensor_scalar(m_[:], w[:], -1.0, None, ALU.add))
                    chain(nc.vector.tensor_scalar(msk[:], m_[:], 0.0, None, ALU.is_equal))
                    chain(nc.vector.tensor_tensor(m_[:], m_[:], msk[:], ALU.add))
                    chain(nc.vector.reciprocal(m_[:], m_[:]))
                elif n == 2:
                    dve.wait_ge(dt_a, 3)
                    chain(nc.vector.tensor_tensor(ln[:], ln[:], msk[:], ALU.add))
                    chain(nc.vector.tensor_tensor(ln[:], ln[:], m_[:], ALU.mult))
                    chain(nc.vector.tensor_tensor(ln[:], ln[:], e[:], ALU.mult))
                    chain(nc.vector.scalar_tensor_tensor(out=dtk[:, 0], in0=v[:], scalar=0.0, in1=ln[:], op0=ALU.max, op1=ALU.add))
                    nc.vector.scalar_tensor_tensor(out=dtk[:, 1], in0=dtk[:, 0], scalar=-1.0,
                                                   in1=a_row[:].unsqueeze(1).to_broadcast([P, NCH + 1, HEADS]),
                                                   op0=ALU.mult, op1=ALU.mult).then_inc(dt_b, 1)
                elif n == 4:
                    dve.wait_ge(cs_mm, 1)
                    nc.vector.tensor_copy(hs_rhs[:, 0:NS], aux[0:HEADS, 3, 0:NS])
                    cs = aux[:, 2, 0:P].rearrange("p (i j) -> p j i", j=4)
                    chain(nc.vector.tensor_copy(cs_split[:, :, 0, :].bitcast(R32), cs))
                    nc.vector.tensor_tensor(cs_split[:, :, 1, :], cs, cs_split[:, :, 0, :], ALU.subtract)
                    nc.vector.tensor_tensor(pick_step[:], ident[0:64, 0:32], ident[0:64, 32:64], ALU.add)
                    chain(nc.vector.tensor_scalar(ncs[:].rearrange(fl), aux[:, 2, 0:P], -1.0, None, ALU.mult))
                    nc.vector.tensor_tensor(dtd[:].rearrange(fl), aux[:, 2, P:2 * P], ncs[:].rearrange(fl), ALU.add).then_inc(cs_v, 1)
                elif n == 5:
                    dve.wait_ge(dt_a, 7)
                    nc.vector.tensor_tensor(dtd[:], dtd[:], dtk[:, 0, 0:NCH], ALU.mult).then_inc(cs_v, 1)

            def conv_front(t, dst, done, i=0):
                dve.wait_ge(evacuated[t % 2], t // 2 + 2 + i * 4)
                b = cbuf[t % 2]
                f = t + i * 8
                nc.vector.tensor_copy(xedge[:, f, :], b[:, SEQ:SEQ + EDGE])
                h = hbuf[t % 2][:]
                chain(nc.vector.tensor_scalar(h, b[:, 0:SEQ], cols[:, bass.ds(C_CW + f, 1)], cols[:, bass.ds(C_CB + f, 1)],
                                              ALU.mult, ALU.add))
                for k in range(1, TAPS):
                    ins = nc.vector.scalar_tensor_tensor(out=h, in0=b[:, k:k + SEQ], scalar=cols[:, bass.ds(C_CW + CT * k + f, 1)],
                                                         in1=h, op0=ALU.mult, op1=ALU.add)
                    if k < TAPS - 1:
                        chain(ins)
                    else:
                        ins.then_inc(conv_done, 1)
                split_lo(dve, t + 2, i, 8)
                dve.wait_ge(tanh_done, t + 1 + i * 8)
                nc.vector.scalar_tensor_tensor(out=dst, in0=tbuf[:], scalar=1.0, in1=h, op0=ALU.add,
                                               op1=ALU.mult).then_inc(done, 1)

            conv_front(0, abuf[0][:], act_ready)
            with dve.Fori(0, 2) as i:
                chain.loop(i, 24)
                for t in range(8):
                    conv_front(t + 1, abuf[(t + 1) % 2][:], act_ready, i)
                chain.end(2)
            dve.wait_ge(act_ready, 17)
            dve.wait_ge(spilled, 16)
            nc.vector.tensor_copy(bc[:, 0, 0:SEQ], abuf[0][:]).then_inc(bc_ready, 1)
            nc.vector.tensor_copy(spread[:].rearrange("h t (j d) -> h (t j) d", j=2),
                                  ident[0:HEADS, 0:HEADS].unsqueeze(2).to_broadcast([HEADS, HEADS, HD])).then_inc(old_ev, 1)
            chain(nc.vector.memset(v[:, NCH, :], 0.0))
            for t in range(17, 24):
                conv_front(t, bc[:, t - 16, 0:SEQ], bc_ready)
                m = t - 17 if t < 21 else t - 18
                if t != 21:
                    dve.wait_ge(old_tr, m + 1)
                    src = aux[:, 2 * (m % 2), :]
                    if m < 2:
                        ins = nc.vector.tensor_copy(sp_cols[:, 4 * m:4 * m + 4, :], src[:, 0:480].rearrange("p (k b) -> p k b", k=4))
                    elif m < 4:
                        ins = nc.vector.tensor_copy(st_cols[:, 12 * m - 24:12 * m - 12, :],
                                                    src[:, 0:288].rearrange("p (k b) -> p k b", k=12))
                    elif m == 5:
                        ins = nc.vector.tensor_copy(cs_rows[:], src[0:64, :])
                    else:
                        ins = nc.vector.tensor_copy(exp_s[:].rearrange("p t j -> p (t j)"), src[:, 0:16 * 17])
                    ins.then_inc(old_ev, 1)
                dt_step(t - 17)

            def heads(t):
                return t.rearrange("p (h d) -> p h d", h=HPG)

            def prep(c, gr):
                hd = slice(gr * HPG, (gr + 1) * HPG)
                xs = heads(xs_tok[:, c, gr * GW:(gr + 1) * GW])
                nc.vector.tensor_tensor(heads(xdt[:]), xs, dtk[:, 0, c, hd].unsqueeze(2).to_broadcast([P, HPG, HD]), ALU.mult)
                nc.vector.tensor_tensor(heads(xdd[:]), xs, dtd[:, c, hd].unsqueeze(2).to_broadcast([P, HPG, HD]),
                                        ALU.mult).then_inc(x_prep, 1)

            def weights_a(s):
                dve.wait_ge(cb_ready, s)
                chain(nc.vector.tensor_tensor(cbm[:], aux[:, 1, 0:P], triu[:], ALU.mult))
                dve.wait_ge(exp_a, s)
                nc.vector.tensor_tensor(decay[:, 0:4, :], decay[:, 0:4, :], cbm[:].unsqueeze(1).to_broadcast([P, 4, P]), ALU.mult)

            def carry(s, c, gr):
                hd = slice(gr * HPG, (gr + 1) * HPG)
                dve.wait_ge(off_ready, s)
                nc.vector.tensor_tensor(heads(yacc[:]), heads(aux[:, 2, :]), ecs[:, c, hd].unsqueeze(2).to_broadcast([P, HPG, HD]), ALU.mult)
                chain(nc.vector.tensor_tensor(heads(state[:, gr, :]), heads(state[:, gr, :]),
                                              cdec[:, c, hd].unsqueeze(2).to_broadcast([P, HPG, HD]), ALU.mult))
                nc.vector.tensor_tensor(state[:, gr, :], state[:, gr, :], aux[:, 3, :], ALU.add)
                dve.wait_ge(exp_b, s)
                nc.vector.tensor_tensor(decay[:, 4:8, :], decay[:, 4:8, :], cbm[:].unsqueeze(1).to_broadcast([P, 4, P]),
                                        ALU.mult).then_inc(m_ready, 1)

            def finish_y(s, c, gr):
                dve.wait_ge(y_mm, s)
                chain(nc.vector.tensor_tensor(yacc[:], yacc[:], aux[:, 2, :], ALU.add))
                dve.wait_ge(skip_ready, s)
                nc.vector.tensor_tensor(xs_tok[:, c, gr * GW:(gr + 1) * GW], yacc[:], xskip[:], ALU.add).then_inc(y_ready, 1)

            def z_tile(t, k, i):
                split_lo(dve, t + 2, i, 8)
                dve.wait_ge(tz_ready, k + 1 + i * 8)
                nc.vector.scalar_tensor_tensor(out=halves(zs[:, k + i * 8, :]), in0=halves(tz[t % 2][:]), scalar=1.0,
                                               in1=in_slot(t % 2), op0=ALU.add, op1=ALU.mult).then_inc(evacuated[t % 2], 1)

            dve.wait_ge(xtr2_evac, 18)
            dve.wait_ge(bc_ready, 8)
            dve.wait_ge(spilled, 16)
            dve.wait_ge(consts, 6)
            dve.wait_ge(cs_v, 2)
            with dve.Fori(0, 2) as i:
                chain.loop(i, 12)
                for gr in range(GROUPS):
                    s = 4 * i + gr + 1
                    prep(i, gr)
                    weights_a(s)
                    z_tile(T_Z + 2 * gr, 2 * gr, i)
                    carry(s, i, gr)
                    z_tile(T_Z + 2 * gr + 1, 2 * gr + 1, i)
                    finish_y(s, i, gr)
                chain.end(2)
            with dve.Fori(0, 2) as i:
                chain.loop(i, 12)
                for gr in range(GROUPS):
                    s = 8 + 4 * i + gr + 1
                    prep(2 + i, gr)
                    weights_a(s)
                    carry(s, 2 + i, gr)
                    split_lo(dve, T_PU + gr + 2, i, 4)
                    finish_y(s, 2 + i, gr)
                chain.end(2)

            dve.wait_ge(smp_a, 1)
            chain(nc.vector.scalar_tensor_tensor(out=acts_s[:], in0=acts_s[:], scalar=1.0, in1=tmp_s[:], op0=ALU.add,
                                                 op1=ALU.mult))
            chain(nc.vector.tensor_copy(bc_cols[:, :, 0:NS].bitcast(R32), acts_s[:, 16:24, :]))
            nc.vector.tensor_tensor(bc_cols[:, :, NS:2 * NS], acts_s[:, 16:24, :], bc_cols[:, :, 0:NS], ALU.subtract)
            nc.vector.tensor_tensor(pick[:], ident[0:2 * NS, 0:NS], ident[0:2 * NS, NS:2 * NS], ALU.add).then_inc(smp_v, 1)
            for n in range(4):
                dve.wait_ge(end_tr, n + 1)
                nc.vector.tensor_copy(state_out[:, 4 * n:4 * n + 4, :], aux[:, n, :].rearrange("p (t n) -> p t n", t=4)).then_inc(end_ev, 1)
            dve.wait_ge(end_tr, 5)
            nc.vector.tensor_copy(bc_s[:, :].rearrange("p (j n) -> p j n", j=2), aux[0:2 * NS, 0:2, :]).then_inc(end_ev, 1)
            dve.wait_ge(smp_v, 2)
            nc.vector.tensor_tensor(xdt_s[:], acts_s[:, 0:16, :], exp_s[:, :, 0:NS], ALU.mult).then_inc(smp_v, 1)
            for n in range(2):
                dve.wait_ge(end_tr, 6 + n)
                nc.vector.tensor_copy(pool_edge[:, n * 512:(n + 1) * 512], aux[0:PEDGE, 2 + n, :]).then_inc(end_ev, 1)
            new = tmp_s[:, 16:24, :]
            for k in range(KT):
                w = WINDOWS[k // 2]
                old = sp_cols[:, k, :].rearrange("p (b j) -> p b j", b=NS)[:, :, PBUF - w + 1:PBUF]
                ins = nc.vector.tensor_reduce(new[:, k, :], old, AX.X, ALU.add)
            chain(ins)
            chain(nc.vector.tensor_tensor(new, new, pu[:, :, SEQ:TT], ALU.add))
            for gi, w in enumerate(WINDOWS):
                two = slice(2 * gi, 2 * gi + 2)
                ins = nc.vector.scalar_tensor_tensor(out=pu[:, two, SEQ:TT], in0=new[:, two, :], scalar=1.0 / w,
                                                     in1=pu[:, two, SEQ:TT], op0=ALU.mult, op1=ALU.subtract)
            ins.then_inc(pool_sum_s, 1)

            def recurrence_s(n):
                b, j = n // 2, n % 2
                dve.wait_ge(st_dec, n + 1)
                dve.wait_ge(bc_mm, b + 1)
                for t in range(8):
                    tt = 8 * j + t
                    gg = tt // 4
                    S = sring[n % SR][:, t, :]
                    ins = nc.vector.scalar_tensor_tensor(out=S, in0=aux[:, 0, gg * P:(gg + 1) * P],
                                                         scalar=xdt_s[:, tt, b:b + 1], in1=S, op0=ALU.mult, op1=ALU.add)
                ins.then_inc(st_new, 1)
                dve.wait_ge(st_new, n + 1)
                for t in range(8):
                    tt = 8 * j + t
                    gg = tt // 4
                    ins = nc.vector.tensor_tensor_reduce(junk_s[:, t, :], sring[n % SR][:, t, :], aux[:, 1, gg * P:(gg + 1) * P],
                                                         1.0, 0.0, ALU.mult, ALU.add, y_s[:, tt, b:b + 1])
                ins.then_inc(bc_used, 1)

            def scale_y(f):
                dve.wait_ge(y_row, f // 4 + 1)
                nc.vector.scalar_tensor_tensor(out=zs[:, f, 0:SEQ], in0=zs[:, f, 0:SEQ], scalar=cols[:, C_SSD + f:C_SSD + f + 1],
                                               in1=aux[:, 2 + f // 4 % 2, :], op0=ALU.mult, op1=ALU.mult).then_inc(ut_ready, 1)

            def y_diagonal(gr):
                dve.wait_ge(ysum_mm, gr + 1)
                for c in range(NCH):
                    ins = nc.vector.tensor_tensor_reduce(diag_junk[:, gr, c, :], ident[:], aux[:, 2 + gr % 2, c * P:(c + 1) * P],
                                                         1.0, 0.0, ALU.mult, ALU.add, y_tok_sum[:, gr, c:c + 1])
                ins.then_inc(diag_done, 1)

            def y_inverse(gr):
                dve.wait_ge(y_rms, gr + 1)
                nc.vector.reciprocal(y_tok_inv[:, gr, :], y_tok_std[:, gr, :]).then_inc(y_inv, 1)

            dve.wait_ge(smp_v, 3)
            recurrence_s(0)
            for k in range(8):
                split_lo(dve, T_GA + k + 2)
                recurrence_s(k + 1)
                for f in (2 * k, 2 * k + 1):
                    dve.wait_ge(yt_mm, f + 1)
                    nc.vector.tensor_tensor(zs[:, f, 0:SEQ], aux[:, 2 + f % 2, :], zs[:, f, 0:SEQ], ALU.mult).then_inc(yt_ev, 1)
            dve.wait_ge(yt_ev, 16)
            for k in range(8):
                split_lo(dve, T_GB + k + 2)
                if k % 2:
                    y_diagonal(k // 2)
                if k < 7:
                    recurrence_s(9 + k)
                if k % 2 and k < 7:
                    y_inverse(k // 2)
                if 2 <= k < 7:
                    scale_y(2 * k - 4)
                    scale_y(2 * k - 3)
            def pool_lo_part(k):
                dve.wait_ge(pool_hi, D_ORDER.index(k) + 1)
                nc.vector.tensor_tensor(a_lo[:, k, :], pu[:, k, :], a_hi[:, k, :].bitcast(F32), ALU.subtract).then_inc(pool_lo, 1)

            def pool_gated(n):
                f = 2 * (n % 4) + n // 4
                dve.wait_ge(pool_mm, n + 1)
                nc.vector.scalar_tensor_tensor(out=halves(gate_b[:, f, :]), in0=halves(gate_b[:, f, :]), scalar=1.0,
                                               in1=pool_bank(n), op0=ALU.add, op1=ALU.mult).then_inc(pool_ev, 1)

            def y_lo(n):
                dve.wait_ge(uh_ready, 8 + n + 1)
                nc.vector.tensor_tensor(b_lo[:, n, 0:SEQ], zs[:, n + 8, 0:SEQ], b_hi[:, n, 0:SEQ].bitcast(F32),
                                        ALU.subtract).then_inc(u_ready, 1)

            pool_lo_part(0)
            pool_lo_part(1)
            scale_y(10)
            scale_y(11)
            dve.wait_ge(bc_used, 16)
            chain(nc.vector.tensor_tensor(tmp_s[:, 0:16, :], acts_s[:, 0:16, :], exp_s[:, :, 16:17].to_broadcast([P, 16, NS]), ALU.mult))
            chain(nc.vector.tensor_tensor(y_s[:], y_s[:], tmp_s[:, 0:16, :], ALU.add))
            nc.vector.tensor_tensor(y_s[:], y_s[:], zs[:, :, SEQ:TT], ALU.mult).then_inc(ys_ready, 1)
            pool_lo_part(2)
            pool_lo_part(3)
            y_inverse(3)
            pool_gated(0)
            pool_gated(1)
            scale_y(12)
            scale_y(13)
            pool_gated(2)
            dve.wait_ge(ys_mm, 1)
            nc.vector.tensor_reduce(y_std[:], slot[0][:, 0, 0:P].rearrange("p (g k b) -> p g b k", g=GROUPS, b=NS), AX.X,
                                    ALU.add).then_inc(ys_sum, 1)
            scale_y(14)
            scale_y(15)
            pool_gated(3)
            y_lo(0)
            y_lo(1)
            dve.wait_ge(ys_std, 1)
            chain(nc.vector.reciprocal(y_std[:], y_std[:]))
            chain(nc.vector.tensor_tensor(y_s[:], y_s[:], cols[:, C_SSD:C_SSD + 16].unsqueeze(2).to_broadcast([P, 16, NS]), ALU.mult))
            nc.vector.tensor_tensor(y_s[:].rearrange("p (g k) b -> p g k b", g=GROUPS), y_s[:].rearrange("p (g k) b -> p g k b", g=GROUPS),
                                    y_std[:].unsqueeze(2).to_broadcast([P, GROUPS, 4, NS]), ALU.mult).then_inc(ys_n, 1)
            pool_gated(4)
            y_lo(2)
            split_lo(dve, T_POOL + 2)
            pool_gated(5)
            y_lo(3)
            y_lo(4)
            pool_gated(6)
            dve.wait_ge(ys_hi, 1)
            nc.vector.tensor_tensor(b_lo[:, :, SEQ:TT], y_s[:, 8:16, :], b_hi[:, :, SEQ:TT].bitcast(F32),
                                    ALU.subtract).then_inc(ys_lo, 1)
            y_lo(5)
            pool_gated(7)
            y_lo(6)
            y_lo(7)
            split_lo(dve, T_POOL + 3)
            for k in range(8):
                dve.wait_ge(uh_ready, 16 + k + 1)
                nc.vector.tensor_tensor(a_lo[:, k, 0:SEQ], zs[:, k, 0:SEQ], a_hi[:, k, 0:SEQ].bitcast(F32),
                                        ALU.subtract).then_inc(u_ready, 1)
            dve.wait_ge(ys_hi, 2)
            nc.vector.tensor_tensor(a_lo[:, :, SEQ:TT], y_s[:, 0:8, :], a_hi[:, :, SEQ:TT].bitcast(F32),
                                    ALU.subtract).then_inc(ys_lo, 1)
            for k in range(SR):
                dve.wait_ge(st_out[k], 16 * len(range(k, 2 * NS, SR)))

            for c4 in range(4):
                for m in range(2):
                    split_lo(dve, T_SSD + 4 * c4 + m + 2)
                for m in range(2):
                    k = 2 * c4 + m
                    t = T_SSD + 4 * c4 + 2 + m
                    split_lo(dve, t + 2)
                    dve.wait_ge(gemm_done, t + 1)
                    if k >= 2:
                        dve.wait_ge(mgl_ready, k - 1)
                    nc.vector.scalar_tensor_tensor(out=halves(ut[k % 2][:]), in0=halves(gate_a[:, k, :]), scalar=1.0,
                                                   in1=in_slot(m), op0=ALU.add, op1=ALU.mult).then_inc(evacuated[m], 1)
                    dve.wait_ge(evacuated[m], uses(T_SSD + 4 * c4 + m) + 2)
                    nc.vector.scalar_tensor_tensor(out=ut[k % 2][:], in0=gate_b[:, k, :], scalar=cols[:, C_PS + k:C_PS + k + 1],
                                                   in1=ut[k % 2][:], op0=ALU.mult, op1=ALU.add).then_inc(mg_ready, 1)
                    dve.wait_ge(mgh_ready, k + 1)
                    nc.vector.tensor_tensor(c_lo[:, k, :], ut[k % 2][:], c_hi[:, k, :].bitcast(F32), ALU.subtract).then_inc(mgl_ready, 1)

            def gained_lo(q, k, gain, hi, lo):
                dve.wait_ge(uh_ready, q + k + 1)
                nc.vector.scalar_tensor_tensor(out=lo[:, k, :], in0=x[:, k, :], scalar=cols[:, gain + k:gain + k + 1],
                                               in1=hi[:, k, :].bitcast(F32), op0=ALU.mult, op1=ALU.subtract).then_inc(u_ready, 1)

            def residual(t, k, i=0, step=0):
                split_lo(dve, t + 2, i, step)
                dve.wait_ge(gemm_done, t + 1 + i * step)
                nc.vector.tensor_tensor(halves(x[:, k, :]), in_slot(t % 2), halves(x[:, k, :]),
                                        ALU.add).then_inc(evacuated[t % 2], 1)

            dve.wait_ge(reloaded, 16)
            for k in range(KT):
                residual(T_O + k, k)
                if k >= 1:
                    gained_lo(24, k - 1, CN_X, a_hi, a_lo)
                if 3 <= k < 7:
                    n = k - 3
                    dve.wait_ge(mem_hi_s, n + 1)
                    nc.vector.tensor_tensor(mem_lo[:, 2 * n:2 * n + 2, :], aux[:, n % 2, :].rearrange("p (k m) -> p k m", k=2),
                                            mem_hi[:, 2 * n:2 * n + 2, :].bitcast(F32), ALU.subtract).then_inc(mem_lo_s, 1)
            gained_lo(24, 7, CN_X, a_hi, a_lo)
            for k in range(8):
                split_lo(dve, T_K + k + 2)
                if k == 7:
                    dve.wait_ge(std_ready, 2)
                    chain(nc.vector.reciprocal(rstd[:], std[:]))
            for k in range(8):
                t = T_Q + k
                split_lo(dve, t + 2)
                nc.vector.tensor_tensor(halves(qT[:, k, :]), in_slot(t % 2), halves(rstd[:]), ALU.mult).then_inc(evacuated[t % 2], 1)
            dve.wait_ge(evacuated[1], uses(T_V) + 1)
            chain(nc.vector.tensor_copy(q_cols[:, :, 0:NS].bitcast(R32), qT[:, :, SEQ:TT]))
            nc.vector.tensor_tensor(q_cols[:, :, NS:2 * NS], qT[:, :, SEQ:TT], q_cols[:, :, 0:NS], ALU.subtract).then_inc(q_split, 1)
            for b in range(NS):
                split_lo(dve, T_V + b + 2)
                dve.wait_ge(qb_mm, b + 1)
                dve.wait_ge(cache_in[b % CR], 16 * (b // CR + 1))
                if b >= 1:
                    dve.wait_ge(cache_used, b)
                for m in range(2):
                    for h in range(XH):
                        c = m * 32 + b * XH + h
                        ins = nc.vector.tensor_tensor_reduce(junk[:, m, h, :], cache[b % CR][:, m, h * XD:(h + 1) * XD],
                                                             q_bank(b)[:, h // 2, h % 2 * XD:(h % 2 + 1) * XD], 1.0, 0.0,
                                                             ALU.mult, ALU.add, s_cols[:, c:c + 1])
                ins.then_inc(cache_used, 1)
            def row_max(n):
                dve.wait_ge(score_mm, n + 1)
                chain(nc.vector.tensor_reduce(stats[:, 48 + n:49 + n], aux[:, n % 2, 0:MEM], AX.X, ALU.max))
                nc.vector.tensor_scalar(stats[:, 16 + n:17 + n], stats[:, 48 + n:49 + n], -(XD ** -0.5), None, ALU.mult).then_inc(negmax, 1)

            row_max(0)
            dve.wait_ge(sm_a, 1)
            chain(nc.vector.tensor_reduce(stats[0:32, 0:1], slot[0][0:32, 1, 0:MEM], AX.X, ALU.max))
            nc.vector.tensor_scalar(stats[0:32, 1:2], stats[0:32, 0:1], -(XD ** -0.5), None, ALU.mult).then_inc(sm_b, 1)
            row_max(1)
            dve.wait_ge(sm_c, 1)
            chain(nc.vector.reciprocal(stats[0:32, 3:4], stats[0:32, 2:3]))
            nc.vector.tensor_scalar(prob_s[:], prob_s[:], stats[0:32, 3:4], None, ALU.mult).then_inc(sm_d, 1)
            dve.wait_ge(sm_e, 1)
            dve.wait_ge(p_zero, 1)
            for m in range(2):
                for b in range(NS):
                    ins = nc.vector.tensor_copy(p_diag[:, m, b, :, b], slot[1][:, 1, m * 32 + b * XH:m * 32 + (b + 1) * XH])
            ins.then_inc(sm_f, 1)

            for n in range(16):
                h = n // 4
                if 1 <= n < 15:
                    row_max(n + 1)
                dve.wait_ge(prob_exp, n + 1)
                chain(nc.vector.reciprocal(stats[:, 64 + n % 16:65 + n % 16], stats[:, 32 + n:33 + n]))
                nc.vector.tensor_scalar(prob[n % 2][:], prob[n % 2][:], stats[:, 64 + n % 16:65 + n % 16], None, ALU.mult).then_inc(prob_n, 1)
                if n == 15:
                    dve.wait_ge(o_s_hi, 1)
                    nc.vector.tensor_tensor(a_lo[:, :, SEQ:TT], slot[0][:, 1, 0:64].rearrange("p (k b) -> p k b", k=KT),
                                            a_hi[:, :, SEQ:TT].bitcast(F32), ALU.subtract).then_inc(o_s_lo, 1)
                if n % 4 == 3:
                    for dt in range(2):
                        k = 2 * h + dt
                        dve.wait_ge(pv_hi, k + 1)
                        nc.vector.tensor_tensor(a_lo[:, k, 0:SEQ], pv_bank(h, dt), a_hi[:, k, 0:SEQ].bitcast(F32),
                                                ALU.subtract).then_inc(pv_lo, 1)
            dve.wait_ge(out_kv, 32)
            for k in range(KT):
                residual(T_XO + k, k)
                if k >= 1:
                    gained_lo(32, k - 1, CN_MLP, b_hi, b_lo)
            gained_lo(32, 7, CN_MLP, b_hi, b_lo)
            dve.wait_ge(std_ready, 3)
            chain(nc.vector.reciprocal(rstd[:], std[:]))

            def ff_up(t, k, n, i=0):
                dve.wait_ge(gemm_done, t + 1 + i * 16)
                if k >= 2:
                    dve.wait_ge(ff_sq, n - 1 + i * 8)
                nc.vector.scalar_tensor_tensor(out=halves(rt[k % 2][:]), in0=in_slot(t % 2), scalar=0.0, in1=halves(rstd[:]),
                                               op0=ALU.max, op1=ALU.mult).then_inc(evacuated[t % 2], 1)
                split_lo(dve, t + 2, i, 16)
                dve.wait_ge(ff_hi, n + 1 + i * 8)
                nc.vector.tensor_tensor(c_lo[:, k, :], ut[k % 2][:], c_hi[:, k, :].bitcast(F32), ALU.subtract).then_inc(ff_lo, 1)

            with dve.Fori(0, FF_CHUNKS - 1) as i:
                for k in range(8):
                    ff_up(T_MLP + k, k, k, i)
                for k in range(8):
                    residual(T_MLP + 8 + k, k, i, 16)
            T_LAST = T_MLP + 16 * (FF_CHUNKS - 1)
            for k in range(8):
                ff_up(T_LAST + k, k, 8 * (FF_CHUNKS - 1) + k)
            for k in range(8):
                residual(T_LAST + 8 + k, k)
            dve.wait_ge(fin_sq, 1)
            nc.vector.tensor_tensor(stats[:, 12:16], stats[:, 0:4], stats[:, 4:8], ALU.add).then_inc(fin_sum, 1)
            dve.wait_ge(fin_std, 1)
            chain(nc.vector.reciprocal(stats[:, 20:24], stats[:, 16:20]))
            dve.wait_ge(gain_in, 16)
            for c in range(NCH):
                nc.vector.scalar_tensor_tensor(out=y_tok[:, c, 0:512], in0=y_tok[:, c, 0:512], scalar=stats[:, 20 + c:21 + c],
                                               in1=gain_row[:, 0:512], op0=ALU.mult, op1=ALU.mult)
                nc.vector.scalar_tensor_tensor(out=y_tok[:, c, 512:D], in0=aux[:, c, :], scalar=stats[:, 20 + c:21 + c],
                                               in1=gain_row[:, 512:D], op0=ALU.mult, op1=ALU.mult).then_inc(fin_ev, 1)
            dve.wait_ge(fin_std, 2)
            chain(nc.vector.reciprocal(stats[0:NS, 10:11], stats[0:NS, 9:10]))
            nc.vector.scalar_tensor_tensor(out=ys_tok[:].rearrange("p (j n) -> p j n", j=2), in0=slot[0][0:NS, :, :],
                                           scalar=stats[0:NS, 10:11], in1=gain_row[0:NS, :].rearrange("p (j n) -> p j n", j=2),
                                           op0=ALU.mult, op1=ALU.mult).then_inc(fin_ev, 1)

        @block.tensor
        def _(pe):
            pe.wait_ge(consts, 5)
            pe.wait_ge(s_in, 16)
            for k in range(KT):
                last = nc.tensor.transpose(slot[0][:, 0, NS * k:NS * k + NS], xs_row[:, k * P:(k + 1) * P], ident[0:NS, 0:NS])
            last.then_inc(xtr_done, 1)
            for n in range(2 * NCH):
                if n % 2 == 0:
                    pe.wait_ge(x_in[n // 2], 16)
                if n >= 4:
                    pe.wait_ge((xtr_evac, xtr_evac_a)[n % 2], n // 2 - (n % 2))
                for j in range(4):
                    k = n % 2 * 4 + j
                    last = nc.tensor.transpose(aux[:, n % 4, j * P:(j + 1) * P], x_tok[:, n // 2, k * P:(k + 1) * P], ident[:])
                last.then_inc(xtr_done, 1)
            pe.wait_ge(vec_in, 16 * 8)
            nc.tensor.transpose(slot[0][:, 1, 0:56], vr1[:], ident[0:56, 0:56])
            nc.tensor.transpose(slot[0][:, 1, 56:176], vr2[:], ident[0:120, 0:120]).then_inc(xtr_done, 1)
            pe.wait_ge(tok_v, 4)
            for c in range(NCH):
                nc.tensor.matmul(slot[1][:, 0, c * P:(c + 1) * P], tok_inv[:, c:c + 1].to_broadcast([P, P]), ident[:],
                                 start=True, stop=True)
            nc.tensor.matmul(slot[1][:, 1, 0:NS], tok_inv[0:NS, NCH:NCH + 1].to_broadcast([NS, P]), ident[0:NS, 0:NS],
                             start=True, stop=True).then_inc(tok_mm, 1)

            def norm_tile(q, k, first, last_one):
                pe.wait_ge(sq_ready, q + k + 1)
                for h in range(2):
                    ins = nc.tensor.matmul(aux[:, 2 + h, 0:HALF], ones[:], sq[k % 2][:, h * HALF:(h + 1) * HALF],
                                           start=first, stop=last_one)
                ins.then_inc(sq_used, 1)
                return ins

            def residual_norm(q):
                pe.wait_ge(sq_used, q + KT - 1)
                for h in range(2):
                    nc.tensor.matmul(aux[:, 2 + h, 0:HALF], ones[:], sq_sum[:, h * HALF:(h + 1) * HALF], start=True, stop=False)
                norm_tile(q, KT - 1, False, True)

            pe.wait_ge(dtw_lo_s, 1)
            for k in range(KT):
                pe.wait_ge(u_ready, k + 1)
                for n, (w, u) in enumerate(((dtw_hi, a_hi), (dtw_hi, a_lo), (dtw_lo, a_hi))):
                    for h in range(2):
                        last = nc.tensor.matmul(aux[0:HEADS, 2 + h, 0:HALF], w[:, k, :], u[:, k, h * HALF:(h + 1) * HALF],
                                                start=(k == 0 and n == 0), stop=(k == KT - 1 and n == 2))
                if k == KT - 1:
                    last.then_inc(dt_mm, 1)
                gemm(pe, 0, a_hi, a_lo, kts=range(k, k + 1))
            pe.wait_ge(dt_evac, 1)
            for c in range(NCH):
                nc.tensor.transpose(aux[:, 2, c * HEADS:(c + 1) * HEADS], dt_raw[:, c * P:(c + 1) * P], ident[0:HEADS, 0:HEADS])
            nc.tensor.transpose(aux[0:NS, 2, P:P + HEADS], dt_raw[:, SEQ:TT], ident[0:HEADS, 0:HEADS]).then_inc(dt_tr, 1)
            with pe.Fori(0, 2) as i:
                for t in range(8):
                    gemm(pe, t + 1, a_hi, a_lo, i, 8)
                    pe.wait_ge(act_ready, t + 1 + i * 8)
                    pe.wait_ge(xtr2_evac, t + 1 + i * 8)
                    for c in range(NCH):
                        last = nc.tensor.transpose(aux[:, t % 2, c * P:(c + 1) * P], abuf[t % 2][:, c * P:(c + 1) * P], ident[:])
                    last.then_inc(xtr2_done, 1)
            def turn_edge(n):
                pe.wait_ge(conv_done, 4 * n + 4)
                if n >= 2:
                    pe.wait_ge(edge_ev, n - 1)
                for j in range(4):
                    last = nc.tensor.transpose(aux[0:EDGE, 1 + 2 * (n % 2), j * P:(j + 1) * P], xedge[:, 4 * n + j, :], ident[:])
                last.then_inc(edge_tr, 1)

            for t in range(17, 24):
                gemm(pe, t, a_hi, a_lo)
                m = t - 17 if t < 21 else t - 18
                if t == 17:
                    pe.wait_ge(xtr2_evac, 18)
                    pe.wait_ge(old_in, 32)
                if t == 18:
                    pe.wait_ge(dt_b, 1)
                if t == 21:
                    pe.wait_ge(dt_b, 3)
                    pe.wait_ge(old_ev, 5)
                    pe.wait_ge(edge_ev, 4)
                    rhs = dtk[:, 1, 0:NCH].rearrange("p c h -> p (c h)")
                    nc.tensor.matmul(aux[:, 2, 0:P], triu[:], rhs, start=True, stop=True)
                    nc.tensor.matmul(aux[:, 2, P:2 * P], ones[:], rhs, start=True, stop=True)
                    nc.tensor.transpose(aux[0:HEADS, 3, 0:NS], dtk[0:NS, 0, NCH, :], ident[0:NS, 0:NS])
                    nc.tensor.transpose(aux[0:HEADS, 3, NS:2 * NS], dtk[0:NS, 1, NCH, :], ident[0:NS, 0:NS]).then_inc(cs_mm, 1)
                if t == 22:
                    pe.wait_ge(dt_a, 7)
                    pe.wait_ge(cs_v, 1)
                if t != 21:
                    bank = aux[:, 2 * (m % 2), :]
                    pe.wait_ge(old_ev, max(1, m))
                    if m < 2:
                        for j in range(4):
                            last = nc.tensor.transpose(bank[:, j * 120:(j + 1) * 120], pool_rows[:, (4 * m + j) * P:(4 * m + j + 1) * P],
                                                       ident[0:120, 0:120])
                    elif m < 4:
                        for j in range(12):
                            f = 12 * m - 24 + j
                            last = nc.tensor.transpose(bank[:, j * 24:(j + 1) * 24], conv_rows[:, f * P:(f + 1) * P], ident[0:24, 0:24])
                    elif m == 5:
                        for j in range(4):
                            last = nc.tensor.transpose(bank[0:64, j * P:(j + 1) * P], cs_split[:, j].rearrange("p q i -> p (q i)"), ident[:])
                    else:
                        for j in range(16):
                            last = nc.tensor.matmul(bank[:, j * 17:(j + 1) * 17], spread[:, j, :], hs_rhs[:], start=True, stop=True)
                    last.then_inc(old_tr, 1)
                n = {17: 0, 18: 1, 19: 2, 20: 3, 22: 4}.get(t)
                if n is not None:
                    turn_edge(n)
            gemm(pe, T_Z, a_hi, a_lo)
            turn_edge(5)
            pe.wait_ge(old_ev, 7)
            pe.wait_ge(edge_ev, 6)
            pe.wait_ge(bc_ready, 8)

            def rows_of_cs(c, gr, j0):
                nc.tensor.matmul(aux[:, 0, :], identb[:], maskneg[:].unsqueeze(1).to_broadcast([P, 4, P]), start=True, stop=False)
                n = 8 * c + 2 * gr + j0 // 4
                return nc.tensor.matmul(aux[:, 0, :], pick_step[:, n:n + 1].to_broadcast([64, P]), cs_rows[:], start=False, stop=True)

            def step_a(c, gr):
                ch = slice(c * P, (c + 1) * P)
                nc.tensor.matmul(aux[:, 1, 0:P], bc[:, gr, ch], bc[:, GROUPS + gr, ch], start=True, stop=True)
                nc.tensor.transpose(aux[:, 3, 0:P], bc[:, gr, ch], ident[:])
                rows_of_cs(c, gr, 0).then_inc(cb_ready, 1)

            def step_b(c, gr, s):
                pe.wait_ge(exp_a, s)
                pe.wait_ge(x_prep, s)
                rows_of_cs(c, gr, 4)
                nc.tensor.matmul(aux[:, 2, :], bc[:, GROUPS + gr, c * P:(c + 1) * P], state[:, gr, :], start=True, stop=True)
                nc.tensor.matmul(aux[:, 3, :], b_tok[:], xdd[:], start=True, stop=True).then_inc(off_ready, 1)

            def step_c(s):
                pe.wait_ge(m_ready, s)
                for j in range(HPG):
                    last = nc.tensor.matmul(aux[:, 2, j * HD:(j + 1) * HD], decay[:, j, :], xdt[:, j * HD:(j + 1) * HD],
                                            start=(j == 0), stop=(j == HPG - 1), skip_group_check=True)
                last.then_inc(y_mm, 1)

            for c in range(NCH):
                for gr in range(GROUPS):
                    s = GROUPS * c + gr + 1
                    step_a(c, gr)
                    if c < 2:
                        if s > 1:
                            gemm(pe, T_Z + 8 * c + 2 * gr, a_hi, a_lo)
                        step_b(c, gr, s)
                        gemm(pe, T_Z + 8 * c + 2 * gr + 1, a_hi, a_lo)
                    else:
                        gemm(pe, T_PU + 4 * (c - 2) + gr, a_hi, a_lo, kts=range(0, 4))
                        step_b(c, gr, s)
                        gemm(pe, T_PU + 4 * (c - 2) + gr, a_hi, a_lo, kts=range(4, 8))
                    step_c(s)

            pe.wait_ge(y_ready, 16)
            for n in range(4):
                for j in range(4):
                    last = nc.tensor.transpose(aux[:, n, j * P:(j + 1) * P], state[:, n, j * P:(j + 1) * P], ident[:])
                last.then_inc(end_tr, 1)
            pe.wait_ge(smp_v, 2)
            pe.wait_ge(end_ev, 2)
            for j in range(8):
                last = nc.tensor.transpose(aux[0:2 * NS, j // 4, j % 4 * P:(j % 4 + 1) * P], bc_cols[:, j, :], ident[:])
            last.then_inc(end_tr, 1)
            pe.wait_ge(evacuated[0], uses(T_GA) + 1)
            pe.wait_ge(evacuated[1], uses(T_GA) + 1)
            for n in range(2):
                pe.wait_ge(end_ev, n + 3)
                for j in range(4):
                    last = nc.tensor.transpose(aux[0:PEDGE, 2 + n, j * P:(j + 1) * P], pu[:, 4 * n + j, SEQ - PBUF:TT], ident[:])
                last.then_inc(end_tr, 1)
            pe.wait_ge(end_ev, 5)

            def spread_bc(b):
                if b >= 1:
                    pe.wait_ge(bc_used, 2 * b)
                for j in range(2):
                    last = nc.tensor.matmul(aux[:, j, :], pick[:, b:b + 1].to_broadcast([2 * NS, P]),
                                            bc_s[:, j * 512:(j + 1) * 512], start=True, stop=True)
                last.then_inc(bc_mm, 1)

            for k in range(8):
                if k % 2 == 0:
                    spread_bc(k // 2)
                gemm(pe, T_GA + k, a_hi, a_lo)
                for f in (2 * k, 2 * k + 1):
                    if f < 2:
                        pe.wait_ge(end_ev, 6 + f)
                    else:
                        pe.wait_ge(yt_ev, f - 1)
                    for c in range(NCH):
                        last = nc.tensor.transpose(aux[:, 2 + f % 2, c * P:(c + 1) * P], xs_tok[:, c, f * P:(f + 1) * P], ident[:])
                    last.then_inc(yt_mm, 1)

            def y_sums(k):
                if k == 0:
                    pe.wait_ge(yt_ev, 16)
                elif k % 2 == 0 and k >= 4:
                    pe.wait_ge(ut_ready, 8 + 2 * k - 4)
                pe.wait_ge(sq_added, k + 1)
                nc.tensor.matmul(aux[:, 2 + k // 2 % 2, :], ones[:], ysq[k][0][:], start=(k % 2 == 0), stop=(k % 2 == 1)).then_inc(sq_used, 2)
                if k % 2:
                    pe.wait_ge(sq_used, 2 * k + 2)
                    pe.sem_inc(ysum_mm, 1)

            def y_rows(gr):
                pe.wait_ge(y_inv, gr + 1)
                for c in range(NCH):
                    last = nc.tensor.matmul(aux[:, 2 + gr % 2, c * P:(c + 1) * P], y_tok_inv[:, gr, c:c + 1].to_broadcast([P, P]),
                                            ident[:], start=True, stop=True)
                last.then_inc(y_row, 1)

            for k in range(8):
                if k % 2 == 0:
                    spread_bc(4 + k // 2)
                gemm(pe, T_GB + k, a_hi, a_lo)
                if k >= 2 and k % 2 == 0:
                    y_rows(k // 2 - 1)
                y_sums(k)
            pe.wait_ge(bc_used, 16)
            for n in range(8):
                m, gi = n // 4, n % 4
                t = T_POOL + m
                if gi == 0:
                    pe.wait_ge(lo_ready, t + 1)
                if n == 1:
                    pe.wait_ge(evacuated[1], uses(T_POOL) + 1)
                if n == 2:
                    y_rows(3)
                if n == 2:
                    pe.wait_ge(ys_sq, 1)
                    pe.wait_ge(evacuated[0], uses(T_POOL) + 1)
                    nc.tensor.matmul(slot[0][:, 0, 0:P], ones[:], y_sq[:].rearrange("p k b -> p (k b)"), start=True,
                                     stop=True).then_inc(ys_mm, 1)
                if n >= 2:
                    pe.wait_ge(pool_ev, n - 1)
                for kk in range(2):
                    k = 2 * gi + kk
                    if m == 0 and k < 4:
                        pe.wait_ge(pool_lo, k + 1)
                    elif m == 0:
                        pe.wait_ge(pool_lo_p, k - 3)
                    for q, (w, u) in enumerate(((w_hi, a_hi), (w_hi, a_lo), (w_lo, a_hi))):
                        for h in range(2):
                            last = nc.tensor.matmul(pool_bank(n)[:, h, :], w[:, m, k, :], u[:, k, h * HALF:(h + 1) * HALF],
                                                    start=(kk == 0 and q == 0), stop=(kk == 1 and q == 2))
                last.then_inc(pool_mm, 1)
                if gi == 3:
                    pe.wait_ge(pool_mm, n + 1)
                    pe.sem_inc(gemm_done, 1)
            pe.wait_ge(ys_sum, 1)
            for c4 in range(4):
                for half in range(2):
                    pe.wait_ge(ys_lo, 1 + half)
                    if half == 0:
                        pe.wait_ge(pool_ev, 8)
                    for m in range(2):
                        gemm(pe, T_SSD + 4 * c4 + 2 * half + m, *((b_hi, b_lo) if half == 0 else (a_hi, a_lo)),
                             start=(half == 0), stop=(half == 1),
                             ktwait=(lambda kk: pe.wait_ge(u_ready, 8 + 8 * half + kk + 1)) if m == 0 and c4 == 0 else None)
            def turn_mem(n):
                if n == 0:
                    pe.wait_ge(mem_in, 16)
                if n >= 2:
                    pe.wait_ge(mem_lo_s, n - 1)
                for kk in range(2):
                    for m in range(2):
                        last = nc.tensor.transpose(aux[:, n % 2, kk * MEM + m * P:kk * MEM + (m + 1) * P],
                                                   mem_tok[:, m, (2 * n + kk) * P:(2 * n + kk + 1) * P], ident[:])
                last.then_inc(mem_tr, 1)

            def gemm_mem(t):
                pe.wait_ge(lo_ready, t + 1)
                pe.wait_ge(evacuated[t % 2], uses(t) + 1)
                for kk in range(KT):
                    for q, (w, u) in enumerate(((w_hi, mem_hi), (w_hi, mem_lo), (w_lo, mem_hi))):
                        last = nc.tensor.matmul(slot[t % 2][:, 0, 0:MEM], w[:, t % 2, kk, :], u[:, kk, :],
                                                start=(kk == 0 and q == 0), stop=(kk == KT - 1 and q == 2))
                last.then_inc(gemm_done, 1)

            def turn_kv(bank, src, n):
                for kk in range(2):
                    for m in range(2):
                        last = nc.tensor.transpose(bank[:, (kk * 2 + m) * P:(kk * 2 + m + 1) * P],
                                                   src[:, 2 * n + kk, m * P:(m + 1) * P], ident[:])
                return last

            for k in range(8):
                gemm(pe, T_O + k, c_hi, c_lo, ktwait=(lambda kk: pe.wait_ge(mgl_ready, kk + 1)) if k == 0 else None)
                if 3 <= k < 7:
                    turn_mem(k - 3)
            pe.wait_ge(mem_lo_s, 4)
            for k in range(8):
                gemm_mem(T_K + k)
                if k == 0:
                    residual_norm(16)
            for k in range(8):
                gemm(pe, T_Q + k, a_hi, a_lo, ktwait=(lambda kk: pe.wait_ge(u_ready, 24 + kk + 1)) if k == 0 else None)
                if k % 2 == 1:
                    n = k // 2
                    if n == 0:
                        pe.wait_ge(evacuated[0], uses(T_Q) + 1)
                        pe.wait_ge(evacuated[1], uses(T_Q) + 1)
                    if n >= 2:
                        pe.wait_ge(kt_ev, n - 1)
                    turn_kv(aux[:, n % 2, :], kT, n).then_inc(kt_mm, 1)

            def turn_v(n):
                pe.wait_ge(evacuated[0], uses(T_V) + n + 2)
                pe.wait_ge(evacuated[1], uses(T_V) + n + 2)
                if n >= 2:
                    pe.wait_ge(vt_ev, n - 1)
                turn_kv(slot[n % 2][:, 1, :], vT, n).then_inc(vt_mm, 1)

            for k in range(8):
                gemm_mem(T_V + k)
                if k == 0:
                    pe.wait_ge(q_split, 1)
                    pe.wait_ge(kt_ev, 4)
                    for n in range(KT):
                        last = nc.tensor.transpose(aux[0:2 * NS, n // 4, n % 4 * P:(n % 4 + 1) * P], q_cols[:, n, :], ident[:])
                    last.then_inc(qt_mm, 1)
                    pe.wait_ge(qt_ev, 1)
                if k >= 2:
                    pe.wait_ge(cache_used, k - 1)
                for j in range(2):
                    last = nc.tensor.matmul(q_bank(k)[:, j, :], pick[:, k:k + 1].to_broadcast([2 * NS, P]),
                                            q_tok[:, j * 512:(j + 1) * 512], start=True, stop=True)
                last.then_inc(qb_mm, 1)
                if k >= 2 and k % 2 == 0:
                    turn_v(k // 2 - 1)
            turn_v(3)
            def scores(n):
                h, tq = n // 4, n % 4
                if n >= 2:
                    pe.wait_ge(prob_exp, n - 1)
                for kk in range(2):
                    last = nc.tensor.matmul(aux[:, n % 2, 0:MEM], qT[:, 2 * h + kk, tq * P:(tq + 1) * P], kT[:, 2 * h + kk, :],
                                            start=(kk == 0), stop=(kk == 1))
                last.then_inc(score_mm, 1)

            def turn(n):
                pe.wait_ge(prob_n, n + 1)
                if n >= 2:
                    pe.wait_ge(pt_ev, n - 1)
                for m in range(2):
                    last = nc.tensor.transpose(aux[:, 2 + n % 2, m * P:(m + 1) * P], prob[n % 2][:, m * P:(m + 1) * P], ident[:])
                last.then_inc(pt_mm, 1)

            def values(h):
                pe.wait_ge(pt_ev, 4 * h + 4)
                for dt in range(2):
                    if h >= 1 and h < XH - 1:
                        pe.wait_ge(pv_lo, 2 * h + dt - 1)
                    for m in range(2):
                        last = nc.tensor.matmul(pv_bank(h, dt), v_tok[:, m, h * XD + dt * P:h * XD + (dt + 1) * P],
                                                probT[h % 2][:, m, :], start=(m == 0), stop=(m == 1))
                    last.then_inc(pv_mm, 1)

            def values_s(b, m):
                n = NS + b
                pe.wait_ge(cache_in[n % CR], 16 * (n // CR + 1))
                for h in range(XH):
                    last = nc.tensor.matmul(slot[h // 2][0:NS, 1, h % 2 * XD:(h % 2 + 1) * XD], p_diag[:, m, b, h, :],
                                            cache[n % CR][:, m, h * XD:(h + 1) * XD], start=(b == 0 and m == 0 and h % 2 == 0),
                                            stop=(b == NS - 1 and m == 1 and h % 2 == 1), skip_group_check=True)
                if m == 1:
                    last.then_inc(cache_used, 1)

            pe.wait_ge(cache_used, NS - 1)
            scores(0)
            scores(1)
            pe.wait_ge(cache_used, NS)
            pe.wait_ge(vt_ev, 4)
            for m in range(2):
                last = nc.tensor.transpose(slot[0][0:32, 1, m * P:(m + 1) * P], s_cols[:, m * 32:(m + 1) * 32], ident[:])
            last.then_inc(sm_a, 1)
            pe.wait_ge(sm_d, 1)
            for m in range(2):
                last = nc.tensor.transpose(slot[1][:, 1, m * 32:(m + 1) * 32], prob_s[:, m * P:(m + 1) * P], ident[0:32, 0:32])
            last.then_inc(sm_e, 1)
            pe.wait_ge(sm_f, 1)
            for n in range(16):
                if 1 <= n < 15:
                    scores(n + 1)
                if n < 15:
                    for half in ((n,) if n < 14 else (14, 15)):
                        values_s(half // 2, half % 2)
                if n == 15:
                    pe.wait_ge(o_s_row, 2)
                    for k in range(KT):
                        last = nc.tensor.transpose(slot[0][:, 1, k * NS:(k + 1) * NS], o_tok[:, k * P:(k + 1) * P], ident[0:NS, 0:NS])
                    last.then_inc(o_s_tr, 1)
                turn(n)
                if n % 4 == 3 and n < 15:
                    values(n // 4)
            pe.wait_ge(pv_lo, 6)
            pe.wait_ge(o_s_lo, 1)
            gemm(pe, T_XO, a_hi, a_lo, kts=range(0, 6))
            values(3)
            gemm(pe, T_XO, a_hi, a_lo, kts=range(6, 8), ktwait=lambda kk: pe.wait_ge(pv_lo, kk + 1))
            for k in range(1, 8):
                gemm(pe, T_XO + k, a_hi, a_lo)
            def up_wait(kk):
                pe.wait_ge(u_ready, 32 + kk + 1)

            gemm(pe, T_MLP, b_hi, b_lo, kts=range(0, 4), ktwait=up_wait)
            residual_norm(24)
            gemm(pe, T_MLP, b_hi, b_lo, kts=range(4, 8), ktwait=up_wait)
            for k in range(1, 8):
                gemm(pe, T_MLP + k, b_hi, b_lo)
            for k in range(8):
                gemm(pe, T_MLP + 8 + k, c_hi, c_lo, ktwait=(lambda kk: pe.wait_ge(ff_lo, kk + 1)) if k == 0 else None)
            with pe.Fori(1, FF_CHUNKS - 1) as i:
                for k in range(8):
                    gemm(pe, T_MLP + k, b_hi, b_lo, i, 16)
                for k in range(8):
                    gemm(pe, T_MLP + 8 + k, c_hi, c_lo, i, 16,
                         ktwait=(lambda kk: pe.wait_ge(ff_lo, kk + 1 + i * 8)) if k == 0 else None)
            T_LAST = T_MLP + 16 * (FF_CHUNKS - 1)
            n0 = 8 * (FF_CHUNKS - 1)
            for k in range(8):
                gemm(pe, T_LAST + k, b_hi, b_lo)
            def turn_x(c, k):
                return nc.tensor.transpose(aux[:, c, k % 4 * P:(k % 4 + 1) * P], x[:, k, c * P:(c + 1) * P], ident[:])

            def turn_xs(k):
                return nc.tensor.transpose(slot[0][0:NS, k // 4, k % 4 * P:(k % 4 + 1) * P], x[:, k, SEQ:TT], ident[:])

            for k in range(8):
                gemm(pe, T_LAST + 8 + k, c_hi, c_lo, ktwait=(lambda kk: pe.wait_ge(ff_lo, n0 + kk + 1)) if k == 0 else None)
                if k == 4:
                    for c in range(NCH):
                        if c == 0:
                            pe.wait_ge(evacuated[0], uses(T_LAST + 8) + 3)
                            pe.wait_ge(evacuated[1], uses(T_LAST + 8) + 3)
                        for j in range(4):
                            last = turn_x(c, j)
                        last.then_inc(fin_mm, 1)
                if k >= 6:
                    pe.wait_ge(evacuated[0], uses(T_LAST + 8) + k - 2)
                    if k == 6:
                        pe.wait_ge(evacuated[1], uses(T_LAST + 8) + 4)
                        pe.wait_ge(fin_copy, 4)
                        for j in (4, 5):
                            for c in range(NCH):
                                turn_x(c, j)
                    else:
                        for c in range(NCH):
                            turn_x(c, 6)
            for j in range(7):
                turn_xs(j)
            pe.wait_ge(evacuated[1], uses(T_LAST + 8) + 5)
            for c in range(NCH):
                turn_x(c, 7).then_inc(fin_mm, 1)
            turn_xs(7).then_inc(fin_mm, 1)


_INS = ["x_prompt", "x_sample", "mem_prompt", "state_ssm", "state_conv", "state_pool", "cache_mem_k", "cache_mem_v",
        "norm_mix", "w_in", "conv_w", "conv_b", "dt_bias", "a_log", "d_skip", "ssd_norm", "w_ssd_proj", "pool_w",
        "pool_scale", "w_o", "norm_x", "w_xq", "w_xk", "w_xv", "w_xo", "norm_mlp", "w_up", "w_down", "norm_final"]
_OUTS = [("y_prompt", (1, SEQ, D)), ("y_sample", (NS, 1, D)),
         ("ssm_prompt", (1, 1, HEADS, HD, N_STATE)), ("conv_prompt", (1, 1, 3, CONV_DIM)), ("pool_prompt", (1, 1, PBUF, D)),
         ("memk_prompt", (1, 1, MEM, XH, XD)), ("memv_prompt", (1, 1, MEM, XH, XD)),
         ("ssm_sample", (1, NS, HEADS, HD, N_STATE)), ("conv_sample", (1, NS, 3, CONV_DIM)), ("pool_sample", (1, NS, PBUF, D))]


def kernel(**inputs):
    import numpy as _np
    import concourse.bacc as _bacc
    from concourse.bass_utils import run_bass_kernel_spmd as _run

    nc = _bacc.Bacc("TRN2", target_bir_lowering=False, num_devices=1)
    arrays, ins, outs = {}, {}, {}
    for name in _INS:
        v = _np.ascontiguousarray(inputs[name])
        arrays[f"in_{name}"] = v
        ins[name] = nc.dram_tensor(f"in_{name}", v.shape, F32, kind="ExternalInput").ap()
    for name, shape in _OUTS:
        outs[name] = nc.dram_tensor(f"out_{name}", shape, F32, kind="ExternalOutput").ap()
    build(nc, ins, outs)
    r = _run(nc, [arrays], core_ids=[0])
    return tuple(r.results[0][f"out_{name}"] for name, _ in _OUTS)
```
